# Optimizing a Trainium2 kernel written in Bass

```python
import math
import jax, jax.numpy as jnp
from jax import lax
import numpy as np

D_MODEL = 2048
BATCH = 1
SEQ = 256
DEPTH = 1
DEC_BATCH = 8
DEC_SEQ = 8
PAST_LEN = 2048
PAGE_SIZE = 128

HEAD_DIM = 64
ATTN_WIDTH = D_MODEL // 2
N_HEADS_A = ATTN_WIDTH // HEAD_DIM
N_KV_HEADS = 4
GQA = N_HEADS_A // N_KV_HEADS
KV_WIDTH = N_KV_HEADS * HEAD_DIM
CMP_BLOCK = 32
CMP_STRIDE = 16
SEL_BLOCK = 64
SEL_TOPK = 16
WINDOW = 512
SEL_Q_BLOCK = 32
WIN_Q_BLOCK = 128
NUM_BUCKETS = 32
MAX_DISTANCE = 128
SSM_WIDTH = D_MODEL // 4
SSM_GROUP = 16
SSM_GROUPS = SSM_WIDTH // SSM_GROUP
SSM_STATE = 64
GMLP_WIDTH = D_MODEL // 4
GMLP_GROUPS = 4
GMLP_GROUP_DIM = GMLP_WIDTH // GMLP_GROUPS
CHUNK = 128
MIX_WIDTH = ATTN_WIDTH + SSM_WIDTH + GMLP_WIDTH
IN_SPLITS = (ATTN_WIDTH, 6 * KV_WIDTH, 3 * N_HEADS_A, SSM_WIDTH, GMLP_WIDTH, GMLP_WIDTH)
IN_WIDTH = ATTN_WIDTH + 6 * KV_WIDTH + 3 * N_HEADS_A + SSM_WIDTH + 2 * GMLP_WIDTH
MOE_GROUPS = 4
EXPERTS_PER_GROUP = 4
N_EXPERTS = MOE_GROUPS * EXPERTS_PER_GROUP
INNER_TOP_K = 2
D_EXPERT = D_MODEL // 4

SCALE = HEAD_DIM ** -0.5
EPS = 1e-6
NEG_INF = -1e30

kernel_name = 'hymba_nsa_s5_gmlp_hmoe_decode_step'

def rms_norm(x, g):
    xf = x.astype(jnp.float32)
    y = xf * lax.rsqrt(jnp.mean(xf * xf, axis=-1, keepdims=True) + EPS)
    return (y * g.astype(jnp.float32)).astype(x.dtype)

def masked_softmax(logits, mask):
    l = jnp.where(mask, logits.astype(jnp.float32), NEG_INF)
    e = jnp.where(mask, jnp.exp(l - jnp.max(l, axis=-1, keepdims=True)), 0.0)
    return e / jnp.maximum(jnp.sum(e, axis=-1, keepdims=True), 1e-30)

def t5_bucket(dist):
    n = jnp.maximum(dist, 0)
    max_exact = NUM_BUCKETS // 2
    nf = jnp.maximum(n, max_exact).astype(jnp.float32)
    large = max_exact + (jnp.log(nf / max_exact) / math.log(MAX_DISTANCE / max_exact)
                         * (NUM_BUCKETS - max_exact)).astype(jnp.int32)
    return jnp.where(n < max_exact, n, jnp.minimum(large, NUM_BUCKETS - 1))

def to_blocks(x, n):
    return jnp.moveaxis(x.reshape(x.shape[0], n, x.shape[1] // n, *x.shape[2:]), 1, 0)

def from_blocks(y):
    y = jnp.moveaxis(y, 0, 1)
    return y.reshape(y.shape[0], y.shape[1] * y.shape[2], *y.shape[3:])

def split_projection(h, w_in):
    Bn, T = h.shape[:2]
    offs = np.cumsum(IN_SPLITS)[:-1].tolist()
    q, kv, gates, u_ssm, u_g, v_g = jnp.split(h @ w_in, offs, axis=-1)
    q = q.reshape(Bn, T, N_HEADS_A, HEAD_DIM)
    kv = kv.reshape(Bn, T, 3, N_KV_HEADS, 2, HEAD_DIM)
    gates = jax.nn.sigmoid(gates.astype(jnp.float32)).reshape(Bn, T, 3, N_KV_HEADS, GQA, 1)
    return q, kv, gates, u_ssm, jax.nn.gelu(u_g), jax.nn.gelu(v_g)

def nsa_rows(q, kv, qk_norm):
    Bn, T = q.shape[:2]
    qg = rms_norm(q, qk_norm[0]).reshape(Bn, T, N_KV_HEADS, GQA, HEAD_DIM)

    def normed(branch, g):
        return jnp.stack([rms_norm(kv[:, :, branch, :, 0], g), kv[:, :, branch, :, 1]], axis=-2)

    return qg, kv[:, :, 0], normed(1, qk_norm[2]), normed(2, qk_norm[3])

def compress(rows, pos, w1, w2):
    Bn, L = rows.shape[:2]
    n_cmp = (L - CMP_BLOCK) // CMP_STRIDE + 1
    idx = jnp.arange(n_cmp)[:, None] * CMP_STRIDE + jnp.arange(CMP_BLOCK)[None, :]
    blocks = rows[:, idx] + pos[:, None, :]
    flat = jnp.swapaxes(blocks, 2, 3).reshape(Bn, n_cmp, N_KV_HEADS, CMP_BLOCK * HEAD_DIM)
    return jax.nn.gelu(flat @ w1) @ w2

def compress_kv(cmp_rows, lp):
    kc = rms_norm(compress(cmp_rows[..., 0, :], lp['cmp_pos'][0], lp['cmp_w1'][0], lp['cmp_w2'][0]),
                  lp['qk_norm'][1])
    vc = compress(cmp_rows[..., 1, :], lp['cmp_pos'][1], lp['cmp_w1'][1], lp['cmp_w2'][1])
    return kc, vc

def cmp_attention(qg, kc, vc, qpos, table):
    Q, n = qpos.shape[0], kc.shape[1]
    dist = qpos[:, None] - (jnp.arange(n) * CMP_STRIDE + CMP_BLOCK - 1)[None, :]
    bias = jnp.transpose(table[t5_bucket(dist)], (2, 0, 1)).reshape(N_KV_HEADS, GQA, Q, n)
    logits = jnp.einsum('bqhgd,bnhd->bhgqn', qg, kc, preferred_element_type=jnp.float32) * SCALE + bias
    p = masked_softmax(logits, dist >= 0)
    o = jnp.einsum('bhgqn,bnhd->bqhgd', p.astype(vc.dtype), vc)
    return o, p

def select_blocks(p_cmp, qpos, n_sel):
    n_cmp = p_cmp.shape[-1]
    c_start = jnp.arange(n_cmp)[:, None] * CMP_STRIDE
    s_start = jnp.arange(n_sel)[None, :] * SEL_BLOCK
    overlap = ((c_start < s_start + SEL_BLOCK) & (c_start + CMP_BLOCK > s_start)).astype(jnp.float32)
    score = jnp.einsum('bhgqn,ns->bhqs', p_cmp, overlap)
    blk = jnp.arange(n_sel)[None, :]
    cur = (qpos // SEL_BLOCK)[:, None]
    forced = (blk == 0) | (blk == cur) | (blk == cur - 1)
    future = blk * SEL_BLOCK > qpos[:, None]
    score = jnp.where(forced, 1e6, jnp.where(future, -1.0, score))
    _, idx = lax.top_k(score, min(SEL_TOPK, n_sel))
    return idx

def sel_attention(qg, qpos, idx, gather, table):
    Bn, Q = qg.shape[:2]
    spos = (idx[..., None] * SEL_BLOCK + jnp.arange(SEL_BLOCK)).reshape(Bn, N_KV_HEADS, Q, -1)
    rows = gather(spos)
    dist = qpos[:, None] - spos
    tab = table.reshape(NUM_BUCKETS, N_KV_HEADS, GQA)
    bias = tab[t5_bucket(dist)[:, :, None], jnp.arange(N_KV_HEADS)[:, None, None, None],
               jnp.arange(GQA)[:, None, None]]
    logits = jnp.einsum('bqhgd,bhqnd->bhgqn', qg, rows[..., 0, :],
                        preferred_element_type=jnp.float32) * SCALE + bias
    p = masked_softmax(logits, (dist >= 0)[:, :, None])
    return jnp.einsum('bhgqn,bhqnd->bqhgd', p.astype(rows.dtype), rows[..., 1, :])

def win_attention(qg, rows, qpos, kpos, table):
    Q, N = qpos.shape[0], kpos.shape[0]
    dist = qpos[:, None] - kpos[None, :]
    mask = (dist >= 0) & (dist <= WINDOW) & (kpos >= 0)[None, :]
    bias = jnp.transpose(table[t5_bucket(dist)], (2, 0, 1)).reshape(N_KV_HEADS, GQA, Q, N)
    logits = jnp.einsum('bqhgd,bnhd->bhgqn', qg, rows[..., 0, :],
                        preferred_element_type=jnp.float32) * SCALE + bias
    p = masked_softmax(logits, mask)
    return jnp.einsum('bhgqn,bnhd->bqhgd', p.astype(rows.dtype), rows[..., 1, :])

def combine_branches(gates, o_cmp, o_sel, o_win):
    g = gates.astype(o_cmp.dtype)
    o = g[:, :, 0] * o_cmp + g[:, :, 1] * o_sel + g[:, :, 2] * o_win
    return o.reshape(o.shape[0], o.shape[1], ATTN_WIDTH)

def nsa_prompt(q, kv, gates, lp, table):
    Bn, T = q.shape[:2]
    qpos = jnp.arange(T)
    qg, cmp_rows, sel_rows, win_rows = nsa_rows(q, kv, lp['qk_norm'])
    kc, vc = compress_kv(cmp_rows, lp)
    o_cmp, p_cmp = cmp_attention(qg, kc, vc, qpos, table)
    idx = select_blocks(p_cmp, qpos, -(-T // SEL_BLOCK))
    bidx = jnp.arange(Bn)[:, None, None, None]
    hidx = jnp.arange(N_KV_HEADS)[None, :, None, None]

    def sel_block(args):
        q_blk, qp, idx_blk = args
        return sel_attention(q_blk, qp, idx_blk, lambda spos: sel_rows[bidx, spos, hidx], table)

    nb = T // SEL_Q_BLOCK
    o_sel = from_blocks(lax.map(sel_block, (to_blocks(qg, nb), qpos.reshape(nb, SEL_Q_BLOCK),
                                            jnp.moveaxis(idx.reshape(Bn, N_KV_HEADS, nb, SEL_Q_BLOCK, -1), 2, 0))))
    nw = T // WIN_Q_BLOCK
    band = WINDOW + WIN_Q_BLOCK
    win_pad = jnp.pad(win_rows, ((0, 0), (WINDOW, 0), (0, 0), (0, 0), (0, 0)))

    def win_block(args):
        q_blk, start = args
        rows = lax.dynamic_slice_in_dim(win_pad, start, band, axis=1)
        return win_attention(q_blk, rows, start + jnp.arange(WIN_Q_BLOCK),
                             start - WINDOW + jnp.arange(band), table)

    o_win = from_blocks(lax.map(win_block, (to_blocks(qg, nw), jnp.arange(nw) * WIN_Q_BLOCK)))
    o = combine_branches(gates, o_cmp, o_sel, o_win)
    return o, (cmp_rows, sel_rows, win_rows[:, T - min(WINDOW, T):])

def nsa_sample(q, kv, gates, lp, table, cmp_pool, sel_pool, win_buf, page_table, layer):
    Bn, S = q.shape[:2]
    P = page_table.shape[1] * PAGE_SIZE
    qpos = P + jnp.arange(S)
    qg, cmp_new, sel_new, win_new = nsa_rows(q, kv, lp['qk_norm'])
    past_cmp = cmp_pool[page_table, layer].reshape(Bn, P, N_KV_HEADS, 2, HEAD_DIM)
    kc, vc = compress_kv(jnp.concatenate([past_cmp.astype(cmp_new.dtype), cmp_new], axis=1), lp)
    o_cmp, p_cmp = cmp_attention(qg, kc, vc, qpos, table)
    idx = select_blocks(p_cmp, qpos, -(-(P + S) // SEL_BLOCK))
    bidx = jnp.arange(Bn)[:, None, None, None]
    hidx = jnp.arange(N_KV_HEADS)[None, :, None, None]

    def gather(spos):
        past_pos = jnp.minimum(spos, P - 1)
        phys = page_table[bidx, past_pos // PAGE_SIZE]
        past = sel_pool[phys, layer, past_pos % PAGE_SIZE, hidx]
        new = sel_new[bidx, jnp.clip(spos - P, 0, S - 1), hidx]
        return jnp.where((spos >= P)[..., None, None], new, past.astype(new.dtype))

    o_sel = sel_attention(qg, qpos, idx, gather, table)
    n_buf = win_buf.shape[1]
    win_all = jnp.concatenate([win_buf.astype(win_new.dtype), win_new], axis=1)
    o_win = win_attention(qg, win_all, qpos, P - n_buf + jnp.arange(n_buf + S), table)
    o = combine_branches(gates, o_cmp, o_sel, o_win)
    return o, (cmp_new, sel_new, win_all[:, S:])

def s5_mixer(u, h0_re, h0_im, lp):
    f32 = jnp.float32
    Bn, T = u.shape[:2]
    a_re, a_im = lp['ssm_a_re'].astype(f32), lp['ssm_a_im'].astype(f32)
    dt = jnp.exp(lp['ssm_log_dt'].astype(f32))[:, None]
    mag = jnp.exp(dt * a_re)
    ab_re, ab_im = mag * jnp.cos(dt * a_im), mag * jnp.sin(dt * a_im)
    den = a_re * a_re + a_im * a_im
    f_re = ((ab_re - 1.0) * a_re + ab_im * a_im) / den
    f_im = (ab_im * a_re - (ab_re - 1.0) * a_im) / den
    b_re, b_im = lp['ssm_b_re'].astype(f32), lp['ssm_b_im'].astype(f32)
    bb_re = f_re[..., None] * b_re - f_im[..., None] * b_im
    bb_im = f_re[..., None] * b_im + f_im[..., None] * b_re
    ug = u.astype(f32).reshape(Bn, T, SSM_GROUPS, SSM_GROUP)
    x_re = jnp.einsum('btgc,gnc->btgn', ug, bb_re)
    x_im = jnp.einsum('btgc,gnc->btgn', ug, bb_im)
    h0_re, h0_im = h0_re.astype(f32), h0_im.astype(f32)
    x_re = x_re.at[:, 0].add(ab_re * h0_re - ab_im * h0_im)
    x_im = x_im.at[:, 0].add(ab_re * h0_im + ab_im * h0_re)

    def combine(e1, e2):
        a1r, a1i, x1r, x1i = e1
        a2r, a2i, x2r, x2i = e2
        return (a1r * a2r - a1i * a2i, a1r * a2i + a1i * a2r,
                a2r * x1r - a2i * x1i + x2r, a2r * x1i + a2i * x1r + x2i)

    elems = (jnp.broadcast_to(ab_re, x_re.shape), jnp.broadcast_to(ab_im, x_re.shape), x_re, x_im)
    _, _, h_re, h_im = lax.associative_scan(combine, elems, axis=1)
    c_re, c_im = lp['ssm_c_re'].astype(f32), lp['ssm_c_im'].astype(f32)
    y = (jnp.einsum('btgn,gcn->btgc', h_re, c_re) - jnp.einsum('btgn,gcn->btgc', h_im, c_im)
         + lp['ssm_d'].astype(f32).reshape(SSM_GROUPS, SSM_GROUP) * ug)
    y = jax.nn.gelu(y.reshape(Bn, T, SSM_WIDTH))
    y = y * jax.nn.sigmoid(y @ lp['ssm_glu_w'].astype(f32) + lp['ssm_glu_b'].astype(f32))
    return y.astype(u.dtype), h_re[:, -1], h_im[:, -1]

def gmlp_mixer(u, v, lp):
    Bn, T = u.shape[:2]
    vn = rms_norm(v.reshape(Bn, T, GMLP_GROUPS, GMLP_GROUP_DIM),
                  lp['gmlp_norm'].reshape(GMLP_GROUPS, GMLP_GROUP_DIM))
    n_chunks = -(-T // CHUNK)
    vc = jnp.pad(vn, ((0, 0), (0, n_chunks * CHUNK - T), (0, 0), (0, 0)))
    vc = vc.reshape(Bn, n_chunks, CHUNK, GMLP_GROUPS, GMLP_GROUP_DIM)
    w = lp['gmlp_ws'] * jnp.tril(jnp.ones((CHUNK, CHUNK), lp['gmlp_ws'].dtype))
    mixed = jnp.einsum('gts,bcsgd->bctgd', w, vc) + lp['gmlp_bs'].T[None, None, :, :, None]
    mixed = mixed.reshape(Bn, n_chunks * CHUNK, GMLP_GROUPS, GMLP_GROUP_DIM)[:, :T]
    out = (u.reshape(Bn, T, GMLP_GROUPS, GMLP_GROUP_DIM) * mixed).reshape(Bn, T, GMLP_WIDTH)
    v_rows = vn.reshape(Bn, T, GMLP_WIDTH)[:, (T - 1) // CHUNK * CHUNK:]
    return out, v_rows

def merge_mixers(o_a, o_b, o_c, lp):
    g = lp['out_norm']
    cat = jnp.concatenate([rms_norm(o_a, g[:ATTN_WIDTH]),
                           rms_norm(o_b, g[ATTN_WIDTH:ATTN_WIDTH + SSM_WIDTH]),
                           rms_norm(o_c, g[ATTN_WIDTH + SSM_WIDTH:])], axis=-1)
    return cat @ lp['w_out']

def hier_moe(h, lp):
    Bn, T, D = h.shape
    x = h.reshape(Bn * T, D)
    g_logits = (x @ lp['router_group_w'] + lp['router_group_b']).astype(jnp.float32)
    g_star = jnp.argmax(g_logits, axis=-1)
    g_prob = jnp.max(jax.nn.softmax(g_logits, axis=-1), axis=-1)
    g_onehot = jax.nn.one_hot(g_star, MOE_GROUPS, dtype=jnp.float32)
    e_logits = (jnp.einsum('nd,gde->nge', x, lp['router_expert_w']) + lp['router_expert_b']).astype(jnp.float32)
    e_logits = jnp.einsum('nge,ng->ne', e_logits, g_onehot)
    top_v, top_i = lax.top_k(e_logits, INNER_TOP_K)
    top_w = jax.nn.softmax(top_v, axis=-1) * g_prob[:, None]
    inner = jnp.sum(jax.nn.one_hot(top_i, EXPERTS_PER_GROUP, dtype=jnp.float32) * top_w[..., None], axis=1)
    gate = (g_onehot[:, :, None] * inner[:, None, :]).reshape(-1, N_EXPERTS).astype(x.dtype)
    hid = jax.nn.silu(jnp.einsum('nd,edf->nef', x, lp['expert_w1'])) * jnp.einsum('nd,edf->nef', x, lp['expert_w3'])
    y = jnp.einsum('nef,efd->nd', hid * gate[:, :, None], lp['expert_w2'])
    return y.reshape(Bn, T, D)

def decoder_layer(x, lp, table, h0_re, h0_im, cache=None):
    h = rms_norm(x, lp['norm_mix'])
    q, kv, gates, u_ssm, u_g, v_g = split_projection(h, lp['w_in'])
    if cache is None:
        o_a, (cmp_rows, sel_rows, win_buf) = nsa_prompt(q, kv, gates, lp, table)
    else:
        o_a, (cmp_rows, sel_rows, win_buf) = nsa_sample(q, kv, gates, lp, table, *cache)
    o_b, s_re, s_im = s5_mixer(u_ssm, h0_re, h0_im, lp)
    o_c, v_rows = gmlp_mixer(u_g, v_g, lp)
    x = x + merge_mixers(o_a, o_b, o_c, lp)
    x = x + hier_moe(rms_norm(x, lp['norm_ffn']), lp)
    return x, (cmp_rows, sel_rows, win_buf, s_re, s_im, v_rows)

def setup_inputs(seed: int = 0) -> dict:
    key = jax.random.key(seed)
    keys = iter(jax.random.split(key, 48))
    f32 = jnp.float32

    def normal(shape, scale):
        return scale * jax.random.normal(next(keys), shape, f32)

    def gain(shape):
        return 1.0 + 0.05 * jax.random.normal(next(keys), shape, f32)

    n_pages = PAST_LEN // PAGE_SIZE
    n_phys = (5 * DEC_BATCH * n_pages + 3) // 4
    n_buf = min(WINDOW, PAST_LEN)
    page_table = jax.random.permutation(next(keys), n_phys)[:DEC_BATCH * n_pages]
    page_table = page_table.reshape(DEC_BATCH, n_pages).astype(jnp.int32)
    kv_pages = (n_phys, DEPTH, PAGE_SIZE, N_KV_HEADS, 2, HEAD_DIM)
    n_idx = jnp.arange(SSM_STATE, dtype=f32)
    return {
        'x_prompt': normal((BATCH, SEQ, D_MODEL), 1.0),
        'x_sample': normal((DEC_BATCH, DEC_SEQ, D_MODEL), 1.0),
        'cache_kv_cmp': normal(kv_pages, 1.0),
        'cache_kv_sel': normal(kv_pages, 1.0),
        'cache_kv_win': normal((DEC_BATCH, DEPTH, n_buf, N_KV_HEADS, 2, HEAD_DIM), 1.0),
        'state_ssm_re': normal((DEC_BATCH, DEPTH, SSM_GROUPS, SSM_STATE), 0.5),
        'state_ssm_im': normal((DEC_BATCH, DEPTH, SSM_GROUPS, SSM_STATE), 0.5),
        'page_table': page_table,
        'rel_bias': normal((NUM_BUCKETS, N_HEADS_A), 0.3),
        'norm_mix': gain((DEPTH, D_MODEL)),
        'w_in': normal((DEPTH, D_MODEL, IN_WIDTH), D_MODEL ** -0.5),
        'qk_norm': gain((DEPTH, 4, HEAD_DIM)),
        'cmp_pos': normal((DEPTH, 2, CMP_BLOCK, HEAD_DIM), 0.3),
        'cmp_w1': normal((DEPTH, 2, CMP_BLOCK * HEAD_DIM, HEAD_DIM), (CMP_BLOCK * HEAD_DIM) ** -0.5),
        'cmp_w2': normal((DEPTH, 2, HEAD_DIM, HEAD_DIM), HEAD_DIM ** -0.5),
        'ssm_a_re': -0.5 + normal((DEPTH, SSM_GROUPS, SSM_STATE), 0.01),
        'ssm_a_im': math.pi * n_idx + normal((DEPTH, SSM_GROUPS, SSM_STATE), 0.01),
        'ssm_log_dt': jax.random.uniform(next(keys), (DEPTH, SSM_GROUPS), f32, math.log(1e-3), math.log(1e-1)),
        'ssm_b_re': normal((DEPTH, SSM_GROUPS, SSM_STATE, SSM_GROUP), (2 * SSM_GROUP) ** -0.5),
        'ssm_b_im': normal((DEPTH, SSM_GROUPS, SSM_STATE, SSM_GROUP), (2 * SSM_GROUP) ** -0.5),
        'ssm_c_re': normal((DEPTH, SSM_GROUPS, SSM_GROUP, SSM_STATE), (2 * SSM_STATE) ** -0.5),
        'ssm_c_im': normal((DEPTH, SSM_GROUPS, SSM_GROUP, SSM_STATE), (2 * SSM_STATE) ** -0.5),
        'ssm_d': normal((DEPTH, SSM_WIDTH), 1.0),
        'ssm_glu_w': normal((DEPTH, SSM_WIDTH, SSM_WIDTH), SSM_WIDTH ** -0.5),
        'ssm_glu_b': normal((DEPTH, SSM_WIDTH), 0.02),
        'gmlp_norm': gain((DEPTH, GMLP_WIDTH)),
        'gmlp_ws': normal((DEPTH, GMLP_GROUPS, CHUNK, CHUNK), CHUNK ** -0.5),
        'gmlp_bs': gain((DEPTH, GMLP_GROUPS, CHUNK)),
        'out_norm': gain((DEPTH, MIX_WIDTH)),
        'w_out': normal((DEPTH, MIX_WIDTH, D_MODEL), MIX_WIDTH ** -0.5),
        'norm_ffn': gain((DEPTH, D_MODEL)),
        'router_group_w': normal((DEPTH, D_MODEL, MOE_GROUPS), D_MODEL ** -0.5),
        'router_group_b': normal((DEPTH, MOE_GROUPS), 0.01),
        'router_expert_w': normal((DEPTH, MOE_GROUPS, D_MODEL, EXPERTS_PER_GROUP), D_MODEL ** -0.5),
        'router_expert_b': normal((DEPTH, MOE_GROUPS, EXPERTS_PER_GROUP), 0.01),
        'expert_w1': normal((DEPTH, N_EXPERTS, D_MODEL, D_EXPERT), D_MODEL ** -0.5),
        'expert_w3': normal((DEPTH, N_EXPERTS, D_MODEL, D_EXPERT), D_MODEL ** -0.5),
        'expert_w2': normal((DEPTH, N_EXPERTS, D_EXPERT, D_MODEL), D_EXPERT ** -0.5),
    }

def reference(x_prompt, x_sample, cache_kv_cmp, cache_kv_sel, cache_kv_win, state_ssm_re, state_ssm_im,
              page_table, rel_bias, norm_mix, w_in, qk_norm, cmp_pos, cmp_w1, cmp_w2,
              ssm_a_re, ssm_a_im, ssm_log_dt, ssm_b_re, ssm_b_im, ssm_c_re, ssm_c_im, ssm_d,
              ssm_glu_w, ssm_glu_b, gmlp_norm, gmlp_ws, gmlp_bs, out_norm, w_out, norm_ffn,
              router_group_w, router_group_b, router_expert_w, router_expert_b,
              expert_w1, expert_w3, expert_w2):
    xp, xs = x_prompt, x_sample
    states_p, states_s = [], []
    zeros_state = jnp.zeros((x_prompt.shape[0], SSM_GROUPS, SSM_STATE), jnp.float32)
    for l in range(DEPTH):
        lp = {
            'norm_mix': norm_mix[l], 'w_in': w_in[l], 'qk_norm': qk_norm[l],
            'cmp_pos': cmp_pos[l], 'cmp_w1': cmp_w1[l], 'cmp_w2': cmp_w2[l],
            'ssm_a_re': ssm_a_re[l], 'ssm_a_im': ssm_a_im[l], 'ssm_log_dt': ssm_log_dt[l],
            'ssm_b_re': ssm_b_re[l], 'ssm_b_im': ssm_b_im[l], 'ssm_c_re': ssm_c_re[l], 'ssm_c_im': ssm_c_im[l],
            'ssm_d': ssm_d[l], 'ssm_glu_w': ssm_glu_w[l], 'ssm_glu_b': ssm_glu_b[l],
            'gmlp_norm': gmlp_norm[l], 'gmlp_ws': gmlp_ws[l], 'gmlp_bs': gmlp_bs[l],
            'out_norm': out_norm[l], 'w_out': w_out[l], 'norm_ffn': norm_ffn[l],
            'router_group_w': router_group_w[l], 'router_group_b': router_group_b[l],
            'router_expert_w': router_expert_w[l], 'router_expert_b': router_expert_b[l],
            'expert_w1': expert_w1[l], 'expert_w3': expert_w3[l], 'expert_w2': expert_w2[l],
        }
        xp, st_p = decoder_layer(xp, lp, rel_bias, zeros_state, zeros_state)
        xs, st_s = decoder_layer(xs, lp, rel_bias, state_ssm_re[:, l], state_ssm_im[:, l],
                                 cache=(cache_kv_cmp, cache_kv_sel, cache_kv_win[:, l], page_table, l))
        states_p.append(st_p)
        states_s.append(st_s)
    p_kv_cmp, p_kv_sel, p_kv_win, p_ssm_re, p_ssm_im, p_gmlp_v = (jnp.stack(z, axis=1) for z in zip(*states_p))
    s_kv_cmp, s_kv_sel, s_kv_win, s_ssm_re, s_ssm_im, s_gmlp_v = (jnp.stack(z, axis=1) for z in zip(*states_s))
    return (xp, xs, p_kv_cmp, p_kv_sel, p_kv_win, p_ssm_re, p_ssm_im, p_gmlp_v,
            s_kv_cmp, s_kv_sel, s_kv_win, s_ssm_re, s_ssm_im, s_gmlp_v)


_drawn_inputs = setup_inputs


def setup_inputs(seed=0):
    import zlib

    import numpy as np

    out = dict(_drawn_inputs(seed))
    spreads = {}
    factors = {'ssm_a_re': 63.866,
     'ssm_glu_b': 11.96,
     'router_group_b': 28.581,
     'router_expert_b': 11.669}
    for name, (base, spread) in spreads.items():
        noise = np.random.default_rng([zlib.crc32(name.encode()), seed]).standard_normal(out[name].shape)
        drawn = base * np.exp(spread * noise) if base else spread * noise
        out[name] = __import__('jax').numpy.asarray(drawn.astype(out[name].dtype))
    for name, factor in factors.items():
        out[name] = (out[name] * factor).astype(out[name].dtype)
    return out
```

```python
from contextlib import ExitStack

import numpy as np

import concourse.bass as bass
from concourse import mybir

F32 = mybir.dt.float32
F32R = mybir.dt.float32r
I32 = mybir.dt.int32
ALU = mybir.AluOpType
ACT = mybir.ActivationFunctionType
AX_X = mybir.AxisListType.X

P = 128
D = 2048
KT = D // P
SEQ, NB, NS = 256, 8, 8
NTS = NB * NS
T = SEQ + NTS
ROWS = (P, P, NTS)
PAST, PAGE = 2048, 128
NPG = PAST // PAGE
N_PHYS = 5 * NB * NPG // 4
HD, NQ, NKV, G = 64, 16, 4, 4
AW, KVW = 1024, 256
WIN = 512
SELB, TOPK = 64, 16
NBLK = (PAST + NS + SELB - 1) // SELB
NC_S = (PAST - 32) // 16 + 1
NC_P = (SEQ - 32) // 16 + 1
IN_W = 4144
O_Q, O_KV, O_GATE, O_U, O_UG, O_VG = 0, 1024, 2560, 2608, 3120, 3632
SCALE = HD ** -0.5
EPS = 1e-6
NEG = -1e30
D0 = WIN + NS - 1
LB = D0 + SEQ
TRI = 3 * P - 1
PCH = 296
NPCH = IN_W // PCH


def bucket(dist):
    n = np.maximum(dist, 0)
    nf = np.maximum(n, 16).astype(np.float32)
    large = 16 + (np.log(nf / np.float32(16)) / np.float32(np.log(8.0)) * np.float32(16)).astype(np.int32)
    return np.where(n < 16, n, np.minimum(large, 31))


def constants():
    f = np.float32
    p = np.arange(P)
    c = {}
    c["ident"] = np.eye(P, dtype=f)
    dist = D0 - np.arange(LB)
    one = (bucket(dist)[None, :] == np.arange(32)[:, None]).astype(f)
    c["bias_onehot"] = np.vstack([one, np.where((dist < 0) | (dist > WIN), f(NEG), f(0))[None]])
    own = np.where(np.arange(NB)[:, None] == np.arange(NB)[None, :], f(0), f(NEG))
    c["own_seq"] = np.tile(np.repeat(own, NS, axis=1).reshape(1, -1), (P, 1))
    c["causal_T"] = (p[:, None] <= p[None, :]).astype(f)
    tok = np.arange(NTS)
    c["causal_seq_T"] = ((tok[:, None] // NS == tok[None, :] // NS) & (tok[:, None] <= tok[None, :])).astype(f)
    c["spread8"] = (np.arange(NS)[:, None] == tok[None, :] % NS).astype(f)
    cs = np.arange(NC_S)[:, None] * 16
    ss = np.arange(NBLK)[None, :] * SELB
    c["overlap"] = ((cs < ss + SELB) & (cs + 32 > ss)).astype(f)
    hs = (p // 32) * NS + p % NS
    c["sum_group"] = (hs[:, None] == hs[None, :]).astype(f)
    blk = np.arange(NBLK)
    cur = PAST // SELB
    forced = (blk == 0) | (blk == cur) | (blk == cur - 1)
    c["sel_keep"] = np.tile(np.where(forced, 0, 1).astype(f), (P, 1))
    c["sel_force"] = np.tile(np.where(forced, 1e6, 0).astype(f), (P, 1))
    c["low_half"] = np.stack([(p < 64), (p >= 64)], 1).astype(f)
    c["even_group"] = np.stack([(p // 16) % 2 == 0, (p // 16) % 2 == 1], 1).astype(f)
    c["half_ones"] = ((p[:, None] // 64) == (p[None, :] // 64)).astype(f)
    c["before"] = (p[:, None] < p[None, :]).astype(f)
    c["ones"] = np.ones((P, P), f)
    c["iota"] = np.tile(p.astype(f), (P, 1))
    c["earlier4"] = np.tile((np.arange(4)[:, None] > np.arange(4)[None, :]).astype(f).reshape(1, -1), (P, 1))
    c["group4"] = np.tile(np.arange(4).astype(f), (P, 1))
    cols = sum(a.shape[1] for a in c.values())
    pack = np.zeros((P, cols), f)
    at, off = {}, 0
    for k, a in c.items():
        pack[:a.shape[0], off:off + a.shape[1]] = a
        at[k] = (off, a.shape[0], a.shape[1])
        off += a.shape[1]
    return pack, at


FEAT = (("norm_mix", 16), ("norm_ffn", 16), ("out_norm", 16), ("ssm_a_re", 16), ("ssm_a_im", 16),
        ("ssm_d", 4), ("ssm_glu_b", 4), ("gmlp_bs", 4), ("cmp_pos", 32))
FEAT_AT = {}
_o = 0
for _n, _r in FEAT:
    FEAT_AT[_n] = (_o, _r)
    _o += _r
NFEAT = _o


def view(ap, *dims):
    return bass.AP(ap.tensor, ap.offset, [list(ap.ap[0])] + [list(d) for d in dims])


def dram(ap, offset, *dims):
    return bass.AP(ap.tensor, offset, [list(d) for d in dims])


class Chain:

    def __init__(self, eng, sem, base=0):
        self.eng, self.sem, self.base, self.n = eng, sem, base, 0

    def mark(self, ins):
        self.n += 1
        ins.then_inc(self.sem, 1)
        return self.n

    def wait(self, n=None):
        self.eng.wait_ge(self.sem, self.base + (self.n if n is None else n))

    def link(self, ins):
        self.mark(ins)
        self.wait()


def split_high(copy, high, x):
    return copy(high.bitcast(F32R), x)


def split_low(dve, low, x, high):
    return dve.tensor_tensor(low.bitcast(F32R), x, high, ALU.subtract)


def matmul_split(pe, out, a_high, a_low, b_high, b_low, start, stop):
    r = lambda ap: ap.bitcast(F32R)
    pe.matmul(out, r(a_high), r(b_high), start=start, stop=False)
    pe.matmul(out, r(a_high), r(b_low), start=False, stop=False)
    return pe.matmul(out, r(a_low), r(b_high), start=False, stop=stop)


def split_turned_act(act, jobs, tmp, sems, high_T):
    turned, stored, high, low = sems
    for n, (t, k0) in enumerate(jobs):
        act.wait_ge(stored, n + 1)
        split_high(act.copy, high_T[:, k0:k0 + 4, t * P:t * P + ROWS[t]], tmp[n % 2][:, :, :ROWS[t]]).then_inc(high, 1)


def split_turned_dve(dve, jobs, bank, tmp, gain, sems, high_T, low_T):
    turned, stored, high, low = sems

    def rest(n):
        t, k0 = jobs[n]
        x = slice(t * P, t * P + ROWS[t])
        dve.wait_ge(high, n + 1)
        split_low(dve, low_T[:, k0:k0 + 4, x], tmp[n % 2][:, :, :ROWS[t]], high_T[:, k0:k0 + 4, x]).then_inc(low, 1)

    for n, (t, k0) in enumerate(jobs):
        r = ROWS[t]
        dve.wait_ge(turned, n + 1)
        if n >= 2:
            dve.wait_ge(low, n - 1)
        dve.tensor_tensor(tmp[n % 2][:, :, :r], view(bank(n), (P, 4), (1, r)), view(gain(k0), (1, 4), (0, r)), ALU.mult).then_inc(stored, 1)
        if n:
            rest(n - 1)
    rest(len(jobs) - 1)


def phase_norm_in(nc, m, io):
    with ExitStack() as ctx:
        junk = ctx.enter_context(nc.sbuf_tensor("norm_junk", [P, D], F32))
        h = ctx.enter_context(nc.sbuf_tensor("norm_h", [P, 3, D], F32))
        x = ctx.enter_context(nc.sbuf_tensor("norm_x", [P, 3, D], F32))
        frow = ctx.enter_context(nc.sbuf_tensor("feat_rows", [NFEAT, P], F32))
        ssq = ctx.enter_context(nc.sbuf_tensor("norm_ssq", [P, 3], F32))
        rms = ctx.enter_context(nc.sbuf_tensor("norm_rms", [P, 3], F32))
        rstd = ctx.enter_context(nc.sbuf_tensor("norm_rstd", [P, 3], F32))
        tps = ctx.enter_context(nc.psum_tensor("norm_tps", [P, 4, 512], F32))
        const_in, feat_in, gain_in = m.sem("const_in"), m.sem("feat_in"), m.sem("gain_in")
        x_in = [m.sem(f"x_in{t}") for t in range(3)]
        eps_set, feat_turned, feat_ready = m.sem("eps_set"), m.sem("feat_turned"), m.sem("feat_ready")
        rms_ready, rstd_ready, h_ready = m.sem("rms_ready"), m.sem("rstd_ready"), m.sem("h_ready")
        turned, stored, ssq_done = m.sem("hT_turned"), m.sem("hT_stored"), m.sem("ssq_done")
        sems = (turned, stored, m.sem("hT_high"), m.sem("hT_low"))
        tmp = [ctx.enter_context(nc.sbuf_tensor(f"hT_tmp{u}", [P, 4, P], F32)) for u in range(2)]
        jobs = [(t, k0) for t in range(3) for k0 in (0, 4, 8, 12)]
        block = ctx.enter_context(nc.Block())
        C = m.const

        @block.sync
        def _(sp):
            sp.dma_start(m.cpack[:], io["cpack"]).then_inc(const_in, 16)
            sp.dma_start(m.ptab[:], dram(io["page_table"], 0, (NB * NPG, 1), (1, NB * NPG))).then_inc(gain_in, 16)
            for name, rows in FEAT:
                o, _ = FEAT_AT[name]
                src = io[name]
                sp.dma_start(frow[o:o + rows, :], dram(src, 0, (P, rows), (1, P))).then_inc(feat_in, 16)
            for t in range(3):
                src = dram(io["x_prompt"], t * P * D, (D, P), (1, D)) if t < 2 else dram(io["x_sample"], 0, (D, NTS), (1, D))
                sp.dma_start(x[:ROWS[t], t, :], src).then_inc(x_in[t], 16)
            for q in range(4):
                load_piece(sp, io["w_in"], PCH, m.wslot, m.w_in_landed, 0, q)
            sp.dma_start(m.qkg[:], dram(io["qk_norm"], 0, (0, P), (1, 4 * HD))).then_inc(gain_in, 16)
            sp.wait_ge(gain_in, 32)

        @block.vector
        def _(dve):
            dve.memset(m.eps[:], EPS).then_inc(eps_set, 1)
            dve.memset(m.tab[32:33, :], 1.0).then_inc(eps_set, 1)
            dve.wait_ge(feat_turned, 1)
            dve.tensor_copy(m.feat[:], tps[:, 0, :NFEAT]).then_inc(feat_ready, 1)
            for t in range(3):
                r = ROWS[t]
                dve.wait_ge(rms_ready, t + 1)
                dve.reciprocal(rstd[:r, t:t + 1], rms[:r, t:t + 1]).then_inc(rstd_ready, 1)
                dve.wait_ge(rstd_ready, t + 1)
                dve.tensor_scalar(h[:r, t, :], x[:r, t, :], rstd[:r, t:t + 1], None, ALU.mult).then_inc(h_ready, 1)
            dve.wait_ge(feat_ready, 1)
            split_turned_dve(dve, jobs, lambda n: tps[:, n % 2 + 1, :], tmp, lambda k0: m.feat[:, FEAT_AT["norm_mix"][0] + k0:][:, :4],
                             sems, m.hTh, m.hTl)

        @block.scalar
        def _(act):
            act.wait_ge(eps_set, 2)
            for t in range(3):
                r = ROWS[t]
                act.wait_ge(x_in[t], 16)
                if t:
                    act.wait_ge(ssq_done, t)
                act.activation(junk[:r, :], x[:r, t, :], ACT.Square, accum_out=ssq[:r, t:t + 1]).then_inc(ssq_done, 1)
                act.wait_ge(ssq_done, t + 1)
                act.activation(rms[:r, t:t + 1], ssq[:r, t:t + 1], ACT.Sqrt, bias=m.eps[:r, :], scale=1.0 / D).then_inc(rms_ready, 1)
            split_turned_act(act, jobs, tmp, sems, m.hTh)

        @block.tensor
        def _(pe):
            pe.wait_ge(const_in, 16)
            pe.wait_ge(feat_in, 16 * len(FEAT))
            pe.transpose(tps[:, 0, :NFEAT], frow[:], C("ident")[:NFEAT, :NFEAT]).then_inc(feat_turned, 1)
            for n in range(12):
                t, q = divmod(n, 4)
                r = ROWS[t]
                pe.wait_ge(h_ready, t + 1)
                if n >= 2:
                    pe.wait_ge(stored, n - 1)
                for j in range(4):
                    k = 4 * q + j
                    mm = pe.transpose(tps[:, n % 2 + 1, j * P:j * P + r], h[:r, t, k * P:(k + 1) * P],
                                      C("ident")[:r, :r])
                mm.then_inc(turned, 1)


class Stream:

    def __init__(self, m, name, pairs, width, matrix, xTh, xTl, slots, highs, lows, landed):
        self.pairs, self.width, self.matrix, self.xTh, self.xTl = pairs, width, matrix, xTh, xTl
        self.slots, self.highs, self.lows, self.landed = slots, highs, lows, landed
        self.high, self.low, self.used = m.sem(name + "_w_high"), m.sem(name + "_w_low"), m.sem(name + "_w_used")


def load_piece(sp, matrix, width, slots, landed, chunk, q):
    src = matrix[0, q * 512:(q + 1) * 512, bass.ds(chunk * width, width)]
    sp.dma_start(slots[q][:], src.rearrange("(k p) n -> p k n", p=P)).then_inc(landed[q], 16)


def stream_load(sp, z):
    def load(i, n):
        sp.wait_ge(z.low, i * 8 + (n + 1))
        load_piece(sp, z.matrix, z.width, z.slots, z.landed, 2 * i + (1 + n // 4), n % 4)

    with sp.Fori(0, z.pairs - 1) as i:
        for n in range(8):
            load(i, n)
    for n in range(4):
        load(z.pairs - 1, n)


def stream_pe(pe, z, acc, free_v, free_a):
    with pe.Fori(0, z.pairs) as i:
        for c in range(2):
            pe.wait_ge(free_v, i * 2 + (c + 1))
            pe.wait_ge(free_a, i * 2 + (c + 1))
            for q in range(4):
                pe.wait_ge(z.low, i * 8 + (4 * c + q + 1))
                for kk in range(4):
                    k = 4 * q + kk
                    for t in range(3):
                        x = slice(t * P, t * P + ROWS[t])
                        mm = matmul_split(pe, acc[c][t][:ROWS[t], :z.width], z.xTh(k)[:, x], z.xTl(k)[:, x],
                                          z.highs[q][:, kk, :], z.lows[q][:, kk, :], k == 0, k == KT - 1)
                mm.then_inc(z.used, 1)


def stream_split(eng, z, split, copy_out):
    def chunk(i, c, last=False):
        split(i, 4 * c + 2)
        split(i, 4 * c + 3)
        if not last:
            split(i, 4 * c + 4)
            split(i, 4 * c + 5)
        copy_out(i, c)

    split(0, 0)
    split(0, 1)
    with eng.Fori(0, z.pairs - 1) as i:
        chunk(i, 0)
        chunk(i, 1)
    chunk(z.pairs - 1, 0)
    chunk(z.pairs - 1, 1, last=True)


def stream_act(act, z, copy_out):
    def split(i, n):
        act.wait_ge(z.landed[n % 4], i * 32 + (n // 4 + 1) * 16)
        act.wait_ge(z.used, i * 8 + (n + 1))
        split_high(act.copy, z.highs[n % 4][:], z.slots[n % 4][:]).then_inc(z.high, 1)

    act.sem_inc(z.used, 4)
    stream_split(act, z, split, copy_out)


def stream_dve(dve, z, copy_out):
    def split(i, n):
        dve.wait_ge(z.high, i * 8 + (n + 1))
        split_low(dve, z.lows[n % 4][:], z.slots[n % 4][:], z.highs[n % 4][:]).then_inc(z.low, 1)

    stream_split(dve, z, split, copy_out)


def phase_project(nc, m, io):
    with ExitStack() as ctx:
        acc = [[ctx.enter_context(nc.psum_tensor(f"proj_acc{c}{t}", [P, 512], F32)) for t in range(3)] for c in range(2)]
        highs = [ctx.enter_context(nc.sbuf_tensor(f"w_in_high{q}", [P, 4, PCH], F32)) for q in range(4)]
        lows = [ctx.enter_context(nc.sbuf_tensor(f"w_in_low{q}", [P, 4, PCH], F32)) for q in range(4)]
        free_v, free_a = m.sem("proj_acc_free_v"), m.sem("proj_acc_free_a")
        z = Stream(m, "proj", NPCH // 2, PCH, io["w_in"], lambda k: m.hTh[:, k, :], lambda k: m.hTl[:, k, :], m.wslot, highs, lows, m.w_in_landed)
        block = ctx.enter_context(nc.Block())

        @block.sync
        def _(sp):
            stream_load(sp, z)

        @block.tensor
        def _(pe):
            stream_pe(pe, z, acc, free_v, free_a)

        @block.vector
        def _(dve):
            def copy_out(i, c):
                dve.wait_ge(z.used, i * 8 + (4 * c + 8))
                dve.nop()
                for t in range(2):
                    cp = dve.tensor_copy(m.proj[:, t, bass.ds((2 * i + c) * PCH, PCH)], acc[c][t][:, :PCH])
                cp.then_inc(free_v, 1)

            dve.sem_inc(free_v, 2)
            stream_dve(dve, z, copy_out)

        @block.scalar
        def _(act):
            def copy_out(i, c):
                act.wait_ge(z.used, i * 8 + (4 * c + 8))
                act.nop()
                act.copy(m.proj[:NTS, 2, bass.ds((2 * i + c) * PCH, PCH)], acc[c][2][:NTS, :PCH]).then_inc(free_a, 1)

            act.sem_inc(free_a, 2)
            stream_act(act, z, copy_out)


def phase_heads(nc, m, io):
    NH = NQ + 2 * NKV
    with ExitStack() as ctx:
        sq = ctx.enter_context(nc.sbuf_tensor("head_sq", [P, NH, HD], F32))
        ssq = ctx.enter_context(nc.sbuf_tensor("head_ssq", [P, 3, NH], F32))
        rms = ctx.enter_context(nc.sbuf_tensor("head_rms", [P, 3, NH], F32))
        rstd = ctx.enter_context(nc.sbuf_tensor("head_rstd", [P, 3, NH], F32))
        brow = ctx.enter_context(nc.sbuf_tensor("bias_row", [NQ, LB], F32))
        near = ctx.enter_context(nc.sbuf_tensor("bias_new_keys", [P, NS], F32))
        bps = ctx.enter_context(nc.psum_tensor("bias_ps", [NQ, 1024], F32))
        tab_in, bias_done, brow_ready = m.sem("tab_in"), m.sem("bias_done"), m.sem("brow_ready")
        bias_out, bias_in = m.sem("bias_out"), m.sem("bias_in")
        sum_done, rms_done, gate_done, gate_out = m.sem("head_ssq_done"), m.sem("head_rms_done"), m.sem("gate_done"), m.sem("gate_out")
        gate_in, v_step, normed = m.sem("gate_in"), m.sem("head_v_step"), m.sem("heads_normed")
        block = ctx.enter_context(nc.Block())
        kv_flat = NKV * 2 * HD

        @block.sync
        def _(sp):
            sp.dma_start(m.tab[:32, :], io["rel_bias"]).then_inc(tab_in, 16)
            for t in range(2):
                sp.dma_start(dram(io["p_kv_cmp"], t * P * kv_flat, (kv_flat, P), (1, kv_flat)),
                             m.proj[:, t, O_KV:O_KV + kv_flat]).then_inc(m.p_cmp_out, 16)
            m.store(sp, dram(io["s_kv_cmp"], 0, (kv_flat, NTS), (1, kv_flat)), m.proj[:NTS, 2, O_KV:O_KV + kv_flat])
            sp.wait_ge(brow_ready, 1)
            sp.dma_start(io["bias_rows"], brow[:]).then_inc(bias_out, 16)
            sp.wait_ge(bias_out, 16)
            for i in range(NS):
                to = slice(i, P, NS)
                sp.dma_start(m.bias_win[to, :], dram(io["bias_rows"], NS - 1 - i, (LB, NQ), (1, WIN))).then_inc(bias_in, 16)
                sp.dma_start(near[to, :], dram(io["bias_rows"], D0 - i, (LB, NQ), (1, NS))).then_inc(bias_in, 16)
                sp.dma_start(m.bias_cmp[to, NC_S - 7:], dram(io["bias_rows"], D0 - 97 - i, (LB, NQ), (16, 7))).then_inc(bias_in, 16)
            sp.dma_start(io["bias_rep"], dram(io["bias_rows"], D0 - 2 * P + 1, (0, P), (LB, NQ), (1, TRI))).then_inc(m.rep_out, 16)
            sp.wait_ge(gate_done, 1)
            sp.dma_start(io["gate_rows"], m.proj[:NTS, 2, O_GATE:O_GATE + 48]).then_inc(gate_out, 16)
            sp.wait_ge(gate_out, 16)
            for i in range(NS):
                for br in range(3):
                    sp.dma_start(m.gate_s[i:P:NS, br, :],
                                 dram(io["gate_rows"], i * 48 + br * NQ, (1, NQ), (48 * NS, NB))).then_inc(gate_in, 16)
            for t in range(3):
                r = ROWS[t]
                sp.wait_ge(normed, t + 1)
                if t < 2:
                    for out, br in ((io["p_kv_sel"], 1), (io["p_kv_win"], 2)):
                        o = O_KV + br * kv_flat
                        m.store(sp, dram(out, t * P * kv_flat, (kv_flat, P), (1, kv_flat)), m.proj[:, t, o:o + kv_flat])
                else:
                    o = O_KV + kv_flat
                    m.store(sp, dram(io["s_kv_sel"], 0, (kv_flat, NTS), (1, kv_flat)), m.proj[:NTS, 2, o:o + kv_flat])
                    for b in range(NB):
                        m.store(sp, dram(io["s_kv_win"], (b * WIN + WIN - NS) * kv_flat, (kv_flat, NS), (1, kv_flat)),
                                m.proj[b * NS:b * NS + NS, 2, o + kv_flat:o + 2 * kv_flat])
            m.store(sp, dram(io["s_kv_win"], 0, (WIN * kv_flat, NB), (1, (WIN - NS) * kv_flat)),
                    dram(io["cache_kv_win"], NS * kv_flat, (WIN * kv_flat, NB), (1, (WIN - NS) * kv_flat)))
            sp.wait_ge(gate_in, 16 * 3 * NS)

        @block.tensor
        def _(pe):
            pe.wait_ge(tab_in, 16)
            pe.matmul(bps[:, :512], m.tab[:], m.const("bias_onehot")[:, :512], start=True, stop=True)
            pe.matmul(bps[:, 512:LB], m.tab[:], m.const("bias_onehot")[:, 512:], start=True, stop=True).then_inc(bias_done, 1)

        @block.vector
        def _(dve):
            v = Chain(dve, v_step)
            dve.wait_ge(bias_done, 1)
            dve.tensor_copy(brow[:], bps[:, :LB]).then_inc(brow_ready, 1)
            for t in range(3):
                r = ROWS[t]
                q = m.proj[:r, t, O_Q:O_Q + AW]
                k = view(m.proj[:r, t, O_KV + kv_flat:O_KV + kv_flat + 1], (kv_flat, 2), (2 * HD, NKV), (1, HD))
                v.mark(dve.tensor_tensor(view(sq[:r, 0, :], (1, AW)), q, q, ALU.mult))
                v.link(dve.tensor_tensor(view(sq[:r, NQ, :], (NKV * HD, 2), (HD, NKV), (1, HD)), k, k, ALU.mult))
                dve.tensor_reduce(ssq[:r, t, :], sq[:r], AX_X, ALU.add).then_inc(sum_done, 1)
                dve.wait_ge(sum_done, t + 1)
            for t in range(3):
                r = ROWS[t]
                q = view(m.proj[:r, t, O_Q:], (HD, NQ), (1, HD))
                k = view(m.proj[:r, t, O_KV + kv_flat:O_KV + kv_flat + 1], (kv_flat, 2), (2 * HD, NKV), (1, HD))
                dve.wait_ge(rms_done, t + 1)
                v.link(dve.reciprocal(rstd[:r, t, :], rms[:r, t, :]))
                v.mark(dve.tensor_tensor(q, q, view(rstd[:r, t, :], (1, NQ), (0, HD)), ALU.mult))
                v.link(dve.tensor_tensor(k, k, view(rstd[:r, t, NQ:], (NKV, 2), (1, NKV), (0, HD)), ALU.mult))
                gain_k = view(m.qkg[:r, 2, :], (HD, 2), (0, NKV), (1, HD))
                for p in range(2):
                    v.mark(dve.tensor_tensor(view(m.q_pairs[:r, t, p * 512:], (HD, 2), (2 * HD, G), (1, HD)),
                                             view(m.proj[:r, t, O_Q + p * 512:], (G * HD, 2), (HD, G), (1, HD)),
                                             view(m.qkg[:r, 0, :], (0, 2), (0, G), (1, HD)), ALU.mult))
                v.mark(dve.tensor_tensor(view(m.k_pairs[:r, t, :], (KVW, 2), (HD, NKV), (1, HD)), k, gain_k, ALU.mult))
                dve.tensor_tensor(k, k, gain_k, ALU.mult).then_inc(normed, 1)
            dve.wait_ge(bias_in, 16 * 3 * NS)
            dve.tensor_copy(m.bias_cmp[:, :NC_S - 7], view(m.bias_win[:, 100:101], (0, NC_S - 7)))
            dve.tensor_tensor(view(m.bias_new[:, 0, :], (NS, NB * NB), (1, NS)), view(m.const("own_seq"), (NS, NB * NB), (1, NS)),
                              view(near[:], (0, NB * NB), (1, NS)), ALU.add)

        @block.scalar
        def _(act):
            for t in range(3):
                r = ROWS[t]
                act.wait_ge(sum_done, t + 1)
                act.activation(rms[:r, t, :], ssq[:r, t, :], ACT.Sqrt, bias=m.eps[:r, :], scale=1.0 / HD).then_inc(rms_done, 1)
            for t in range(3):
                r = ROWS[2 - t]
                g = m.proj[:r, 2 - t, O_GATE:O_GATE + 48]
                act.activation(g, g, ACT.Sigmoid).then_inc(gate_done, 1)


class Compression:
    pass


class CompressSems:
    def __init__(self, m, who):
        self.turned, self.stored_v, self.stored_a = m.sem(who + "_turned"), m.sem(who + "_stored_v"), m.sem(who + "_stored_a")
        self.half_blocks, self.half_stored = m.sem(who + "_half_blocks"), m.sem(who + "_half_stored")
        self.pre_gelu, self.gelu = m.sem(who + "_pre_gelu"), m.sem(who + "_gelu")
        self.kv_made, self.kv_stored = m.sem(who + "_kv_made"), m.sem(who + "_kv_stored")


class CompressCounts:

    def __init__(self, b):
        self.turn, self.group, self.two, self.one = b * 16, b * 8, b * 2, b


def compress_pe(pe, m, z, b):
    s = z.s
    n_groups = 8 * z.tiles // 4
    for n in range(n_groups):
        if n >= 4:
            pe.wait_ge((s.stored_v, s.stored_a)[n % 2], b.group + ((n - 4) // 2 + 1))
        for c in range(4):
            hk, j = divmod(4 * n + c, z.tiles)
            kv, h = divmod(hk, NKV)
            pair = z.pages[:, j, (h * 2 + kv) * P:(h * 2 + kv + 1) * P]
            mm = pe.transpose(z.tps[:, n % 4, c * P:(c + 1) * P], pair, m.const("ident"))
        mm.then_inc(s.turned, 1)
        if (n + 1) % (n_groups // 2) == 0:
            kv = (n + 1) // (n_groups // 2) - 1
            pe.wait_ge(s.stored_v, b.group + (n // 2 + 1))
            pe.wait_ge(s.stored_a, b.group + (n + 1) // 2)
            for rp in range(8):
                mov = view(z.xT[:, rp:], (z.tiles * P, NKV), (8, z.hb))
                mm = pe.matmul(view(z.zps[:, kv, :], (z.hb, NKV), (1, z.hb)), m.w1[:, kv, rp, :], mov, start=(rp == 0), stop=(rp == 7))
            mm.then_inc(s.half_blocks, 1)
    n = z.hb - 1
    for kv in range(2):
        pe.wait_ge(s.half_stored, b.two + (kv + 1))
        out = view(z.gps[kv * HD:kv * HD + HD, :], (n, NKV), (1, n))
        for half in range(2):
            mm = pe.matmul(out, m.const("ident")[:, half * HD:half * HD + HD],
                           view(z.zz[:, kv, half:], (z.hb, NKV), (1, n)), start=(half == 0), stop=(half == 1))
    mm.then_inc(s.pre_gelu, 1)
    pe.wait_ge(s.gelu, b.one + 1)
    for h in range(NKV):
        mm = pe.matmul(z.ops[:n, h * HD:(h + 1) * HD], z.gel[HD:, h * n:(h + 1) * n], m.w2[HD:, :],
                       start=True, stop=True)
    for hh in range(2):
        mm = pe.matmul(view(z.zps[hh * HD:hh * HD + HD, 0, :], (n, 2), (1, n)), m.w2[:HD, :],
                       view(z.gel[:HD, hh * n:], (2 * n, 2), (1, n)), start=True, stop=True)
    mm.then_inc(s.kv_made, 1)


def compress_copy(eng, copy, m, z, b, me):
    s = z.s
    n_groups = 8 * z.tiles // 4
    for n in range(me, n_groups, 2):
        eng.wait_ge(s.turned, b.turn + (n + 1))
        o = n % (n_groups // 2) * 512
        copy(z.xT[:, o:o + 512], z.tps[:, n % 4, :]).then_inc((s.stored_v, s.stored_a)[me], 1)


def phase_compress(nc, m, io):
    with ExitStack() as ctx:
        sb = lambda n, sh: ctx.enter_context(nc.sbuf_tensor(n, sh, F32))
        pages = [sb(f"cmp_pages{u}", [P, 8, 2 * NKV * 2 * HD]) for u in range(2)]
        xT, zz, gel = sb("cmp_xT", [P, 4 * 8 * P]), sb("cmp_half", [P, 2, 512]), sb("cmp_gelu", [P, 512])
        ksq, kinv = sb("cmp_ksq", [P, 512]), sb("cmp_kinv", [P, 512])
        posb = sb("cmp_posb", [P, 1])
        m.w1, m.w2 = sb("cmp_w1s", [P, 2, 8, P]), sb("cmp_w2s", [P, HD])
        tps = ctx.enter_context(nc.psum_tensor("cmp_tps", [P, 4, 512], F32))
        zps = ctx.enter_context(nc.psum_tensor("cmp_zps", [P, 2, 512], F32))
        gps = ctx.enter_context(nc.psum_tensor("cmp_gps", [P, 512], F32))
        ops = ctx.enter_context(nc.psum_tensor("cmp_ops", [P, 512], F32))
        sems = [CompressSems(m, w) for w in ("pc", "sc")]
        w_in, pages_in0 = m.sem("cmp_w_in"), m.sem("p_pages_in")
        pages_in = [m.sem(f"cmp_pages_in{u}") for u in range(2)]
        pos_done, pos_ready, kn = m.sem("cmp_pos_done"), m.sem("cmp_pos_ready"), m.sem("kc_step")
        kn_sum, kn_rms, kc_inv = m.sem("kc_sum"), m.sem("kc_rms"), m.sem("kc_inv")
        zp, zs = Compression(), Compression()
        for z, z.s, z.tiles, z.hb in ((zp, sems[0], 1, 16), (zs, sems[1], 8, 128)):
            z.tps, z.zps, z.gps, z.ops, z.zz, z.gel, z.xT = tps, zps, gps, ops, zz, gel, xT
        zero = CompressCounts(0)
        block = ctx.enter_context(nc.Block())

        at = CompressCounts
        @block.sync
        def _(sp):
            for kv in range(2):
                for half in range(2):
                    sp.dma_start(m.w1[:, kv, :, half * HD:half * HD + HD],
                                 dram(io["cmp_w1"], (kv * 2048 + half * 1024) * HD, (HD, P), (P * HD, 8), (1, HD))).then_inc(w_in, 16)
            sp.dma_start(m.w2[:], dram(io["cmp_w2"], 0, (HD, P), (1, HD))).then_inc(w_in, 16)
            for hh in range(2):
                sp.dma_start(m.qkcol[hh * HD:hh * HD + HD, :], dram(io["qk_norm"], 0, (1, HD), (HD, 4))).then_inc(w_in, 16)
            sp.wait_ge(m.p_cmp_out, 32)
            for r2 in range(2):
                sp.dma_start(view(pages[1][:, 0, r2 * HD:], (P, 8), (1, HD)),
                             dram(io["p_kv_cmp"], r2 * 512, (1024, P), (HD, 8), (1, HD))).then_inc(pages_in0, 16)

            def load(b, u):
                for j in range(NPG):
                    r = sp.value_load(m.ptab[0:1, bass.ds(b * NPG + j, 1)], min_val=0, max_val=N_PHYS - 1)
                    page = io["cache_kv_cmp"][bass.ds(r, 1)].rearrange("n l (p q) h k d -> q p (n l h k) d", q=2)
                    for r2 in range(2):
                        sp.dma_start(view(pages[u][(j % 2) * 64:(j % 2) * 64 + 64, j // 2, r2 * HD:], (P, 8), (1, HD)),
                                     page[r2]).then_inc(pages_in[u], 16)

            load(0, 0)
            sp.wait_ge(sems[0].turned, 2)
            load(1, 1)
            with sp.Fori(1, NB // 2) as i:
                for u in range(2):
                    sp.wait_ge(sems[1].turned, i * 32 + (16 * u - 16))
                    load(2 * i + u, u)

        @block.tensor
        def _(pe):
            pe.wait_ge(w_in, 16 * 7)
            for kv in range(2):
                for n in range(16):
                    col = FEAT_AT["cmp_pos"][0] + kv * 16 + n
                    mm = pe.matmul(gps[kv * HD:kv * HD + HD, 0:1], m.w1[:, kv, n % 8, (n // 8) * HD:(n // 8) * HD + HD],
                                   m.feat[:, col:col + 1], start=(n == 0), stop=(n == 15))
            mm.then_inc(pos_done, 1)
            pe.wait_ge(pages_in0, 32)
            pe.wait_ge(pos_ready, 1)
            zp.pages = pages[1]
            compress_pe(pe, m, zp, zero)
            pe.wait_ge(sems[0].kv_stored, 2)
            with pe.Fori(0, NB // 2) as i:
                for u in range(2):
                    pe.wait_ge(pages_in[u], (i + 1) * (32 * NPG))
                    zs.pages = pages[u]
                    compress_pe(pe, m, zs, at(2 * i + u))
                    pe.wait_ge(sems[1].kv_stored, (2 * i + u) * 2 + 2)
            for c in range(5):
                n = 2 * NC_P if c == 4 else 4 * NC_S
                pe.wait_ge(kn, c + 1)
                if c:
                    pe.wait_ge(kn_rms, c)
                pe.matmul(gps[:, :n], m.const("half_ones"), ksq[:, :n], start=True, stop=True).then_inc(kn_sum, 1)

        @block.vector
        def _(dve):
            dve.wait_ge(pos_done, 1)
            dve.tensor_copy(posb[:], gps[:, 0:1]).then_inc(pos_ready, 1)

            def one(z, b, kdst):
                s, n = z.s, z.hb - 1
                compress_copy(dve, dve.tensor_copy, m, z, b, 0)
                dve.wait_ge(s.half_blocks, b.two + 1)
                dve.tensor_copy(zz[:, 0, :NKV * z.hb], zps[:, 0, :NKV * z.hb]).then_inc(s.half_stored, 1)
                dve.wait_ge(s.half_blocks, b.two + 2)
                dve.wait_ge(s.half_stored, b.two + 1)
                dve.tensor_copy(zz[:, 1, :NKV * z.hb], zps[:, 1, :NKV * z.hb]).then_inc(s.half_stored, 1)
                dve.wait_ge(s.kv_made, b.one + 1)
                dve.nop()
                dve.tensor_copy(kdst, zps[:, 0, :2 * n]).then_inc(s.kv_stored, 1)

            one(zp, zero, m.kc_p[:])
            with dve.Fori(0, NB // 2) as i:
                for u in range(2):
                    one(zs, at(2 * i + u), m.kc_s[:, bass.ds((2 * i + u) * 2 * NC_S, 2 * NC_S)])
            dve.wait_ge(sems[1].kv_stored, 2 * NB)
            gain = m.qkcol[:, 1:2]
            for c in range(5):
                n = 2 * NC_P if c == 4 else 4 * NC_S
                k = m.kc_p[:] if c == 4 else m.kc_s[:, c * n:(c + 1) * n]
                if c:
                    dve.wait_ge(kn_sum, c)
                dve.tensor_tensor(ksq[:, :n], k, k, ALU.mult).then_inc(kn, 1)
                dve.wait_ge(kn_rms, c + 1)
                dve.reciprocal(kinv[:, :n], kinv[:, :n]).then_inc(kc_inv, 1)
                dve.wait_ge(kc_inv, 2 * c + 1)
                dve.scalar_tensor_tensor(out=k, in0=k, scalar=gain, in1=kinv[:, :n], op0=ALU.mult, op1=ALU.mult).then_inc(kc_inv, 1)

        @block.scalar
        def _(act):
            def one(z, b, vdst):
                s, n = z.s, z.hb - 1
                compress_copy(act, act.copy, m, z, b, 1)
                act.wait_ge(s.pre_gelu, b.one + 1)
                act.activation(gel[:, :NKV * n], gps[:, :NKV * n], ACT.Gelu_apprx_tanh, bias=posb[:]).then_inc(s.gelu, 1)
                act.wait_ge(s.kv_made, b.one + 1)
                act.nop()
                act.copy(vdst, ops[:n, :KVW]).then_inc(s.kv_stored, 1)

            act.wait_ge(pos_ready, 1)
            one(zp, zero, m.vc_p[:])
            with act.Fori(0, NB // 2) as i:
                for u in range(2):
                    one(zs, at(2 * i + u), m.vc_s[:, bass.ds((2 * i + u) * KVW, KVW)])
            for c in range(5):
                n = 2 * NC_P if c == 4 else 4 * NC_S
                act.wait_ge(kn_sum, c + 1)
                if c:
                    act.wait_ge(kc_inv, 2 * c)
                act.activation(kinv[:, :n], gps[:, :n], ACT.Sqrt, bias=m.eps[:], scale=1.0 / HD).then_inc(kn_rms, 1)


def phase_turn_heads(nc, m, io):
    with ExitStack() as ctx:
        tps = ctx.enter_context(nc.psum_tensor("turn_tps", [P, 4, 512], F32))
        turned, stored_v, stored_a = m.sem("heads_turned"), m.sem("heads_stored_v"), m.sem("heads_stored_a")
        block = ctx.enter_context(nc.Block())

        @block.tensor
        def _(pe):
            for n in range(9):
                t, q = divmod(n, 3)
                r = ROWS[t]
                if n >= 4:
                    pe.wait_ge((stored_v, stored_a)[n % 2], (n - 4) // 2 + 1)
                for c in range(4):
                    src = m.q_pairs[:r, t, (4 * q + c) * P:][:, :P] if q < 2 else m.k_pairs[:r, t, c * P:(c + 1) * P]
                    mm = pe.transpose(tps[:, n % 4, c * P:c * P + r], src, m.const("ident")[:r, :r])
                mm.then_inc(turned, 1)

        def copy_out(eng, copy, me, sem):
            for n in range(me, 9, 2):
                t, q = divmod(n, 3)
                eng.wait_ge(turned, n + 1)
                copy(m.qkT[:, 4 * q:4 * q + 4, t * P:t * P + ROWS[t]], view(tps[:, n % 4, :], (P, 4), (1, ROWS[t]))).then_inc(sem, 1)

        @block.vector
        def _(dve):
            copy_out(dve, dve.tensor_copy, 0, stored_v)

        @block.scalar
        def _(act):
            copy_out(act, act.copy, 1, stored_a)


def phase_prompt_attention(nc, m, io):
    steps = [(t, h) for t in range(2) for h in range(NKV)]
    kv_flat = NKV * 2 * HD
    with ExitStack() as ctx:
        sb = lambda n, sh: ctx.enter_context(nc.sbuf_tensor(n, sh, F32))
        lg = [sb(f"pa_logits{u}", [P, 2, G, 2 * P]) for u in range(2)]
        lc = [sb(f"pa_logits_cmp{u}", [P, G, 16]) for u in range(2)]
        mx, nmx = sb("pa_max", [P, 12]), [sb(f"pa_neg_max{u}", [P, 12]) for u in range(2)]
        den = [sb(f"pa_den{u}", [P, 12]) for u in range(2)]
        rden, ok, fac = sb("pa_rden", [P, 12]), sb("pa_any_key", [P, 4]), sb("pa_fac", [P, 12])
        pT, pTc = sb("pa_pT", [P, 4, 512]), sb("pa_pTc", [NC_P, 512])
        osw, oc = sb("pa_osw", [P, 2, G * HD]), sb("pa_oc", [P, G * HD])
        S = ctx.enter_context(nc.psum_tensor("pa_S", [P, 4, 512], F32))
        X = ctx.enter_context(nc.psum_tensor("pa_X", [P, 512], F32))
        tps = ctx.enter_context(nc.psum_tensor("pa_tps", [P, 2, 512], F32))
        O = ctx.enter_context(nc.psum_tensor("pa_O", [P, 512], F32))
        bias_tri = sb("pa_bias", [P, NQ, 2 * P])
        n_ = lambda n: m.sem("pa_" + n)
        tri_in = n_("bias_in")
        logits, logits_read, neg_max, probs = n_("logits"), n_("logits_read"), n_("neg_max"), n_("probs")
        turned, stored_v, stored_a, pv, o_read, v_step = n_("turned"), n_("stored_v"), n_("stored_a"), n_("pv"), n_("o_read"), n_("v_step")
        block = ctx.enter_context(nc.Block())

        def groups(t):
            return [(0, 0)] + [(br, kt) for br in (1, 2) for kt in range(t + 1)]

        first = [0]
        for t, h in steps:
            first.append(first[-1] + len(groups(t)))

        @block.sync
        def _(sp):
            sp.wait_ge(m.rep_out, 16)
            sp.dma_start(bias_tri[:], dram(io["bias_rep"], P - 1, (NQ * TRI - 1, P), (TRI, NQ), (1, 2 * P))).then_inc(tri_in, 16)

        @block.tensor
        def _(pe):
            def score(i):
                t, h = steps[i]
                p, r0 = h // 2, h % 2 * HD
                if i:
                    pe.wait_ge(logits_read, i)
                    pe.wait_ge(o_read, i)
                nc_ = NC_P if t else 7
                for g in range(G):
                    q = m.qkT[r0:r0 + HD, p * G + g, t * P:t * P + P]
                    for br in range(2):
                        pe.matmul(S[:, br * 2 + g // 2, g % 2 * 256:g % 2 * 256 + (t + 1) * P], q,
                                  m.qkT[r0:r0 + HD, 8 + br * 2 + p, :(t + 1) * P], start=True, stop=True)
                    mm = pe.matmul(X[:, g * 16:g * 16 + nc_], q, m.kc_p[r0:r0 + HD, p * NC_P:p * NC_P + nc_], start=True, stop=True)
                mm.then_inc(logits, 1)

            score(0)
            for i, (t, h) in enumerate(steps):
                nc_ = NC_P if t else 7
                pe.wait_ge(probs, i + 1)
                for j, (br, kt) in enumerate(groups(t)):
                    n = first[i] + j
                    if n >= 2:
                        pe.wait_ge((stored_v, stored_a)[n % 2], n // 2)
                    for g in range(G):
                        if br:
                            mm = pe.transpose(tps[:, n % 2, g * P:(g + 1) * P], lg[i % 2][:, br - 1, g, kt * P:(kt + 1) * P], m.const("ident"))
                        else:
                            mm = pe.transpose(tps[:nc_, n % 2, g * P:(g + 1) * P], lc[i % 2][:, g, :nc_], m.const("ident"))
                    mm.then_inc(turned, 1)
                n = first[i + 1]
                pe.wait_ge(stored_v, (n + 1) // 2)
                pe.wait_ge(stored_a, n // 2)
                for g in range(G):
                    pe.matmul(X[:, 256 + g * HD:256 + (g + 1) * HD], pTc[:nc_, g * P:(g + 1) * P],
                              m.vc_p[:nc_, h * HD:(h + 1) * HD], start=True, stop=True)
                    for br in (1, 2):
                        for kt in range(t + 1):
                            v = O_KV + br * kv_flat + h * 2 * HD + HD
                            mm = pe.matmul(O[:, (br - 1) * 256 + g * HD:(br - 1) * 256 + (g + 1) * HD],
                                           pT[:, (br - 1) * 2 + kt, g * P:(g + 1) * P], m.proj[:, kt, v:v + HD],
                                           start=(kt == 0), stop=(kt == t))
                mm.then_inc(pv, 1)
                if i + 1 < len(steps):
                    score(i + 1)

        def copy_groups(eng, copy, me, sem, i):
            t, h = steps[i]
            nc_ = NC_P if t else 7
            for j, (br, kt) in enumerate(groups(t)):
                n = first[i] + j
                if n % 2 == me:
                    eng.wait_ge(turned, n + 1)
                    if i:
                        eng.wait_ge(pv, i)
                    if br:
                        copy(pT[:, (br - 1) * 2 + kt, :], tps[:, n % 2, :]).then_inc(sem, 1)
                    else:
                        copy(pTc[:nc_, :], tps[:nc_, n % 2, :]).then_inc(sem, 1)

        @block.vector
        def _(dve):
            v = Chain(dve, v_step)
            dve.wait_ge(tri_in, 16)
            for i, (t, h) in enumerate(steps):
                nk, nc_ = (t + 1) * P, NC_P if t else 7
                L, Lc = lg[i % 2], lc[i % 2]
                tri = bias_tri[:, h * G, (1 - t) * P:]
                dve.wait_ge(logits, i + 1)
                for br in range(2):
                    v.mark(dve.scalar_tensor_tensor(out=view(L[:, br, 0, :], (2 * P, G), (1, nk)), in0=view(S[:, br * 2, :], (256, G), (1, nk)),
                                                    scalar=SCALE, in1=view(tri, (2 * P, G), (1, nk)), op0=ALU.mult, op1=ALU.add))
                dve.scalar_tensor_tensor(out=Lc[:, :, :nc_], in0=view(X[:], (16, G), (1, nc_)), scalar=SCALE,
                                         in1=view(bias_tri[:, h * G, (1 - t) * P + 31:], (2 * P, G), (16, nc_)),
                                         op0=ALU.mult, op1=ALU.add).then_inc(logits_read, 1)
                v.wait()
                dve.wait_ge(logits_read, i + 1)
                v.mark(dve.tensor_reduce(mx[:, 4:12], view(L[:, 0, 0, :], (2 * P, 2 * G), (1, nk)), AX_X, ALU.max))
                v.link(dve.tensor_reduce(mx[:, 0:4], Lc[:, :, :nc_], AX_X, ALU.max))
                dve.tensor_scalar(nmx[i % 2][:], mx[:], -1.0, None, ALU.mult).then_inc(neg_max, 1)
                dve.wait_ge(neg_max, i + 1)
                v.mark(dve.tensor_scalar(ok[:], nmx[i % 2][:, 0:4], 1e29, None, ALU.is_lt))
                dve.wait_ge(probs, i + 1)
                v.link(dve.reciprocal(rden[:], den[i % 2][:]))
                gates = view(m.proj[:, t, O_GATE + h * G:], (NQ, 3), (1, G))
                v.link(dve.tensor_tensor(view(fac[:], (G, 3), (1, G)), view(rden[:], (G, 3), (1, G)), gates, ALU.mult))
                v.link(dve.tensor_tensor(fac[:, 0:4], fac[:, 0:4], ok[:], ALU.mult))
                copy_groups(dve, dve.tensor_copy, 0, stored_v, i)
                dve.wait_ge(pv, i + 1)
                o = m.proj[:, t, O_Q + h * G * HD:O_Q + (h + 1) * G * HD]
                v.mark(dve.tensor_tensor(view(osw[:, 0, :], (HD, 2 * G), (1, HD)), view(O[:], (HD, 2 * G), (1, HD)), view(fac[:, 4:], (1, 2 * G), (0, HD)), ALU.mult))
                v.link(dve.tensor_tensor(view(oc[:], (HD, G), (1, HD)), view(X[:, 256:], (HD, G), (1, HD)), view(fac[:], (1, G), (0, HD)), ALU.mult))
                v.link(dve.tensor_tensor(oc[:], oc[:], osw[:, 0, :], ALU.add))
                dve.tensor_tensor(o, oc[:], osw[:, 1, :], ALU.add).then_inc(o_read, 1)
                dve.wait_ge(o_read, i + 1)

        @block.scalar
        def _(act):
            for i, (t, h) in enumerate(steps):
                nk, nc_ = (t + 1) * P, NC_P if t else 7
                L, Lc = lg[i % 2], lc[i % 2]
                act.wait_ge(neg_max, i + 1)
                for g in range(G):
                    act.activation(Lc[:, g, :nc_], Lc[:, g, :nc_], ACT.Exp, bias=nmx[i % 2][:, g:g + 1], accum_out=den[i % 2][:, g:g + 1])
                    for br in range(2):
                        c = 4 + br * G + g
                        e = act.activation(L[:, br, g, :nk], L[:, br, g, :nk], ACT.Exp, bias=nmx[i % 2][:, c:c + 1], accum_out=den[i % 2][:, c:c + 1])
                e.then_inc(probs, 1)
                copy_groups(act, act.copy, 1, stored_a, i)


def phase_sample_attention(nc, m, io):
    kv_flat = NKV * 2 * HD
    NK = PAST + NTS
    with ExitStack() as ctx:
        sb = lambda n, sh: ctx.enter_context(nc.sbuf_tensor(n, sh, F32))
        pages, wrows = sb("sel_pages", [P, NPG, kv_flat]), sb("win_rows", [P, 4, kv_flat])
        kT, wkT = sb("sel_kT", [P, 2, PAST]), sb("win_kT", [P, 2, WIN])
        qb, kcb, gb = sb("q_blocks", [P, 2, 64]), sb("kc_b", [P, 2 * NC_S]), sb("gate_b", [P, 3])
        Ls, Lw, Lc = sb("sel_logits", [P, NK]), sb("win_logits", [P, WIN + NTS]), sb("cmp_logits", [P, NC_S])
        mx, nmx, den, rden, fac = sb("sa_max", [P, 3]), sb("sa_neg_max", [P, 3]), sb("sa_den", [P, 3]), sb("sa_rden", [P, 3]), sb("sa_fac", [P, 3])
        pT, pTw, pTc = sb("sel_pT", [P, (NPG + 1) * P]), sb("win_pT", [P, 5 * P]), sb("cmp_pT", [NC_S, P])
        U, sc, top8 = sb("blk_part", [P, NBLK]), sb("blk_score", [P, NBLK]), sb("blk_top8", [P, 8])
        mask, mb, tail = sb("blk_mask", [P, NBLK]), sb("blk_bias", [P, NBLK]), sb("blk_tail", [P, P])
        osum = sb("sa_out", [P, HD])
        psm = lambda n, sh: ctx.enter_context(nc.psum_tensor(n, sh, F32))
        tps, S, X, O = psm("sa_tps", [P, 2, 512]), psm("sa_S", [P, 4, 512]), psm("sa_X", [P, 512]), psm("sa_O", [P, 512])
        n_ = lambda n: m.sem("sa_" + n)
        sel_in, win_in, pages_used, wrows_used = n_("sel_in"), n_("win_in"), n_("pages_used"), n_("wrows_used")
        q_ready, x_ready, turned, stored_v, stored_a = n_("q_ready"), n_("x_ready"), n_("turned"), n_("stored_v"), n_("stored_a")
        win_ready, early_read, neg_c, neg_w, neg_s = n_("win_ready"), n_("early_read"), n_("neg_c"), n_("neg_w"), n_("neg_s")
        exp_c, exp_w, exp_s, pc_ready = n_("exp_c"), n_("exp_w"), n_("exp_s"), n_("pc_ready")
        u_ready, u_stored, score_ready, score_read = n_("u_ready"), n_("u_stored"), n_("score_ready"), n_("score_read")
        oc_ready, oc_read, sel_ready, sel_read, o_ready, o_done, o_out = (n_("oc_ready"), n_("oc_read"), n_("sel_ready"),
                                                                         n_("sel_read"), n_("o_ready"), n_("o_done"), n_("o_out"))
        o_free = n_("o_free")
        zeroed, v_step, o_back = n_("zeroed"), n_("v_step"), n_("o_back")
        block = ctx.enter_context(nc.Block())
        NG = 9

        @block.sync
        def _(sp):
            def load(b):
                for kv in range(2):
                    src = io["cache_kv_win"][bass.ds(b, 1)].rearrange("b l (t p) h k d -> k t p (b l h) d", p=P)[kv]
                    for t in range(4):
                        sp.dma_start(view(wrows[:, t, kv * KVW:], (HD, NKV), (1, HD)), src[t]).then_inc(win_in, 16)
                for j in range(NPG):
                    r = sp.value_load(m.ptab[0:1, bass.ds(b * NPG + j, 1)], min_val=0, max_val=N_PHYS - 1)
                    page = io["cache_kv_sel"][bass.ds(r, 1)].rearrange("n l p h k d -> k p (n l h) d")
                    for kv in range(2):
                        sp.dma_start(view(pages[:, j, kv * KVW:], (HD, NKV), (1, HD)), page[kv]).then_inc(sel_in, 16)

            sp.sem_inc(o_free, 1)
            load(0)
            with sp.Fori(1, NB) as b:
                sp.wait_ge(wrows_used, b)
                sp.wait_ge(pages_used, b)
                load(b)
                sp.wait_ge(o_done, b)
                sp.dma_start(io["o_rows"][bass.ds(b - 1, 1)].rearrange("b p d -> p (b d)"), osum[:]).then_inc(o_out, 16)
                sp.wait_ge(o_out, b * 16)
                sp.sem_inc(o_free, 1)
            sp.wait_ge(o_done, NB)
            sp.dma_start(io["o_rows"][NB - 1], osum[:]).then_inc(o_out, 16)
            sp.wait_ge(o_out, 16 * NB)
            for b in range(NB):
                sp.dma_start(view(m.proj[b * NS:b * NS + NS, 2, O_Q:], (HD, NQ), (1, HD)),
                             dram(io["o_rows"], b * P * HD, (HD, NS), (NS * HD, NQ), (1, HD))).then_inc(o_back, 16)
            sp.wait_ge(o_back, 16 * NB)

        @block.tensor
        def _(pe):
            with pe.Fori(0, NB) as b:
                def bank(n):
                    if n >= 2:
                        pe.wait_ge((stored_v, stored_a)[n % 2], b * NG + n // 2)

                pe.wait_ge(q_ready, b + 1)
                for p in range(2):
                    pe.matmul(X[p * 64:p * 64 + 64, 256:256 + NTS], qb[:, p, :], m.qkT[:, 10 + p, 2 * P:], start=True, stop=True)
                for p in range(2):
                    mm = pe.matmul(X[p * 64:p * 64 + 64, :NC_S], qb[:, p, :], kcb[:, p * NC_S:(p + 1) * NC_S], start=True, stop=True)
                mm.then_inc(x_ready, 1)
                pe.wait_ge(win_in, (b + 1) * (16 * 8))
                for p in range(2):
                    for t in range(4):
                        mm = pe.transpose(tps[:, p, t * P:(t + 1) * P], wrows[:, t, p * P:(p + 1) * P], m.const("ident"))
                    mm.then_inc(turned, 1)
                pe.wait_ge(stored_v, b * NG + 1)
                pe.wait_ge(stored_a, b * NG + 1)
                for p in range(2):
                    mm = pe.matmul(S[p * 64:p * 64 + 64, 0, :], qb[:, p, :], wkT[:, p, :], start=True, stop=True)
                mm.then_inc(win_ready, 1)
                pe.wait_ge(sel_in, (b + 1) * (16 * 2 * NPG))
                for n in range(2, 10):
                    quad, p = divmod(n - 2, 2)
                    bank(n)
                    for t in range(4):
                        mm = pe.transpose(tps[:, n % 2, t * P:(t + 1) * P], pages[:, quad * 4 + t, p * P:(p + 1) * P], m.const("ident"))
                    mm.then_inc(turned, 1)
                bank(10)
                pe.wait_ge(pc_ready, b + 1)
                pe.transpose(tps[:NC_S, 0, :P], Lc[:], m.const("ident")).then_inc(turned, 1)
                pe.wait_ge(stored_v, b * NG + 6)
                pe.matmul(X[:, 128:128 + NBLK], pTc[:], m.const("overlap"), start=True, stop=True).then_inc(u_ready, 1)
                pe.wait_ge(early_read, b + 1)
                pe.matmul(S[:, 1, :KVW], pTc[:], m.vc_s[:, bass.ds(b * KVW, KVW)], start=True, stop=True).then_inc(oc_ready, 1)
                pe.wait_ge(u_stored, b + 1)
                pe.matmul(X[:, 192:192 + NBLK], m.const("sum_group"), U[:], start=True, stop=True).then_inc(score_ready, 1)
                pe.wait_ge(exp_w, b + 1)
                for n, tiles in ((11, (0, 1, 2)), (12, (3, 4))):
                    bank(n)
                    for c, t in enumerate(tiles):
                        w = P if t < 4 else NTS
                        mm = pe.transpose(tps[:w, n % 2, c * P:(c + 1) * P], Lw[:, t * P:t * P + w], m.const("ident"))
                    mm.then_inc(turned, 1)
                pe.wait_ge(stored_v, b * NG + 5)
                pe.wait_ge(stored_a, b * NG + 5)
                pe.wait_ge(oc_read, b + 1)
                for c in range(4):
                    for p in range(2):
                        mm = pe.matmul(S[p * 64:p * 64 + 64, c, :], qb[:, p, :], kT[:, p, c * 512:(c + 1) * 512], start=True, stop=True)
                    mm.then_inc(sel_ready, 1)
                pe.wait_ge(score_read, b + 1)
                for p in range(2):
                    mm = pe.matmul(X[p * 64:p * 64 + 64, 320:320 + NTS], qb[:, p, :], m.qkT[:, 8 + p, 2 * P:], start=True, stop=True)
                mm.then_inc(sel_ready, 1)
                new_v = lambda br: view(m.proj[:NTS, 2, O_KV + br * kv_flat + HD:], (2 * HD, NKV), (1, HD))
                pe.wait_ge(stored_a, b * NG + 6)
                pe.wait_ge(stored_v, b * NG + 7)
                for t in range(4):
                    mm = pe.matmul(O[:, KVW:], pTw[:, t * P:(t + 1) * P], wrows[:, t, KVW:], start=(t == 0), stop=False)
                mm = pe.matmul(O[:, KVW:], pTw[:NTS, 4 * P:], new_v(2), start=False, stop=True)
                mm.then_inc(wrows_used, 1)
                pe.wait_ge(exp_s, b + 1)
                for n, (lo, hi) in ((13, (0, 4)), (14, (4, 8)), (15, (8, 12)), (16, (12, 15)), (17, (15, 17))):
                    bank(n)
                    for t in range(lo, hi):
                        w = P if t < NPG else NTS
                        mm = pe.transpose(tps[:w, n % 2, (t - lo) * P:(t - lo + 1) * P], Ls[:, t * P:t * P + w], m.const("ident"))
                    mm.then_inc(turned, 1)
                pe.wait_ge(stored_v, b * NG + 9)
                pe.wait_ge(stored_a, b * NG + 9)
                for t in range(NPG):
                    mm = pe.matmul(O[:, :KVW], pT[:, t * P:(t + 1) * P], pages[:, t, KVW:], start=(t == 0), stop=False)
                mm.then_inc(pages_used, 1)
                pe.matmul(O[:, :KVW], pT[:NTS, NPG * P:], new_v(1), start=False, stop=True).then_inc(o_ready, 1)

        def copy_turned(eng, copy, b, me, sem, n):
            src = tps[:, n % 2, :]
            if n < 2:
                pairs = [(wkT[:, n, :], src)]
            elif n < 10:
                quad, p = divmod(n - 2, 2)
                pairs = [(kT[:, p, quad * 512:(quad + 1) * 512], src)]
            elif n == 10:
                pairs = [(pTc[:], tps[:NC_S, 0, :P])]
            elif n == 11:
                pairs = [(pTw[:, :3 * P], src[:, :3 * P])]
            elif n == 12:
                pairs = [(pTw[:, 3 * P:4 * P], src[:, :P]), (pTw[:NTS, 4 * P:], src[:NTS, P:2 * P])]
            elif n == 17:
                pairs = [(pT[:, 15 * P:16 * P], src[:, :P]), (pT[:NTS, 16 * P:], src[:NTS, P:2 * P])]
            else:
                w = 3 if n == 16 else 4
                pairs = [(pT[:, (n - 13) * 4 * P:((n - 13) * 4 + w) * P], src[:, :w * P])]
            eng.wait_ge(turned, b * (2 * NG) + (n + 1))
            for dst, s_ in pairs:
                c = copy(dst, s_)
            c.then_inc(sem, 1)

        @block.vector
        def _(dve):
            dve.memset(qb[:], 0.0).then_inc(zeroed, 1)
            dve.wait_ge(zeroed, 1)
            with dve.Fori(0, NB) as b:
                v = Chain(dve, v_step, b * m.SA_V)
                out = lambda n: copy_turned(dve, dve.tensor_copy, b, 0, stored_v, n)
                for hh in range(2):
                    r0 = hh * HD
                    dve.tensor_copy(view(qb[r0:r0 + HD, 0, hh * 32:], (64, 2), (NS, G), (1, NS)),
                                         view(m.qkT[r0:r0 + HD, 0, bass.ds(b * NS + 2 * P, NS)], (G * T, 2), (T, G), (1, NS)))
                dve.tensor_copy(kcb[:], m.kc_s[:, bass.ds(b * (2 * NC_S), 2 * NC_S)]).then_inc(q_ready, 1)
                v.mark(dve.tensor_copy(gb[:], view(m.gate_s[:, 0, bass.ds(b, 1)], (NB, 3))))
                dve.wait_ge(x_ready, b + 1)
                v.mark(dve.scalar_tensor_tensor(out=Lc[:], in0=X[:, :NC_S], scalar=SCALE, in1=m.bias_cmp[:], op0=ALU.mult, op1=ALU.add))
                dve.wait_ge(x_ready, b + 1)
                v.link(dve.scalar_tensor_tensor(out=Lw[:, WIN:], in0=X[:, 256:256 + NTS], scalar=SCALE,
                                                in1=m.bias_new[:, bass.ds(b, 1), :].rearrange("p a b -> p (a b)"), op0=ALU.mult, op1=ALU.add))
                v.link(dve.tensor_reduce(mx[:, 0:1], Lc[:], AX_X, ALU.max))
                dve.tensor_scalar(nmx[:, 0:1], mx[:, 0:1], -1.0, None, ALU.mult).then_inc(neg_c, 1)
                out(0)
                dve.wait_ge(win_ready, b + 1)
                dve.scalar_tensor_tensor(out=Lw[:, :WIN], in0=S[:, 0, :], scalar=SCALE, in1=m.bias_win[:], op0=ALU.mult, op1=ALU.add).then_inc(early_read, 1)
                dve.wait_ge(early_read, b + 1)
                v.link(dve.tensor_reduce(mx[:, 1:2], Lw[:], AX_X, ALU.max))
                dve.tensor_scalar(nmx[:, 1:2], mx[:, 1:2], -1.0, None, ALU.mult).then_inc(neg_w, 1)
                for n in (2, 4, 6, 8):
                    out(n)
                dve.wait_ge(exp_c, b + 1)
                v.link(dve.reciprocal(rden[:, 0:1], den[:, 0:1]))
                dve.tensor_scalar(Lc[:], Lc[:], rden[:, 0:1], None, ALU.mult).then_inc(pc_ready, 1)
                out(10)
                dve.wait_ge(u_ready, b + 1)
                dve.tensor_copy(U[:], X[:, 128:128 + NBLK]).then_inc(u_stored, 1)
                dve.wait_ge(oc_ready, b + 1)
                dve.wait_ge(o_free, b + 1)
                for h in range(NKV):
                    r = slice(h * 32, h * 32 + 32)
                    cp = dve.tensor_scalar(osum[r, :], S[r, 1, h * HD:(h + 1) * HD], gb[r, 0:1], None, ALU.mult)
                cp.then_inc(oc_read, 1)
                dve.wait_ge(score_ready, b + 1)
                dve.tensor_tensor(sc[:], X[:, 192:192 + NBLK], m.const("sel_keep"), ALU.mult).then_inc(score_read, 1)
                dve.wait_ge(score_read, b + 1)
                v.link(dve.tensor_tensor(sc[:], sc[:], m.const("sel_force"), ALU.add))
                for _ in range(TOPK // 8):
                    dve.nop(nofuse=True)
                    v.link(dve.max(top8[:], sc[:]))
                    dve.nop(nofuse=True)
                    v.link(dve.match_replace(sc[:], top8[:], sc[:], NEG))
                v.link(dve.tensor_scalar(mask[:], sc[:], NEG / 10, NEG, ALU.is_gt, ALU.mult))
                v.mark(dve.tensor_scalar(mb[:], mask[:], m.bias_win[:, 100:101], None, ALU.add))
                v.link(dve.tensor_tensor(view(tail[:], (SELB, 2), (1, SELB)), view(m.bias_win[:, WIN - P:], (SELB, 2), (1, SELB)),
                                         view(mask[:, NBLK - 3:], (1, 2), (0, SELB)), ALU.add))
                out(12)
                for c in range(4):
                    dve.wait_ge(sel_ready, b * 5 + (c + 1))
                    w = 8 if c < 3 else 6
                    ins = dve.scalar_tensor_tensor(out=view(Ls[:, c * 512:], (SELB, w), (1, SELB)), in0=view(S[:, c, :], (SELB, w), (1, SELB)), scalar=SCALE,
                                                   in1=view(mb[:, c * 8:], (1, w), (0, SELB)), op0=ALU.mult, op1=ALU.add)
                    v.mark(ins)
                v.mark(dve.scalar_tensor_tensor(out=Ls[:, PAST - P:PAST], in0=S[:, 3, 384:], scalar=SCALE, in1=tail[:], op0=ALU.mult, op1=ALU.add))
                dve.wait_ge(sel_ready, b * 5 + 5)
                v.link(dve.scalar_tensor_tensor(out=Ls[:, PAST:], in0=X[:, 320:320 + NTS], scalar=SCALE,
                                                in1=m.bias_new[:, bass.ds(b, 1), :].rearrange("p a b -> p (a b)"), op0=ALU.mult, op1=ALU.add))
                v.link(dve.tensor_reduce(mx[:, 2:3], Ls[:], AX_X, ALU.max))
                dve.tensor_scalar(nmx[:, 2:3], mx[:, 2:3], -1.0, None, ALU.mult).then_inc(neg_s, 1)
                out(14)
                out(16)
                v.link(dve.reciprocal(rden[:, 1:3], den[:, 1:3]))
                v.mark(dve.tensor_tensor(fac[:, 1:2], rden[:, 1:2], gb[:, 2:3], ALU.mult))
                v.link(dve.tensor_tensor(fac[:, 2:3], rden[:, 2:3], gb[:, 1:2], ALU.mult))
                dve.wait_ge(o_ready, b + 1)
                for part, col in ((2, 1), (1, 2)):
                    for h in range(NKV):
                        r = slice(h * 32, h * 32 + 32)
                        c0 = (KVW if part == 2 else 0) + h * HD
                        ins = dve.scalar_tensor_tensor(out=osum[r, :], in0=O[r, c0:c0 + HD], scalar=fac[r, col:col + 1], in1=osum[r, :], op0=ALU.mult, op1=ALU.add)
                        if part == 1 and h == NKV - 1:
                            ins.then_inc(o_done, 1)
                        else:
                            v.mark(ins)
                    if part == 2:
                        v.wait()
                dve.wait_ge(o_done, b + 1)
                m.SA_V_seen = v.n

        @block.scalar
        def _(act):
            with act.Fori(0, NB) as b:
                out = lambda n: copy_turned(act, act.copy, b, 1, stored_a, n)
                out(1)
                act.wait_ge(neg_c, b + 1)
                act.activation(Lc[:], Lc[:], ACT.Exp, bias=nmx[:, 0:1], accum_out=den[:, 0:1]).then_inc(exp_c, 1)
                act.wait_ge(neg_w, b + 1)
                act.activation(Lw[:], Lw[:], ACT.Exp, bias=nmx[:, 1:2], accum_out=den[:, 1:2]).then_inc(exp_w, 1)
                for n in (3, 5, 7, 9, 11):
                    out(n)
                act.wait_ge(neg_s, b + 1)
                act.activation(Ls[:], Ls[:], ACT.Exp, bias=nmx[:, 2:3], accum_out=den[:, 2:3]).then_inc(exp_s, 1)
                for n in (13, 15, 17):
                    out(n)


TWO_PI_HI = 6.28125
TWO_PI_LO = float(2 * np.pi - 6.28125)
ROUND = 12582912.0
SG, SN, SC = 32, 64, 16
ST = SG * SN // P
CH = 16


def phase_s5(nc, m, io):
    with ExitStack() as ctx:
        sb = lambda n, sh: ctx.enter_context(nc.sbuf_tensor(n, sh, F32))
        ldt, A = sb("s5_dt", [P, ST]), sb("s5_small", [P, 16, ST])
        braw, bb, bx = sb("s5_b", [P, 2, ST, SC]), sb("s5_bb", [P, 3, ST, SC]), sb("s5_bx", [P, 2, ST, 2, SC])
        craw, cx = sb("s5_c", [P, 2, 4, SN]), sb("s5_cx", [P, 2, 4, 2, SN])
        BT, CT = sb("s5_BT", [P, 2, 4, P]), sb("s5_CT", [P, 2, 4, P])
        uT, H = sb("s5_uT", [P, 4, T]), sb("s5_H", [P, 2, ST, T])
        h0r, h0 = sb("s5_h0rows", [P, 2, P]), sb("s5_h0", [P, 2, NB, ST])
        a2, ai2 = sb("s5_a_re", [P, 2, ST]), sb("s5_a_im_signed", [P, 2, ST])
        t1, t2 = sb("s5_t1", [P, 2, ST, CH]), sb("s5_t2", [P, 2, ST, CH])
        q1, q2 = sb("s5_q1", [P, 2, ST, NB]), sb("s5_q2", [P, 2, ST, NB])
        pw, carry = sb("s5_powers", [P, 2, ST, CH]), sb("s5_carry", [P, 2, ST, CH])
        fx = sb("s5_fix", [P, 2, 4, (CH - 1) * CH])
        endp, ends, endrow = sb("s5_end_p", [P, 2, ST]), sb("s5_end_s", [P, 2, NB, ST]), sb("s5_end_rows", [P, 3, P])
        glu, y, yg, sg = sb("s5_glu_w", [P, 4, 512]), sb("s5_y", [P, 4, T]), sb("s5_yg", [P, 4, T]), sb("s5_sig", [P, 4, T])
        tps = ctx.enter_context(nc.psum_tensor("s5_tps", [P, 4, 512], F32))
        yps = ctx.enter_context(nc.psum_tensor("s5_yps", [P, 4, 512], F32))
        n_ = lambda n: m.sem("s5_" + n)
        in_done, v_step, a_dt, v_arg, a_sin = n_("in"), n_("v_step"), n_("dt"), n_("arg"), n_("sin")
        bx_ready, turned, stored, x_made, x_stored = n_("bx_ready"), n_("turned"), n_("stored"), n_("x_made"), n_("x_stored")
        init, pool_step, p_done, s_done = n_("sample_ready"), n_("pool_step"), n_("prompt_done"), n_("sample_done")
        y_made, y_ready, gelu, z_made, sig, sq_ready = n_("y_made"), n_("y_ready"), n_("gelu"), n_("z_made"), n_("sig"), n_("sq_ready")
        n_ready, n_high = n_("norm_ready"), n_("norm_high")
        sum_made, rms, ends_ready, ends_turned, ends_stored = n_("sum_made"), n_("rms"), n_("ends_ready"), n_("ends_turned"), n_("ends_stored")
        block = ctx.enter_context(nc.Block())
        AR, AI = m.feat[:, FEAT_AT["ssm_a_re"][0]:][:, :ST], m.feat[:, FEAT_AT["ssm_a_im"][0]:][:, :ST]

        @block.sync
        def _(sp):
            for par in range(2):
                sp.dma_start(ldt[par * SN:(par + 1) * SN, :], dram(io["ssm_log_dt"], par, (0, SN), (2, ST))).then_inc(in_done, 16)
            for ri, src in enumerate((io["ssm_b_re"], io["ssm_b_im"])):
                sp.dma_start(braw[:, ri], dram(src, 0, (SC, P), (P * SC, ST), (1, SC))).then_inc(in_done, 16)
            for ri, src in enumerate((io["ssm_c_re"], io["ssm_c_im"])):
                sp.dma_start(craw[:, ri], dram(src, 0, (SN, P), (P * SN, 4), (1, SN))).then_inc(in_done, 16)
            for ri, src in enumerate((io["state_ssm_re"], io["state_ssm_im"])):
                sp.dma_start(h0r[:, ri, :], dram(src, 0, (P, P), (1, P))).then_inc(in_done, 16)
            sp.dma_start(glu[:], dram(io["ssm_glu_w"], 0, (512, P), (P * 512, 4), (1, 512))).then_inc(in_done, 16)
            sp.wait_ge(ends_stored, 3)
            m.store(sp, dram(io["s_ssm_re"], 0, (P, P), (1, P)), endrow[:, 0, :])
            m.store(sp, dram(io["s_ssm_im"], 0, (P, P), (1, P)), endrow[:, 1, :])
            m.store(sp, dram(io["p_ssm_re"], 0, (P, ST), (1, P)), endrow[:ST, 2, :])
            m.store(sp, dram(io["p_ssm_im"], 0, (P, ST), (1, P)), endrow[ST:2 * ST, 2, :])

        N_IN = 16 * 9
        @block.tensor
        def _(pe):
            pe.wait_ge(in_done, N_IN)
            I = m.const("ident")
            n = 0
            for t in range(3):
                if n >= 4:
                    pe.wait_ge(stored, n - 3)
                for k in range(4):
                    mm = pe.transpose(tps[:, n % 4, k * P:k * P + ROWS[t]], m.proj[:ROWS[t], t, O_U + k * P:O_U + (k + 1) * P], I[:ROWS[t], :ROWS[t]])
                mm.then_inc(turned, 1)
                n += 1
            for ri in range(2):
                mm = pe.transpose(tps[:, 3, ri * P:(ri + 1) * P], h0r[:, ri, :], I)
            mm.then_inc(turned, 1)
            pe.wait_ge(bx_ready, 2)
            for n, (src, ri) in enumerate(((bx, 0), (bx, 1), (cx, 0), (cx, 1)), 4):
                pe.wait_ge(stored, n - 3)
                for k in range(4):
                    w = view(src[:, ri, 4 * k, 0, :] if src is bx else src[:, ri, k, 0, :], (1, P))
                    mm = pe.transpose(tps[:, n % 4, k * P:(k + 1) * P], w, I)
                mm.then_inc(turned, 1)
            pe.wait_ge(stored, 8)
            for j in range(2 * ST):
                ri, i = divmod(j, ST)
                r0 = i % 4 * 32
                if j >= 4:
                    pe.wait_ge(x_stored, j - 3)
                pe.matmul(tps[:, j % 4, :T], BT[r0:r0 + 32, ri, i // 4, :], uT[r0:r0 + 32, i // 4, :], start=True, stop=True).then_inc(x_made, 1)
            pe.wait_ge(p_done, 2)
            pe.wait_ge(s_done, 1)
            for i in range(ST):
                r0 = i % 4 * 32
                for ri in range(2):
                    mm = pe.matmul(yps[r0:r0 + 32, i // 4, :T], CT[:, ri, i // 4, r0:r0 + 32], H[:, ri, i, :], start=(ri == 0), stop=(ri == 1))
                if i % 4 == 3:
                    mm.then_inc(y_made, 1)
            pe.wait_ge(ends_ready, 1)
            pe.wait_ge(x_stored, 2 * ST)
            for ri in range(2):
                pe.transpose(tps[:, ri, :P], view(ends[:, ri, 0, :], (1, P)), I).then_inc(ends_turned, 1)
            pe.transpose(tps[:2 * ST, 2, :P], view(endp[:, 0, :], (1, 2 * ST)), I).then_inc(ends_turned, 1)
            pe.wait_ge(y_ready, 4)
            pe.wait_ge(gelu, 4)
            for mo in range(4):
                for k in range(4):
                    mm = pe.matmul(yps[:, mo, :T], glu[:, k, mo * P:(mo + 1) * P], yg[:, k, :], start=(k == 0), stop=(k == 3))
                mm.then_inc(z_made, 1)
            pe.wait_ge(ends_stored, 3)
            pe.wait_ge(sq_ready, 4)
            for mo in range(4):
                mm = pe.matmul(tps[:, 3, :T], m.const("ones"), y[:, mo, :], start=(mo == 0), stop=(mo == 3))
            mm.then_inc(sum_made, 1)

        @block.scalar
        def _(act):
            act.wait_ge(in_done, N_IN)
            act.activation(ldt[:], ldt[:], ACT.Exp).then_inc(a_dt, 1)
            act.wait_ge(v_arg, 1)
            act.activation(A[:, 0, :], A[:, 0, :], ACT.Exp).then_inc(a_dt, 1)
            act.wait_ge(v_arg, 2)
            act.activation(view(A[:, 3, :], (1, 2 * ST)), view(A[:, 1, :], (1, 2 * ST)), ACT.Sin).then_inc(a_sin, 1)
            for k in range(4):
                act.wait_ge(y_ready, k + 1)
                act.activation(yg[:, k, :], y[:, k, :], ACT.Gelu_apprx_tanh).then_inc(gelu, 1)
            gb = FEAT_AT["ssm_glu_b"][0]
            for mo in range(4):
                act.wait_ge(z_made, mo + 1)
                act.activation(sg[:, mo, :], yps[:, mo, :T], ACT.Sigmoid, bias=m.feat[:, gb + mo:gb + mo + 1]).then_inc(sig, 1)
            act.wait_ge(sum_made, 1)
            act.activation(sg[:, 0, :], tps[:, 3, :T], ACT.Sqrt, bias=m.eps[:], scale=1.0 / 512).then_inc(rms, 1)
            for mo in range(4):
                act.wait_ge(n_ready, mo + 1)
                split_high(act.copy, m.ssmTh[:, mo, :], y[:, mo, :]).then_inc(n_high, 1)

        def recur(eng, ch, cur, prev, w, sa, sb_):
            ar = view(a2[:, 0, :], (ST, 2), (1, ST), (0, w))
            ai = view(ai2[:, 0, :], (ST, 2), (1, ST), (0, w))
            ch.mark(eng.tensor_tensor(sa[:], prev, ar, ALU.mult))
            ch.mark(eng.tensor_tensor(sb_[:], prev, ai, ALU.mult))
            ch.wait()
            ch.link(eng.tensor_tensor(cur, cur, sa[:], ALU.add))
            for ri in range(2):
                c = view(cur[:, ri], *cur.ap[2:])
                ch.mark(eng.tensor_tensor(c, c, view(sb_[:, 1 - ri], (w, ST), (1, w)), ALU.add))
            ch.wait()

        def at_p(j):
            return view(H[:, 0, 0, j:], (ST * T, 2), (T, ST), (CH, CH))

        def at_s(j):
            return view(H[:, 0, 0, 2 * P + j:], (ST * T, 2), (T, ST), (NS, NB))

        @block.gpsimd
        def _(pool):
            c = Chain(pool, pool_step)
            pool.wait_ge(init, 1)
            for j in range(1, NS):
                recur(pool, c, at_s(j), at_s(j - 1), NB, q1, q2)
            c.link(pool.tensor_copy(ends[:], view(H[:, 0, 0, 2 * P + NS - 1:], (ST * T, 2), (NS, NB), (T, ST))))
            pool.sem_inc(s_done, 1)

        @block.vector
        def _(dve):
            v = Chain(dve, v_step)
            tt, ts = dve.tensor_tensor, dve.tensor_scalar
            dve.wait_ge(a_dt, 1)
            v.mark(tt(A[:, 6, :], ldt[:], AI, ALU.mult))
            tt(A[:, 0, :], ldt[:], AR, ALU.mult).then_inc(v_arg, 1)
            v.wait()
            v.link(ts(A[:, 7, :], A[:, 6, :], 1.0 / (2 * np.pi), None, ALU.mult))
            v.link(ts(A[:, 7, :], A[:, 7, :], ROUND, None, ALU.add))
            v.link(ts(A[:, 7, :], A[:, 7, :], ROUND, None, ALU.subtract))
            v.link(dve.scalar_tensor_tensor(out=A[:, 6, :], in0=A[:, 7, :], scalar=-TWO_PI_HI, in1=A[:, 6, :], op0=ALU.mult, op1=ALU.add))
            v.link(dve.scalar_tensor_tensor(out=A[:, 6, :], in0=A[:, 7, :], scalar=-TWO_PI_LO, in1=A[:, 6, :], op0=ALU.mult, op1=ALU.add))
            v.link(ts(A[:, 2, :], A[:, 6, :], 3.1415925, -3.1415925, ALU.min, ALU.max))
            v.link(dve.scalar_tensor_tensor(out=A[:, 7, :], in0=A[:, 2, :], scalar=-1.0, in1=A[:, 2, :], op0=ALU.mult, op1=ALU.min))
            ts(A[:, 1, :], A[:, 7, :], float(np.pi / 2), None, ALU.add).then_inc(v_arg, 1)
            v.mark(tt(A[:, 8, :], AR, AR, ALU.mult))
            v.link(tt(A[:, 9, :], AI, AI, ALU.mult))
            v.link(tt(A[:, 8, :], A[:, 8, :], A[:, 9, :], ALU.add))
            v.link(dve.reciprocal(A[:, 9, :], A[:, 8, :]))
            dve.wait_ge(a_dt, 2)
            dve.wait_ge(a_sin, 1)
            v.mark(tt(a2[:, 0, :], A[:, 0, :], A[:, 3, :], ALU.mult))
            v.mark(tt(a2[:, 1, :], A[:, 0, :], A[:, 3, :], ALU.mult))
            v.link(tt(ai2[:, 0, :], A[:, 0, :], A[:, 4, :], ALU.mult))
            v.mark(ts(ai2[:, 1, :], ai2[:, 0, :], -1.0, None, ALU.mult))
            v.link(ts(A[:, 5, :], a2[:, 0, :], -1.0, None, ALU.add))
            v.mark(tt(A[:, 10, :], A[:, 5, :], AR, ALU.mult))
            v.mark(tt(A[:, 11, :], ai2[:, 0, :], AI, ALU.mult))
            v.mark(tt(A[:, 12, :], ai2[:, 0, :], AR, ALU.mult))
            v.link(tt(A[:, 13, :], A[:, 5, :], AI, ALU.mult))
            v.mark(tt(A[:, 10, :], A[:, 10, :], A[:, 11, :], ALU.add))
            v.link(tt(A[:, 12, :], A[:, 12, :], A[:, 13, :], ALU.subtract))
            v.mark(tt(A[:, 10, :], A[:, 10, :], A[:, 9, :], ALU.mult))
            v.link(tt(A[:, 12, :], A[:, 12, :], A[:, 9, :], ALU.mult))
            fr, fi = (view(A[:, x, :], (1, ST), (0, SC)) for x in (10, 12))
            v.mark(tt(bb[:, 0], braw[:, 0], fr, ALU.mult))
            v.mark(tt(bb[:, 1], braw[:, 1], fr, ALU.mult))
            v.link(tt(bb[:, 2], braw[:, 1], fi, ALU.mult))
            v.link(tt(bb[:, 0], bb[:, 0], bb[:, 2], ALU.subtract))
            v.link(tt(bb[:, 2], braw[:, 0], fi, ALU.mult))
            v.link(tt(bb[:, 1], bb[:, 1], bb[:, 2], ALU.add))
            for ri in range(2):
                for par in range(2):
                    last = ts(bx[:, ri, :, par, :], bb[:, ri], m.const("low_half")[:, par:par + 1], None, ALU.mult)
            last.then_inc(bx_ready, 1)
            for ri in range(2):
                for par in range(2):
                    last = ts(cx[:, ri, :, par, :], craw[:, ri], m.const("even_group")[:, par:par + 1], (1.0, -1.0)[ri], ALU.mult, ALU.mult)
            last.then_inc(bx_ready, 1)
            for n in range(8):
                dve.wait_ge(turned, n + 1)
                if n < 3:
                    c = dve.tensor_copy(uT[:, :, n * P:n * P + ROWS[n]], view(tps[:, n, :], (P, 4), (1, ROWS[n])))
                elif n == 3:
                    c = dve.tensor_copy(view(h0[:, 0, 0, :], (1, 2 * P)), tps[:, 3, :2 * P])
                else:
                    c = dve.tensor_copy(view((BT if n < 6 else CT)[:, n % 2, 0, :], (1, 512)), tps[:, n % 4, :])
                c.then_inc(stored, 1)
            v.mark(dve.tensor_copy(pw[:, 0, :, 0], a2[:, 0, :]))
            v.link(dve.tensor_copy(pw[:, 1, :, 0], ai2[:, 0, :]))
            w = 1
            while w < CH:
                lo = [pw[:, ri, :, :w] for ri in range(2)]
                top = [view(pw[:, ri, 0, w - 1:w], (CH, ST), (0, w)) for ri in range(2)]
                tmp = [t1[:, ri, :, :w] for ri in range(2)]
                new = [pw[:, ri, :, w:2 * w] for ri in range(2)]
                v.mark(tt(new[0], lo[0], top[0], ALU.mult))
                v.mark(tt(tmp[0], lo[1], top[1], ALU.mult))
                v.mark(tt(new[1], lo[0], top[1], ALU.mult))
                v.link(tt(tmp[1], lo[1], top[0], ALU.mult))
                v.mark(tt(new[0], new[0], tmp[0], ALU.subtract))
                v.link(tt(new[1], new[1], tmp[1], ALU.add))
                w *= 2
            for j in range(2 * ST):
                ri, i = divmod(j, ST)
                dve.wait_ge(x_made, j + 1)
                dve.tensor_copy(H[:, ri, i, :], tps[:, j % 4, :T]).then_inc(x_stored, 1)
            dve.wait_ge(x_stored, 2 * ST)
            h0v = view(h0[:, 0, 0, :], (P, 2), (1, ST), (ST, NB))
            v.mark(tt(q1[:], h0v, view(a2[:, 0, :], (ST, 2), (1, ST), (0, NB)), ALU.mult))
            v.link(tt(q2[:], h0v, view(ai2[:, 0, :], (ST, 2), (1, ST), (0, NB)), ALU.mult))
            v.link(tt(at_s(0), at_s(0), q1[:], ALU.add))
            for ri in range(2):
                c = view(H[:, ri, 0, 2 * P:], (T, ST), (NS, NB))
                v.mark(tt(c, c, q2[:, 1 - ri], ALU.add))
            v.wait()
            dve.sem_inc(init, 1)
            for j in range(1, CH):
                recur(dve, v, at_p(j), at_p(j - 1), CH, t1, t2)
            v.link(dve.tensor_copy(carry[:], at_p(CH - 1)))
            p16 = [view(pw[:, ri, 0, CH - 1:], (CH, ST)) for ri in range(2)]
            for c in range(1, CH - 1):
                pr, cr = [carry[:, ri, :, c - 1] for ri in range(2)], [carry[:, ri, :, c] for ri in range(2)]
                x = [t1[:, 0, 0, :], t1[:, 0, 1, :], t1[:, 0, 2, :], t1[:, 0, 3, :]]
                v.mark(tt(x[0], p16[0], pr[0], ALU.mult))
                v.mark(tt(x[1], p16[1], pr[1], ALU.mult))
                v.mark(tt(x[2], p16[0], pr[1], ALU.mult))
                v.link(tt(x[3], p16[1], pr[0], ALU.mult))
                v.mark(tt(cr[0], cr[0], x[0], ALU.add))
                v.mark(tt(cr[1], cr[1], x[2], ALU.add))
                v.wait()
                v.mark(tt(cr[0], cr[0], x[1], ALU.subtract))
                v.link(tt(cr[1], cr[1], x[3], ALU.add))
            N = CH - 1
            for qi in range(4):
                i0 = qi * 4
                pv_ = [view(pw[:, ri, i0, :], (CH, 4), (0, N), (1, CH)) for ri in range(2)]
                cv = [view(carry[:, ri, i0, :], (CH, 4), (1, N), (0, CH)) for ri in range(2)]
                hv = [view(H[:, ri, i0, CH:], (T, 4), (CH, N), (1, CH)) for ri in range(2)]
                f = [view(fx[:, ri, 0, :], (N * CH, 4), (CH, N), (1, CH)) for ri in range(2)]
                for ri in range(2):
                    v.mark(tt(f[0], pv_[0], cv[ri], ALU.mult))
                    v.link(tt(f[1], pv_[1], cv[1 - ri], ALU.mult))
                    v.link(tt(hv[ri], hv[ri], f[0], ALU.add))
                    v.link(tt(hv[ri], hv[ri], f[1], (ALU.subtract, ALU.add)[ri]))
            dve.sem_inc(p_done, 2)
            dve.tensor_copy(endp[:], view(H[:, 0, 0, SEQ - 1:], (ST * T, 2), (T, ST))).then_inc(ends_ready, 1)
            dcol = FEAT_AT["ssm_d"][0]
            for k in range(4):
                dve.wait_ge(y_made, k + 1)
                dve.scalar_tensor_tensor(out=y[:, k, :], in0=uT[:, k, :], scalar=m.feat[:, dcol + k:dcol + k + 1], in1=yps[:, k, :T],
                                         op0=ALU.mult, op1=ALU.add).then_inc(y_ready, 1)
            for n in range(3):
                dve.wait_ge(ends_turned, n + 1)
                r = 2 * ST if n == 2 else P
                dve.tensor_copy(endrow[:r, n, :], tps[:r, n, :P]).then_inc(ends_stored, 1)
            dve.wait_ge(gelu, 4)
            for mo in range(4):
                if mo == 0:
                    dve.wait_ge(sig, 4)
                v.link(tt(yg[:, mo, :], yg[:, mo, :], sg[:, mo, :], ALU.mult))
                tt(y[:, mo, :], yg[:, mo, :], yg[:, mo, :], ALU.mult).then_inc(sq_ready, 1)
            dve.wait_ge(rms, 1)
            v.link(dve.reciprocal(sg[:, 1, :], sg[:, 0, :]))
            oc = FEAT_AT["out_norm"][0] + 8
            for mo in range(4):
                dve.scalar_tensor_tensor(out=y[:, mo, :], in0=yg[:, mo, :], scalar=m.feat[:, oc + mo:oc + mo + 1], in1=sg[:, 1, :],
                                         op0=ALU.mult, op1=ALU.mult).then_inc(n_ready, 1)
            for mo in range(4):
                dve.wait_ge(n_high, mo + 1)
                split_low(dve, m.ssmTl[:, mo, :], y[:, mo, :], m.ssmTh[:, mo, :])


def phase_gmlp(nc, m, io):
    with ExitStack() as ctx:
        sb = lambda n, sh: ctx.enter_context(nc.sbuf_tensor(n, sh, F32))
        ws, wT, wS = sb("gm_w", [P, 4, P]), sb("gm_wT", [P, 4, P]), sb("gm_wS", [NTS, 4, NTS])
        gain, sq, bsS = sb("gm_gain", [P, 512]), sb("gm_sq", [P, 512]), sb("gm_bsS", [NTS, 4])
        ssq, rms, rstd = sb("gm_ssq", [P, 3, 4]), sb("gm_rms", [P, 3, 4]), sb("gm_rstd", [P, 3, 4])
        tps = ctx.enter_context(nc.psum_tensor("gm_tps", [P, 512], F32))
        sps = ctx.enter_context(nc.psum_tensor("gm_sps", [NTS, 64], F32))
        mps = ctx.enter_context(nc.psum_tensor("gm_mix", [P, 3, 512], F32))
        n_ = lambda n: m.sem("gm_" + n)
        in_done, gelu, summed, rooted, vn, v_step = n_("in"), n_("gelu"), n_("summed"), n_("rooted"), n_("vn"), n_("v_step")
        turned, wT_ready, spread, wS_ready, mixed = n_("turned"), n_("wT_ready"), n_("spread"), n_("wS_ready"), n_("mixed")
        block = ctx.enter_context(nc.Block())
        bs = FEAT_AT["gmlp_bs"][0]

        @block.sync
        def _(sp):
            sp.dma_start(ws[:], dram(io["gmlp_ws"], 0, (P, P), (P * P, 4), (1, P))).then_inc(in_done, 16)
            sp.dma_start(gain[:], dram(io["gmlp_norm"], 0, (0, P), (1, 512))).then_inc(in_done, 16)
            sp.wait_ge(vn, 3)
            m.store(sp, dram(io["p_gmlp_v"], 0, (512, P), (1, 512)), m.proj[:, 1, O_VG:O_VG + 512])
            m.store(sp, dram(io["s_gmlp_v"], 0, (512, NTS), (1, 512)), m.proj[:NTS, 2, O_VG:O_VG + 512])

        @block.scalar
        def _(act):
            for t in range(3):
                g = m.proj[:ROWS[t], t, O_UG:O_UG + 1024]
                act.activation(g, g, ACT.Gelu_apprx_tanh).then_inc(gelu, 1)
            for t in range(3):
                r = ROWS[t]
                act.wait_ge(summed, t + 1)
                act.activation(rms[:r, t, :], ssq[:r, t, :], ACT.Sqrt, bias=m.eps[:r, :], scale=1.0 / P).then_inc(rooted, 1)

        @block.tensor
        def _(pe):
            pe.wait_ge(in_done, 32)
            for g in range(4):
                mm = pe.transpose(tps[:, g * P:(g + 1) * P], ws[:, g, :], m.const("ident"))
            mm.then_inc(turned, 1)
            pe.wait_ge(wT_ready, 1)
            pe.matmul(sps[:, :32], m.const("spread8"), view(wT[:NS, 0, :], (P, 4), (1, NS)), start=True, stop=True)
            pe.matmul(sps[:, 32:36], m.const("spread8"), m.feat[:NS, bs:bs + 4], start=True, stop=True).then_inc(spread, 1)
            pe.wait_ge(wS_ready, 1)
            for t in range(3):
                pe.wait_ge(vn, t + 1)
                for g in range(4):
                    v = m.proj[:ROWS[t], t, O_VG + g * P:O_VG + (g + 1) * P]
                    mm = pe.matmul(mps[:ROWS[t], t, g * P:(g + 1) * P], wT[:, g, :] if t < 2 else wS[:, g, :], v, start=True, stop=True)
                mm.then_inc(mixed, 1)

        @block.vector
        def _(dve):
            v = Chain(dve, v_step)
            dve.wait_ge(turned, 1)
            dve.tensor_tensor(wT[:], view(tps[:], (P, 4), (1, P)), view(m.const("causal_T"), (0, 4), (1, P)), ALU.mult).then_inc(wT_ready, 1)
            dve.wait_ge(spread, 1)
            v.link(dve.tensor_copy(bsS[:], sps[:, 32:36]))
            dve.tensor_tensor(view(wS[:, 0, :], (NTS, 4), (NS, NB), (1, NS)), view(sps[:], (NS, 4), (0, NB), (1, NS)),
                              view(m.const("causal_seq_T"), (0, 4), (NS, NB), (1, NS)), ALU.mult).then_inc(wS_ready, 1)
            for t in range(3):
                r = ROWS[t]
                x = m.proj[:r, t, O_VG:O_VG + 512]
                dve.wait_ge(gelu, t + 1)
                v.link(dve.tensor_tensor(sq[:r], x, x, ALU.mult))
                dve.tensor_reduce(ssq[:r, t, :], view(sq[:r], (P, 4), (1, P)), AX_X, ALU.add).then_inc(summed, 1)
                dve.wait_ge(summed, t + 1)
            for t in range(3):
                r = ROWS[t]
                x = view(m.proj[:r, t, O_VG:], (P, 4), (1, P))
                dve.wait_ge(rooted, t + 1)
                v.link(dve.reciprocal(rstd[:r, t, :], rms[:r, t, :]))
                v.link(dve.tensor_tensor(x, x, view(rstd[:r, t, :], (1, 4), (0, P)), ALU.mult))
                dve.tensor_tensor(x, x, view(gain[:r], (P, 4), (1, P)), ALU.mult).then_inc(vn, 1)
            for t in range(3):
                r = ROWS[t]
                dve.wait_ge(mixed, t + 1)
                for g in range(4):
                    u = m.proj[:r, t, O_UG + g * P:O_UG + (g + 1) * P]
                    b_ = m.feat[:, bs + g:bs + g + 1] if t < 2 else bsS[:, g:g + 1]
                    v.mark(dve.scalar_tensor_tensor(out=u, in0=mps[:r, t, g * P:(g + 1) * P], scalar=b_, in1=u, op0=ALU.add, op1=ALU.mult))


def turn_with_gain_pe(pe, m, src, tps, jobs, ready, turned, stored):
    for n, (t, k0) in enumerate(jobs):
        r = ROWS[t]
        ready(pe, n)
        if n >= 2:
            pe.wait_ge(stored, n - 1)
        for j in range(4):
            mm = pe.transpose(tps[:, n % 2, j * P:j * P + r], src(t, k0 + j), m.const("ident")[:r, :r])
        mm.then_inc(turned, 1)


def phase_merge(nc, m, io):
    with ExitStack() as ctx:
        sb = lambda n, sh: ctx.enter_context(nc.sbuf_tensor(n, sh, F32))
        junk, ssq, rms, rstd = sb("mg_junk", [P, 1024]), sb("mg_ssq", [P, 6]), sb("mg_rms", [P, 6]), sb("mg_rstd", [P, 6])
        tps = ctx.enter_context(nc.psum_tensor("mg_tps", [P, 2, 512], F32))
        n_ = lambda n: m.sem("mg_" + n)
        summed, rooted, normed, turned, stored, v_step = n_("summed"), n_("rooted"), n_("normed"), n_("turned"), n_("stored"), n_("v_step")
        sems = (turned, stored, n_("high"), n_("low"))
        tmp = [sb(f"mg_tmp{u}", [P, 4, P]) for u in range(2)]
        jobs = [(t, k0) for t in range(3) for k0 in (0, 4, 8)]
        block = ctx.enter_context(nc.Block())

        def part(t, c):
            r = ROWS[t]
            return m.proj[:r, t, O_Q:O_Q + AW] if c == 0 else m.proj[:r, t, O_UG:O_UG + 512]

        @block.sync
        def _(sp):
            for q in range(4):
                load_piece(sp, io["w_out"], 512, m.oslot, m.w_out_landed, 0, q)

        @block.scalar
        def _(act):
            for t in range(3):
                r = ROWS[t]
                for c in range(2):
                    i = 2 * t + c
                    if i:
                        act.wait_ge(summed, i)
                    act.activation(junk[:r, :(AW, 512)[c]], part(t, c), ACT.Square, accum_out=ssq[:r, i:i + 1]).then_inc(summed, 1)
                    act.wait_ge(summed, i + 1)
                    act.activation(rms[:r, i:i + 1], ssq[:r, i:i + 1], ACT.Sqrt, bias=m.eps[:r, :], scale=1.0 / (AW, 512)[c]).then_inc(rooted, 1)
            split_turned_act(act, jobs, tmp, sems, m.agTh)

        @block.tensor
        def _(pe):
            src = lambda t, k: m.proj[:ROWS[t], t, O_Q + k * P:O_Q + (k + 1) * P] if k < 8 else \
                m.proj[:ROWS[t], t, O_UG + (k - 8) * P:O_UG + (k - 7) * P]
            turn_with_gain_pe(pe, m, src, tps, jobs, lambda e, n: e.wait_ge(normed, 2 * (n // 3) + n % 3 // 2 + 1), turned, stored)

        @block.vector
        def _(dve):
            v = Chain(dve, v_step)
            for i in range(6):
                t, c = divmod(i, 2)
                r = ROWS[t]
                dve.wait_ge(rooted, i + 1)
                v.link(dve.reciprocal(rstd[:r, i:i + 1], rms[:r, i:i + 1]))
                dve.tensor_scalar(part(t, c), part(t, c), rstd[:r, i:i + 1], None, ALU.mult).then_inc(normed, 1)
            split_turned_dve(dve, jobs, lambda n: tps[:, n % 2, :], tmp,
                             lambda k0: m.feat[:, FEAT_AT["out_norm"][0] + (k0 if k0 < 8 else 12):][:, :4],
                             sems, m.agTh, m.agTl)


def cat(ag, ssm, k):
    return ssm[:, k - 8, :] if 8 <= k < 12 else ag[:, k if k < 8 else k - 4, :]


def phase_out(nc, m, io):
    NCH = D // 512
    with ExitStack() as ctx:
        sb = lambda n, sh: ctx.enter_context(nc.sbuf_tensor(n, sh, F32))
        ssq, rms, rstd = sb("ffn_ssq", [P, 3]), sb("ffn_rms", [P, 3]), sb("ffn_rstd", [P, 3])
        gain = view(m.oslot[0][:], (1, D))
        acc = [[ctx.enter_context(nc.psum_tensor(f"out_acc{c}{t}", [P, 512], F32)) for t in range(3)] for c in range(2)]
        n_ = lambda n: m.sem("out_" + n)
        free_v, free_a, x_in, step = n_("acc_free_v"), n_("acc_free_a"), n_("x_in"), n_("v_step")
        summed, rooted = n_("summed"), n_("rooted")
        highs = [sb(f"w_out_high{q}", [P, 4, 512]) for q in range(4)]
        lows = [sb(f"w_out_low{q}", [P, 4, 512]) for q in range(4)]
        z = Stream(m, "out", NCH // 2, 512, io["w_out"], lambda k: cat(m.agTh, m.ssmTh, k), lambda k: cat(m.agTl, m.ssmTl, k), m.oslot, highs, lows, m.w_out_landed)
        gain_in = n_("gain_in")
        block = ctx.enter_context(nc.Block())

        @block.sync
        def _(sp):
            for t in range(3):
                src = dram(io["x_prompt"], t * P * D, (D, P), (1, D)) if t < 2 else dram(io["x_sample"], 0, (D, NTS), (1, D))
                sp.dma_start(m.x1[:ROWS[t], t, :], src).then_inc(x_in, 16)
            stream_load(sp, z)
            sp.wait_ge(z.low, 4 * NCH - 3)
            sp.dma_start(gain, dram(io["norm_ffn"], 0, (0, P), (1, D))).then_inc(gain_in, 16)

        @block.tensor
        def _(pe):
            stream_pe(pe, z, acc, free_v, free_a)

        @block.vector
        def _(dve):
            v = Chain(dve, step)

            def copy_out(i, c):
                dve.wait_ge(z.used, i * 8 + (4 * c + 8))
                for t in range(3):
                    r = ROWS[t]
                    x = m.x1[:r, t, bass.ds((2 * i + c) * 512, 512)]
                    ad = dve.tensor_tensor(x, acc[c][t][:r, :], x, ALU.add)
                ad.then_inc(free_v, 1)

            dve.sem_inc(free_v, 2)
            dve.wait_ge(x_in, 48)
            stream_dve(dve, z, copy_out)
            dve.wait_ge(gain_in, 16)
            for t in range(3):
                r = ROWS[t]
                dve.wait_ge(rooted, t + 1)
                v.link(dve.reciprocal(rstd[:r, t:t + 1], rms[:r, t:t + 1]))
                v.link(dve.tensor_scalar(m.h2[:r, t, :], m.x1[:r, t, :], rstd[:r, t:t + 1], None, ALU.mult))
                v.mark(dve.tensor_tensor(m.h2[:r, t, :], m.h2[:r, t, :], gain[:r, :], ALU.mult))

        @block.scalar
        def _(act):
            act.sem_inc(free_a, 2 + NCH)
            stream_act(act, z, lambda i, c: None)
            act.wait_ge(free_v, 2 + NCH)
            for t in range(3):
                r = ROWS[t]
                act.activation(m.h2[:r, t, :], m.x1[:r, t, :], ACT.Square, accum_out=ssq[:r, t:t + 1]).then_inc(summed, 1)
                act.wait_ge(summed, t + 1)
                act.activation(rms[:r, t:t + 1], ssq[:r, t:t + 1], ACT.Sqrt, bias=m.eps[:r, :], scale=1.0 / D).then_inc(rooted, 1)


NE, NG4 = 4, 4
ITEMS = 6


def phase_route(nc, m, io):
    with ExitStack() as ctx:
        sb = lambda n, sh: ctx.enter_context(nc.sbuf_tensor(n, sh, F32))
        h2T, rw, rb = sb("rt_h2T", [P, KT, T]), sb("rt_w", [P, KT, 20]), sb("rt_b", [P, 20])
        lg, le = sb("rt_lg", [P, 3, 4]), sb("rt_le", [P, 12, 4])
        c1, c2 = sb("rt_c1", [P, 12, 4, 4]), sb("rt_c2", [P, 12, 4, 4])
        rk, oh, sel = sb("rt_rank", [P, 12, 4]), sb("rt_onehot", [P, 3, 4]), sb("rt_sel", [P, 12, 4])
        mg, eg, gs, gp = sb("rt_mg", [P, 3]), sb("rt_eg", [P, 3, 4]), sb("rt_gs", [P, 3]), sb("rt_gp", [P, 3])
        me, ex, es, gt = sb("rt_me", [P, 12]), sb("rt_ex", [P, 12, 4]), sb("rt_es", [P, 12]), sb("rt_gate", [P, 12, 4])
        pos, cnt, nt, start, nx = sb("rt_pos", [P, 3, 4]), sb("rt_cnt", [P, 4]), sb("rt_nt", [P, 4]), sb("rt_start", [P, 4]), sb("rt_nx", [P, 4])
        actv, wst, w_t, w_g = sb("rt_active", [P, ITEMS, 4]), sb("rt_wst", [P, ITEMS, 4]), sb("rt_wtile", [P, ITEMS]), sb("rt_wgroup", [P, ITEMS])
        big = sb("rt_big", [P, 3, ITEMS, 4])
        has, plan = sb("rt_has", [P, 3, ITEMS]), sb("rt_plan", [1, 8])
        tps = ctx.enter_context(nc.psum_tensor("rt_tps", [P, 2, 512], F32))
        lps = ctx.enter_context(nc.psum_tensor("rt_lps", [P, 3, 512], F32))
        pps = ctx.enter_context(nc.psum_tensor("rt_pps", [P, 64], F32))
        n_ = lambda n: m.sem("rt_" + n)
        in_done, turned, stored, logits, oh_ready, counted = n_("in"), n_("turned"), n_("stored"), n_("logits"), n_("oh_ready"), n_("counted")
        sub_done, exps, v_step = n_("sub_done"), n_("exps"), n_("v_step")
        jobs = [(t, k0) for t in range(3) for k0 in (0, 4, 8, 12)]
        block = ctx.enter_context(nc.Block())

        @block.sync
        def _(sp):
            sp.dma_start(rw[:, :, :4], dram(io["router_group_w"], 0, (4, P), (P * 4, KT), (1, 4))).then_inc(in_done, 16)
            for g in range(4):
                sp.dma_start(rw[:, :, 4 + 4 * g:8 + 4 * g], dram(io["router_expert_w"], g * D * 4, (4, P), (P * 4, KT), (1, 4))).then_inc(in_done, 16)
            sp.dma_start(rb[:, :4], dram(io["router_group_b"], 0, (0, P), (1, 4))).then_inc(in_done, 16)
            sp.dma_start(rb[:, 4:], dram(io["router_expert_b"], 0, (0, P), (1, 16))).then_inc(in_done, 16)

        @block.tensor
        def _(pe):
            turn_with_gain_pe(pe, m, lambda t, k: m.h2[:ROWS[t], t, k * P:(k + 1) * P], tps, jobs, lambda e, n: None, turned, stored)
            pe.wait_ge(in_done, 16 * 7)
            for t in range(3):
                r = ROWS[t]
                pe.wait_ge(stored, 4 * t + 4)
                for k in range(KT):
                    mm = pe.matmul(lps[:r, t, :20], h2T[:, k, t * P:t * P + r], rw[:, k, :], start=(k == 0), stop=(k == KT - 1))
                mm.then_inc(logits, 1)
            pe.wait_ge(oh_ready, 1)
            for t in range(3):
                for t2 in range(t + 1):
                    pe.matmul(pps[:, 4 * t:4 * t + 4], m.const("before" if t2 == t else "ones"), oh[:, t2, :], start=(t2 == 0), stop=(t2 == t))
            for t in range(3):
                mm = pe.matmul(pps[:, 12:16], m.const("ones"), oh[:, t, :], start=(t == 0), stop=(t == 2))
            mm.then_inc(counted, 1)

        @block.scalar
        def _(act):
            act.wait_ge(sub_done, 1)
            act.activation(eg[:], eg[:], ACT.Exp)
            act.activation(ex[:], ex[:], ACT.Exp).then_inc(exps, 1)

        @block.vector
        def _(dve):
            v = Chain(dve, v_step)
            tt, ts, red = dve.tensor_tensor, dve.tensor_scalar, dve.tensor_reduce
            v.mark(dve.memset(lg[:], 0.0))
            v.link(dve.memset(le[:], 0.0))
            for n, (t, k0) in enumerate(jobs):
                dve.wait_ge(turned, n + 1)
                dve.tensor_copy(h2T[:, k0:k0 + 4, t * P:t * P + ROWS[t]], view(tps[:, n % 2, :], (P, 4), (1, ROWS[t]))).then_inc(stored, 1)
            for t in range(3):
                r = ROWS[t]
                dve.wait_ge(logits, t + 1)
                v.mark(tt(lg[:r, t, :], lps[:r, t, :4], rb[:r, :4], ALU.add))
                v.mark(tt(view(le[:r, 4 * t, :], (1, 16)), lps[:r, t, 4:20], rb[:r, 4:], ALU.add))
            v.wait()

            def rank(x, n, out):
                vj = view(x, (4, n), (0, 4), (1, 4))
                vi = view(x, (4, n), (1, 4), (0, 4))
                a_, b_ = (view(c[:, 0, 0, :], (16, n), (4, 4), (1, 4)) for c in (c1, c2))
                v.mark(tt(a_, vj, vi, ALU.is_gt))
                v.link(tt(b_, vj, vi, ALU.is_equal))
                v.link(tt(b_, b_, view(m.const("earlier4"), (0, n), (4, 4), (1, 4)), ALU.mult))
                v.link(tt(a_, a_, b_, ALU.add))
                v.link(red(out, a_, AX_X, ALU.add))

            rank(lg[:], 3, rk[:, :3, :])
            v.link(ts(oh[:], rk[:, :3, :], 0.5, None, ALU.is_lt))
            ts(oh[:, 2, :], oh[:, 2, :], m.const("low_half")[:, 0:1], None, ALU.mult).then_inc(oh_ready, 1)
            dve.wait_ge(oh_ready, 1)
            rank(le[:], 12, rk[:])
            v.mark(ts(sel[:], rk[:], 1.5, None, ALU.is_lt))
            v.mark(red(mg[:], lg[:], AX_X, ALU.max))
            v.link(red(me[:], le[:], AX_X, ALU.max))
            v.mark(tt(eg[:], lg[:], view(mg[:], (1, 3), (0, 4)), ALU.subtract))
            tt(ex[:], le[:], view(me[:], (1, 12), (0, 4)), ALU.subtract).then_inc(sub_done, 1)
            v.wait()
            dve.wait_ge(exps, 1)
            v.mark(red(gs[:], eg[:], AX_X, ALU.add))
            v.link(tt(ex[:], ex[:], sel[:], ALU.mult))
            v.mark(dve.reciprocal(gp[:], gs[:]))
            v.link(red(es[:], ex[:], AX_X, ALU.add))
            v.link(dve.reciprocal(es[:], es[:]))
            v.link(tt(ex[:], ex[:], view(es[:], (1, 12), (0, 4)), ALU.mult))
            v.link(tt(gt[:], ex[:], view(oh[:, 0, :], (1, 12), (0, 4)), ALU.mult))
            v.link(red(m.gate4[:], view(gt[:, 0, :], (16, 3), (1, 4), (4, 4)), AX_X, ALU.add))
            v.mark(tt(m.gate4[:], m.gate4[:], view(gp[:], (1, 3), (0, 4)), ALU.mult))
            dve.wait_ge(counted, 1)
            v.mark(dve.tensor_copy(pos[:], view(pps[:], (4, 3), (1, 4))))
            v.link(dve.tensor_copy(cnt[:], pps[:, 12:16]))
            v.mark(ts(nt[:], cnt[:], 0.5, None, ALU.is_gt))
            v.link(ts(nx[:], cnt[:], 128.5, None, ALU.is_gt))
            v.link(tt(nt[:], nt[:], nx[:], ALU.add))
            v.link(ts(nx[:], cnt[:], 256.5, None, ALU.is_gt))
            v.link(tt(nt[:], nt[:], nx[:], ALU.add))
            v.link(dve.memset(start[:, 0:1], 0.0))
            for g in range(1, 4):
                v.link(tt(start[:, g:g + 1], start[:, g - 1:g], nt[:, g - 1:g], ALU.add))
            v.link(tt(wst[:], view(m.const("iota"), (1, ITEMS), (0, 4)), view(start[:], (0, ITEMS), (1, 4)), ALU.subtract))
            v.mark(ts(actv[:], wst[:], -0.5, None, ALU.is_gt))
            v.link(tt(view(big[:, 0, 0, :], (4, ITEMS), (1, 4)), wst[:], view(nt[:], (0, ITEMS), (1, 4)), ALU.is_lt))
            v.link(tt(actv[:], actv[:], view(big[:, 0, 0, :], (4, ITEMS), (1, 4)), ALU.mult))
            v.link(tt(wst[:], wst[:], actv[:], ALU.mult))
            v.link(red(w_t[:], wst[:], AX_X, ALU.add))
            v.link(tt(wst[:], actv[:], view(m.const("group4"), (0, ITEMS), (1, 4)), ALU.mult))
            v.link(red(w_g[:], wst[:], AX_X, ALU.add))
            v.mark(ts(plan[:, :ITEMS], w_g[0:1, :], 4.0, None, ALU.mult))
            v.mark(red(plan[:, 6:7], nt[0:1, :], AX_X, ALU.add))
            v.link(dve.memset(plan[:, 7:8], 0.0))
            v.link(dve.tensor_copy(m.plan[:], plan[:]))
            v.link(tt(pos[:], pos[:], oh[:], ALU.mult))
            ax = lambda q: view(q, (0, 1), (4, ITEMS), (1, 4))
            for t in range(3):
                v.mark(tt(big[:, t], view(actv[:, 0, :], (4, ITEMS), (1, 4)), view(pos[:, t, :], (0, ITEMS), (1, 4)), ALU.mult))
            v.wait()
            v.link(red(m.slot[:], big[:], AX_X, ALU.add))
            for t in range(3):
                v.mark(tt(big[:, t], view(actv[:, 0, :], (4, ITEMS), (1, 4)), view(oh[:, t, :], (0, ITEMS), (1, 4)), ALU.mult))
            v.wait()
            v.link(red(has[:], big[:], AX_X, ALU.add))
            v.link(ts(w_t[:], w_t[:], float(P), None, ALU.mult))
            v.link(tt(m.slot[:], m.slot[:], view(w_t[:], (0, 3), (1, ITEMS)), ALU.subtract))
            v.link(ts(m.slot[:], m.slot[:], 1.0, None, ALU.add))
            v.link(tt(m.slot[:], m.slot[:], has[:], ALU.mult))
            v.link(ts(m.slot[:], m.slot[:], -1.0, None, ALU.add))


RING = 4
AHEAD = 3
CHUNKS = 48


def weight_order():
    order = [("w1", 0)]
    for e in range(NE):
        order.append(("w3", e))
        if e + 1 < NE:
            order.append(("w1", e + 1))
        order.append(("w2", e))
    return order


def phase_moe(nc, m, io):
    with ExitStack() as ctx:
        sb = lambda n, sh: ctx.enter_context(nc.sbuf_tensor(n, sh, F32))
        ring = [sb(f"ex_w{s}", [P, 4, 512]) for s in range(RING)]
        high = [sb(f"ex_w_high{s}", [P, 4, 512]) for s in range(RING)]
        low = [sb(f"ex_w_low{s}", [P, 4, 512]) for s in range(RING)]
        Dm, DT, XT, XTh = sb("ex_D", [P, 3, P]), sb("ex_DT", [P, 3, P]), sb("ex_XT", [P, KT, P]), sb("ex_XT_high", [P, KT, P])
        sl, gsl = sb("ex_slot", [P, 3]), sb("ex_gate", [P, NE])
        s1, hid, hT, hTh = sb("ex_silu", [P, 512]), sb("ex_hid", [P, 512]), sb("ex_hT", [P, 4, P]), sb("ex_hT_high", [P, 4, P])
        ysb, yh = sb("ex_y", [P, 4, 512]), sb("ex_y_high", [P, 4, 512])
        Y = ctx.enter_context(nc.psum_tensor("ex_Y", [P, 4, 512], F32))
        A = ctx.enter_context(nc.psum_tensor("ex_A", [P, 2, 512], F32))
        B = ctx.enter_context(nc.psum_tensor("ex_B", [P, 2, 512], F32))
        n_ = lambda n: m.sem("ex_" + n)
        landed = [n_(f"landed{s}") for s in range(RING)]
        free, D_ready, D_turned, DT_ready, g_made, g_ready = n_("slot_free"), n_("D_ready"), n_("D_turned"), n_("DT_ready"), n_("g_made"), n_("g_ready")
        x_made, x_high, x_low, silu, gated = n_("x_made"), n_("x_high"), n_("x_low"), n_("silu"), n_("gated")
        w_high, w_low = n_("w_high"), n_("w_low")
        h_turned, h_high, h_low, y_high, y_low = n_("h_turned"), n_("h_high"), n_("h_low"), n_("y_high"), n_("y_low")
        back, added, slot_ready = n_("back"), n_("added"), n_("slot_ready")
        order = weight_order()

        turn_at = [4 * order.index(("w1", e + 1)) + 2 for e in range(NE - 1)] + [4 * order.index(("w2", NE - 1))]

        def used(mat, e, w):
            return w * CHUNKS + (RING + 4 * (order.index((mat, e)) + 1))

        block = ctx.enter_context(nc.Block())

        def count(eng):
            return eng.value_load(m.plan[0:1, 6:7], min_val=1, max_val=ITEMS)

        @block.sync
        def _(sp):
            sp.sem_inc(w_low, RING)
            with sp.Fori(0, count(sp)) as w:
                e0 = sp.value_load(m.plan[0:1, bass.ds(w, 1)], min_val=0, max_val=12)
                for q, (mat, e) in enumerate(order):
                    src = {"w1": io["expert_w1"], "w3": io["expert_w3"], "w2": io["expert_w2"]}[mat][0, bass.ds(e0 + e, 1)]
                    for c in range(4):
                        n = 4 * q + c
                        sp.wait_ge(w_low, w * CHUNKS + (n + 1))
                        if mat == "w2":
                            part, dst = src[:, c * P:(c + 1) * P, :].rearrange("e p n -> p (e n)"), view(ring[n % RING][:], (1, D))
                        else:
                            part, dst = src[:, c * 512:(c + 1) * 512, :].rearrange("e (k p) n -> p (e k) n", p=P), ring[n % RING][:]
                        sp.dma_start(dst, part).then_inc(landed[n % RING], 16)

        @block.tensor
        def _(pe):
            I = m.const("ident")
            with pe.Fori(0, count(pe)) as w:
                pe.wait_ge(D_ready, w + 1)
                for t in range(3):
                    mm = pe.transpose(B[:, 0, t * P:t * P + ROWS[t]], Dm[:ROWS[t], t, :], I[:ROWS[t], :ROWS[t]])
                mm.then_inc(D_turned, 1)
                for t in range(3):
                    mm = pe.matmul(B[:, 1, :NE], Dm[:ROWS[t], t, :], m.gate4[:ROWS[t], t, :], start=(t == 0), stop=(t == 2))
                mm.then_inc(g_made, 1)
                for q in range(4):
                    if q < 2:
                        bank = A[:, q, :]
                    else:
                        if q == 2:
                            pe.wait_ge(DT_ready, w + 1)
                            pe.wait_ge(g_ready, w + 1)
                        bank = B[:, q - 2, :]
                    for j in range(4):
                        k = 4 * q + j
                        for t in range(3):
                            mm = pe.matmul(bank[:, j * P:(j + 1) * P], m.h2[:ROWS[t], t, k * P:(k + 1) * P], Dm[:ROWS[t], t, :],
                                           start=(t == 0), stop=(t == 2))
                    mm.then_inc(x_made, 1)
                pe.wait_ge(x_low, w * 4 + 4)
                for q, (mat, e) in enumerate(order):
                    if mat == "w2" and e < NE - 1:
                        pe.wait_ge(h_low, w * NE + (e + 1))
                    elif mat != "w2" and e > 0:
                        pe.wait_ge(silu if mat == "w1" else gated, w * NE + e)
                    for c in range(4):
                        n = 4 * q + c
                        if n in turn_at:
                            f_ = turn_at.index(n)
                            pe.wait_ge(gated, w * NE + (f_ + 1))
                            for f in range(4):
                                mm = pe.transpose(B[:, f_ % 2, f * P:(f + 1) * P], hid[:, f * P:(f + 1) * P], I)
                            mm.then_inc(h_turned, 1)
                            if f_ == NE - 1:
                                pe.wait_ge(h_low, w * NE + NE)
                        pe.wait_ge(w_low, w * CHUNKS + (RING + n + 1))
                        for j in range(4):
                            if mat == "w2":
                                mm = matmul_split(pe, Y[:, j, :], hTh[:, c, :], hT[:, c, :], high[n % RING][:, j, :], low[n % RING][:, j, :],
                                                  e == 0 and c == 0, e == NE - 1 and c == 3)
                            else:
                                k = 4 * c + j
                                mm = matmul_split(pe, A[:, 0 if mat == "w1" else 1, :], XTh[:, k, :], XT[:, k, :],
                                                  high[n % RING][:, j, :], low[n % RING][:, j, :], k == 0, k == KT - 1)
                        mm.then_inc(free, 1)
                for n in range(12):
                    t, c = divmod(n, 4)
                    if t == 0:
                        pe.wait_ge(y_low, w * 4 + (c + 1))
                    if n >= 4:
                        pe.wait_ge(added, w * 12 + (n - 3))
                    bank = A[:, n % 4, :] if n % 4 < 2 else B[:, n % 4 - 2, :]
                    sel = DT[:, t, :ROWS[t]].bitcast(F32R)
                    pe.matmul(bank[:ROWS[t], :], sel, yh[:, c, :].bitcast(F32R), start=True, stop=False)
                    pe.matmul(bank[:ROWS[t], :], sel, ysb[:, c, :].bitcast(F32R), start=False, stop=True).then_inc(back, 1)
                pe.wait_ge(added, w * 12 + 12)

        @block.scalar
        def _(act):
            act.sem_inc(free, RING)
            with act.Fori(0, count(act)) as w:
                def split(n):
                    act.wait_ge(free, w * CHUNKS + (n + 1))
                    act.wait_ge(landed[n % RING], w * (CHUNKS // RING * 16) + (n // RING + 1) * 16)
                    split_high(act.copy, high[n % RING][:], ring[n % RING][:]).then_inc(w_high, 1)

                for q in range(4):
                    act.wait_ge(x_made, w * 4 + (q + 1))
                    split_high(act.copy, view(XTh[:, 4 * q, :], (1, 512)), (A if q < 2 else B)[:, q % 2, :]).then_inc(x_high, 1)
                    if q < AHEAD:
                        split(q)
                for n in range(CHUNKS):
                    if n + AHEAD < CHUNKS:
                        split(n + AHEAD)
                    mat, e = order[n // 4]
                    if mat == "w1" and n % 4 == 3:
                        act.wait_ge(free, used("w1", e, w))
                        if e:
                            act.wait_ge(gated, w * NE + e)
                        act.activation(s1[:], A[:, 0, :], ACT.Silu).then_inc(silu, 1)
                    if n in turn_at:
                        f_ = turn_at.index(n)
                        act.wait_ge(h_turned, w * NE + (f_ + 1))
                        split_high(act.copy, view(hTh[:, 0, :], (1, 512)), B[:, f_ % 2, :]).then_inc(h_high, 1)
                act.wait_ge(free, used("w2", NE - 1, w))
                for c in range(4):
                    split_high(act.copy, yh[:, c, :], Y[:, c, :]).then_inc(y_high, 1)

        @block.vector
        def _(dve):
            with dve.Fori(0, count(dve)) as w:
                dve.tensor_copy(sl[:], view(m.slot[:, 0, bass.ds(w, 1)], (ITEMS, 3))).then_inc(slot_ready, 1)
                dve.wait_ge(slot_ready, w + 1)
                for t in range(3):
                    d = dve.tensor_scalar(Dm[:, t, :], m.const("iota"), sl[:, t:t + 1], None, ALU.is_equal)
                d.then_inc(D_ready, 1)
                dve.wait_ge(D_turned, w + 1)
                dve.tensor_copy(view(DT[:, 0, :], (1, T)).bitcast(F32R), B[:, 0, :T]).then_inc(DT_ready, 1)
                dve.wait_ge(g_made, w + 1)
                dve.tensor_copy(gsl[:], B[:, 1, :NE]).then_inc(g_ready, 1)

                def split(n):
                    dve.wait_ge(w_high, w * CHUNKS + (n + 1))
                    split_low(dve, low[n % RING][:], ring[n % RING][:], high[n % RING][:]).then_inc(w_low, 1)

                for q in range(4):
                    dve.wait_ge(x_high, w * 4 + (q + 1))
                    split_low(dve, view(XT[:, 4 * q, :], (1, 512)), (A if q < 2 else B)[:, q % 2, :], view(XTh[:, 4 * q, :], (1, 512))).then_inc(x_low, 1)
                    if q < AHEAD:
                        split(q)
                for n in range(CHUNKS):
                    if n + AHEAD < CHUNKS:
                        split(n + AHEAD)
                    mat, e = order[n // 4]
                    if mat == "w3" and n % 4 == 3:
                        dve.wait_ge(silu, w * NE + (e + 1))
                        dve.wait_ge(free, used("w3", e, w))
                        dve.scalar_tensor_tensor(out=hid[:], in0=A[:, 1, :], scalar=gsl[:, e:e + 1], in1=s1[:], op0=ALU.mult, op1=ALU.mult).then_inc(gated, 1)
                    if n in turn_at:
                        f_ = turn_at.index(n)
                        dve.wait_ge(h_high, w * NE + (f_ + 1))
                        split_low(dve, view(hT[:, 0, :], (1, 512)), B[:, f_ % 2, :], view(hTh[:, 0, :], (1, 512))).then_inc(h_low, 1)
                for c in range(4):
                    dve.wait_ge(y_high, w * 4 + (c + 1))
                    split_low(dve, ysb[:, c, :], Y[:, c, :], yh[:, c, :]).then_inc(y_low, 1)
                for n in range(12):
                    t, c = divmod(n, 4)
                    bank = A[:, n % 4, :] if n % 4 < 2 else B[:, n % 4 - 2, :]
                    dve.wait_ge(back, w * 12 + (n + 1))
                    x = m.x1[:ROWS[t], t, c * 512:(c + 1) * 512]
                    dve.tensor_tensor(x, bank[:ROWS[t], :], x, ALU.add).then_inc(added, 1)


def phase_store_y(nc, m, io):
    with ExitStack() as ctx:
        block = ctx.enter_context(nc.Block())

        @block.sync
        def _(sp):
            for t in range(3):
                dst = dram(io["y_prompt"], t * P * D, (D, P), (1, D)) if t < 2 else dram(io["y_sample"], 0, (D, NTS), (1, D))
                m.store(sp, dst, m.x1[:ROWS[t], t, :])
            sp.wait_ge(m.out_done, m.n_out)
            sp.wait_ge(m.p_cmp_out, 32)


class Memory:
    pass


def memory(nc, ctx):
    m = Memory()
    m.pack, at = constants()
    m.sem = nc.alloc_semaphore
    sb = lambda name, shape: ctx.enter_context(nc.sbuf_tensor(name, shape, F32))
    m.cpack = sb("cpack", list(m.pack.shape))

    def const(name):
        off, rows, cols = at[name]
        return m.cpack[:rows, off:off + cols]

    m.const = const
    m.feat = sb("feat", [P, NFEAT])
    m.eps = sb("eps", [P, 1])
    m.tab = sb("rel_table", [33, NQ])
    m.qkg = sb("qk_gain", [P, 4, HD])
    m.qkcol = sb("qk_gain_col", [P, 4])
    m.ptab = ctx.enter_context(nc.sbuf_tensor("page_ids", [1, NB * NPG], I32))
    m.plan = ctx.enter_context(nc.sbuf_tensor("work_plan", [1, 8], I32))
    m.slot, m.gate4 = sb("token_slots", [P, 3, ITEMS]), sb("token_gates", [P, 3, NE])
    m.out_done, m.p_cmp_out, m.rep_out = m.sem("out_done"), m.sem("p_cmp_out"), m.sem("bias_rep_out")
    m.n_out = 0

    def store(eng, dst, src, then=None):
        m.n_out += 16
        eng.dma_start(dst, src).then_inc(m.out_done, 16)

    m.SA_V = 31
    m.store = store
    m.w_in_landed = [m.sem(f"w_in_landed{s}") for s in range(4)]
    m.w_out_landed = [m.sem(f"w_out_landed{s}") for s in range(4)]
    m.phase_sems = []

    def phase_sem(name):
        m.phase_sems.append(nc.alloc_semaphore(name))
        return m.phase_sems[-1]

    m.sem = phase_sem
    return m


def recycle_semaphores(nc, m):
    nums = [s.num for s in m.phase_sems]
    with nc.Block() as block:

        @block.gpsimd
        def _(pool):
            pool.sem_clear(range(min(nums), max(nums) + 1))

    for s in m.phase_sems:
        nc.release_semaphore(s)
    m.phase_sems.clear()


def decoder_step(nc, io):
    with ExitStack() as ctx:
        ctx.enter_context(nc.allow_non_contiguous_dma(reason="small tables, and diagonals of the bias row"))
        m = memory(nc, ctx)

        def sb(scope, name, shape):
            return scope.enter_context(nc.sbuf_tensor(name, shape, F32))

        m.proj = sb(ctx, "proj", [P, 3, IN_W])
        with ExitStack() as s:
            m.hTh, m.hTl = sb(s, "hT_high", [P, KT, T]), sb(s, "hT_low", [P, KT, T])
            m.wslot = [sb(s, f"w_in_slot{i}", [P, 4, PCH]) for i in range(4)]
            phase_norm_in(nc, m, io)
            phase_project(nc, m, io)
        with ExitStack() as s:
            m.bias_win, m.bias_cmp = sb(s, "bias_win", [P, WIN]), sb(s, "bias_cmp", [P, NC_S])
            m.bias_new, m.gate_s = sb(s, "bias_new", [P, NB, NTS]), sb(s, "gate_s", [P, 3, NB])
            m.kc_s, m.vc_s = sb(s, "kc_s", [P, NB * 2 * NC_S]), sb(s, "vc_s", [NC_S, NB * KVW])
            m.qkT = sb(s, "qkT", [P, 12, T])
            with ExitStack() as s2:
                m.q_pairs, m.k_pairs = sb(s2, "q_pairs", [P, 3, AW]), sb(s2, "k_pairs", [P, 3, 2 * KVW])
                phase_heads(nc, m, io)
                phase_turn_heads(nc, m, io)
            with ExitStack() as s2:
                m.kc_p, m.vc_p = sb(s2, "kc_p", [P, 2 * NC_P]), sb(s2, "vc_p", [NC_P, KVW])
                phase_compress(nc, m, io)
                phase_prompt_attention(nc, m, io)
            phase_sample_attention(nc, m, io)
        recycle_semaphores(nc, m)
        with ExitStack() as s:
            m.ssmTh, m.ssmTl = sb(s, "ssmT_high", [P, 4, T]), sb(s, "ssmT_low", [P, 4, T])
            phase_s5(nc, m, io)
            phase_gmlp(nc, m, io)
            m.agTh, m.agTl = sb(s, "agT_high", [P, 12, T]), sb(s, "agT_low", [P, 12, T])
            m.oslot = [sb(s, f"w_out_slot{i}", [P, 4, 512]) for i in range(4)]
            phase_merge(nc, m, io)
            m.x1, m.h2 = m.proj[:, :, 0:D], m.proj[:, :, D:2 * D]
            phase_out(nc, m, io)
        phase_route(nc, m, io)
        phase_moe(nc, m, io)
        phase_store_y(nc, m, io)


KV_TAIL = (NKV, 2, HD)
OUTS = (("y_prompt", (1, SEQ, D)), ("y_sample", (NB, NS, D)),
        ("p_kv_cmp", (1, 1, SEQ) + KV_TAIL), ("p_kv_sel", (1, 1, SEQ) + KV_TAIL), ("p_kv_win", (1, 1, SEQ) + KV_TAIL),
        ("p_ssm_re", (1, 1, SG, SN)), ("p_ssm_im", (1, 1, SG, SN)), ("p_gmlp_v", (1, 1, P, 512)),
        ("s_kv_cmp", (NB, 1, NS) + KV_TAIL), ("s_kv_sel", (NB, 1, NS) + KV_TAIL), ("s_kv_win", (NB, 1, WIN) + KV_TAIL),
        ("s_ssm_re", (NB, 1, SG, SN)), ("s_ssm_im", (NB, 1, SG, SN)), ("s_gmlp_v", (NB, 1, NS, 512)))


def kernel(**inputs):
    import concourse.bacc as bacc
    from concourse.bass_utils import run_bass_kernel_spmd

    nc = bacc.Bacc("TRN2", target_bir_lowering=False, num_devices=1)
    arrays = {f"in_{name}": np.ascontiguousarray(a) for name, a in inputs.items()}
    arrays["in_cpack"] = constants()[0]
    io = {}
    for name, a in arrays.items():
        io[name[3:]] = nc.dram_tensor(name, a.shape, mybir.dt.from_np(a.dtype), kind="ExternalInput").ap()
    for name, shape in OUTS:
        io[name] = nc.dram_tensor(name, shape, F32, kind="ExternalOutput").ap()
    io["bias_rows"] = nc.dram_tensor("bias_rows", (NQ, LB), F32).ap()
    io["bias_rep"] = nc.dram_tensor("bias_rep", (P, NQ, TRI), F32).ap()
    io["gate_rows"] = nc.dram_tensor("gate_rows", (NTS, 3 * NQ), F32).ap()
    io["o_rows"] = nc.dram_tensor("o_rows", (NB, P, HD), F32).ap()
    decoder_step(nc, io)
    got = run_bass_kernel_spmd(nc, [arrays], core_ids=[0]).results[0]
    return tuple(got[name] for name, _ in OUTS)
```

```python
from contextlib import ExitStack

import numpy as np

import concourse.bass as bass
from concourse import mybir

F32 = mybir.dt.float32
F32R = mybir.dt.float32r
I32 = mybir.dt.int32
ALU = mybir.AluOpType
ACT = mybir.ActivationFunctionType
AX_X = mybir.AxisListType.X

P = 128
D = 2048
KT = D // P
SEQ, NB, NS = 256, 8, 8
NTS = NB * NS
T = SEQ + NTS
ROWS = (P, P, NTS)
PAST, PAGE = 2048, 128
NPG = PAST // PAGE
N_PHYS = 5 * NB * NPG // 4
HD, NQ, NKV, G = 64, 16, 4, 4
AW, KVW = 1024, 256
WIN = 512
SELB, TOPK = 64, 16
NBLK = (PAST + NS + SELB - 1) // SELB
NC_S = (PAST - 32) // 16 + 1
NC_P = (SEQ - 32) // 16 + 1
IN_W = 4144
O_Q, O_KV, O_GATE, O_U, O_UG, O_VG = 0, 1024, 2560, 2608, 3120, 3632
SCALE = HD ** -0.5
EPS = 1e-6
NEG = -1e30
D0 = WIN + NS - 1
LB = D0 + SEQ
TRI = 3 * P - 1
PCH = 296
NPCH = IN_W // PCH


def bucket(dist):
    n = np.maximum(dist, 0)
    nf = np.maximum(n, 16).astype(np.float32)
    large = 16 + (np.log(nf / np.float32(16)) / np.float32(np.log(8.0)) * np.float32(16)).astype(np.int32)
    return np.where(n < 16, n, np.minimum(large, 31))


def constants():
    f = np.float32
    p = np.arange(P)
    c = {}
    c["ident"] = np.eye(P, dtype=f)
    dist = D0 - np.arange(LB)
    one = (bucket(dist)[None, :] == np.arange(32)[:, None]).astype(f)
    c["bias_onehot"] = np.vstack([one, np.where((dist < 0) | (dist > WIN), f(NEG), f(0))[None]])
    own = np.where(np.arange(NB)[:, None] == np.arange(NB)[None, :], f(0), f(NEG))
    c["own_seq"] = np.tile(np.repeat(own, NS, axis=1).reshape(1, -1), (P, 1))
    c["causal_T"] = (p[:, None] <= p[None, :]).astype(f)
    tok = np.arange(NTS)
    c["causal_seq_T"] = ((tok[:, None] // NS == tok[None, :] // NS) & (tok[:, None] <= tok[None, :])).astype(f)
    c["spread8"] = (np.arange(NS)[:, None] == tok[None, :] % NS).astype(f)
    cs = np.arange(NC_S)[:, None] * 16
    ss = np.arange(NBLK)[None, :] * SELB
    c["overlap"] = ((cs < ss + SELB) & (cs + 32 > ss)).astype(f)
    hs = (p // 32) * NS + p % NS
    c["sum_group"] = (hs[:, None] == hs[None, :]).astype(f)
    blk = np.arange(NBLK)
    cur = PAST // SELB
    forced = (blk == 0) | (blk == cur) | (blk == cur - 1)
    c["sel_keep"] = np.tile(np.where(forced, 0, 1).astype(f), (P, 1))
    c["sel_force"] = np.tile(np.where(forced, 1e6, 0).astype(f), (P, 1))
    c["low_half"] = np.stack([(p < 64), (p >= 64)], 1).astype(f)
    c["even_group"] = np.stack([(p // 16) % 2 == 0, (p // 16) % 2 == 1], 1).astype(f)
    c["half_ones"] = ((p[:, None] // 64) == (p[None, :] // 64)).astype(f)
    c["before"] = (p[:, None] < p[None, :]).astype(f)
    c["ones"] = np.ones((P, P), f)
    c["iota"] = np.tile(p.astype(f), (P, 1))
    c["earlier4"] = np.tile((np.arange(4)[:, None] > np.arange(4)[None, :]).astype(f).reshape(1, -1), (P, 1))
    c["group4"] = np.tile(np.arange(4).astype(f), (P, 1))
    cols = sum(a.shape[1] for a in c.values())
    pack = np.zeros((P, cols), f)
    at, off = {}, 0
    for k, a in c.items():
        pack[:a.shape[0], off:off + a.shape[1]] = a
        at[k] = (off, a.shape[0], a.shape[1])
        off += a.shape[1]
    return pack, at


FEAT = (("norm_mix", 16), ("norm_ffn", 16), ("out_norm", 16), ("ssm_a_re", 16), ("ssm_a_im", 16),
        ("ssm_d", 4), ("ssm_glu_b", 4), ("gmlp_bs", 4), ("cmp_pos", 32))
FEAT_AT = {}
_o = 0
for _n, _r in FEAT:
    FEAT_AT[_n] = (_o, _r)
    _o += _r
NFEAT = _o


def view(ap, *dims):
    return bass.AP(ap.tensor, ap.offset, [list(ap.ap[0])] + [list(d) for d in dims])


def dram(ap, offset, *dims):
    return bass.AP(ap.tensor, offset, [list(d) for d in dims])


class Chain:

    def __init__(self, eng, sem, base=0):
        self.eng, self.sem, self.base, self.n = eng, sem, base, 0

    def mark(self, ins):
        self.n += 1
        ins.then_inc(self.sem, 1)
        return self.n

    def wait(self, n=None):
        self.eng.wait_ge(self.sem, self.base + (self.n if n is None else n))

    def link(self, ins):
        self.mark(ins)
        self.wait()


def split_high(copy, high, x):
    return copy(high.bitcast(F32R), x)


def split_low(dve, low, x, high):
    return dve.tensor_tensor(low.bitcast(F32R), x, high, ALU.subtract)


def matmul_split(pe, out, a_high, a_low, b_high, b_low, start, stop):
    r = lambda ap: ap.bitcast(F32R)
    pe.matmul(out, r(a_high), r(b_high), start=start, stop=False)
    pe.matmul(out, r(a_high), r(b_low), start=False, stop=False)
    return pe.matmul(out, r(a_low), r(b_high), start=False, stop=stop)


def split_turned_act(act, jobs, tmp, sems, high_T):
    turned, stored, high, low = sems
    for n, (t, k0) in enumerate(jobs):
        act.wait_ge(stored, n + 1)
        split_high(act.copy, high_T[:, k0:k0 + 4, t * P:t * P + ROWS[t]], tmp[n % 2][:, :, :ROWS[t]]).then_inc(high, 1)


def split_turned_dve(dve, jobs, bank, tmp, gain, sems, high_T, low_T):
    turned, stored, high, low = sems

    def rest(n):
        t, k0 = jobs[n]
        x = slice(t * P, t * P + ROWS[t])
        dve.wait_ge(high, n + 1)
        split_low(dve, low_T[:, k0:k0 + 4, x], tmp[n % 2][:, :, :ROWS[t]], high_T[:, k0:k0 + 4, x]).then_inc(low, 1)

    for n, (t, k0) in enumerate(jobs):
        r = ROWS[t]
        dve.wait_ge(turned, n + 1)
        if n >= 2:
            dve.wait_ge(low, n - 1)
        dve.tensor_tensor(tmp[n % 2][:, :, :r], view(bank(n), (P, 4), (1, r)), view(gain(k0), (1, 4), (0, r)), ALU.mult).then_inc(stored, 1)
        if n:
            rest(n - 1)
    rest(len(jobs) - 1)


def phase_norm_in(nc, m, io):
    with ExitStack() as ctx:
        junk = ctx.enter_context(nc.sbuf_tensor("norm_junk", [P, D], F32))
        h = ctx.enter_context(nc.sbuf_tensor("norm_h", [P, 3, D], F32))
        x = ctx.enter_context(nc.sbuf_tensor("norm_x", [P, 3, D], F32))
        frow = ctx.enter_context(nc.sbuf_tensor("feat_rows", [NFEAT, P], F32))
        ssq = ctx.enter_context(nc.sbuf_tensor("norm_ssq", [P, 3], F32))
        rms = ctx.enter_context(nc.sbuf_tensor("norm_rms", [P, 3], F32))
        rstd = ctx.enter_context(nc.sbuf_tensor("norm_rstd", [P, 3], F32))
        tps = ctx.enter_context(nc.psum_tensor("norm_tps", [P, 4, 512], F32))
        const_in, feat_in, gain_in = m.sem("const_in"), m.sem("feat_in"), m.sem("gain_in")
        x_in = [m.sem(f"x_in{t}") for t in range(3)]
        eps_set, feat_turned, feat_ready = m.sem("eps_set"), m.sem("feat_turned"), m.sem("feat_ready")
        rms_ready, rstd_ready, h_ready = m.sem("rms_ready"), m.sem("rstd_ready"), m.sem("h_ready")
        turned, stored, ssq_done = m.sem("hT_turned"), m.sem("hT_stored"), m.sem("ssq_done")
        sems = (turned, stored, m.sem("hT_high"), m.sem("hT_low"))
        tmp = [ctx.enter_context(nc.sbuf_tensor(f"hT_tmp{u}", [P, 4, P], F32)) for u in range(2)]
        jobs = [(t, k0) for t in range(3) for k0 in (0, 4, 8, 12)]
        block = ctx.enter_context(nc.Block())
        C = m.const

        @block.sync
        def _(sp):
            for t in range(3):
                src = dram(io["x_prompt"], t * P * D, (D, P), (1, D)) if t < 2 else dram(io["x_sample"], 0, (D, NTS), (1, D))
                sp.dma_start(x[:ROWS[t], t, :], src).then_inc(x_in[t], 16)
            sp.dma_start(m.cpack[:], io["cpack"]).then_inc(const_in, 16)
            sp.dma_start(m.ptab[:], dram(io["page_table"], 0, (NB * NPG, 1), (1, NB * NPG))).then_inc(gain_in, 16)
            for name, rows in FEAT:
                o, _ = FEAT_AT[name]
                src = io[name]
                sp.dma_start(frow[o:o + rows, :], dram(src, 0, (P, rows), (1, P))).then_inc(feat_in, 16)
            for q in range(4):
                load_piece(sp, io["w_in"], PCH, m.wslot, m.w_in_landed, 0, q)
            sp.dma_start(m.qkg[:], dram(io["qk_norm"], 0, (0, P), (1, 4 * HD))).then_inc(gain_in, 16)
            sp.wait_ge(gain_in, 32)

        @block.vector
        def _(dve):
            dve.memset(m.eps[:], EPS).then_inc(eps_set, 1)
            dve.memset(m.tab[32:33, :], 1.0).then_inc(eps_set, 1)
            dve.wait_ge(feat_turned, 1)
            dve.tensor_copy(m.feat[:], tps[:, 0, :NFEAT]).then_inc(feat_ready, 1)
            for t in range(3):
                r = ROWS[t]
                dve.wait_ge(rms_ready, t + 1)
                dve.reciprocal(rstd[:r, t:t + 1], rms[:r, t:t + 1]).then_inc(rstd_ready, 1)
                dve.wait_ge(rstd_ready, t + 1)
                dve.tensor_scalar(h[:r, t, :], x[:r, t, :], rstd[:r, t:t + 1], None, ALU.mult).then_inc(h_ready, 1)
            dve.wait_ge(feat_ready, 1)
            split_turned_dve(dve, jobs, lambda n: tps[:, n % 2 + 1, :], tmp, lambda k0: m.feat[:, FEAT_AT["norm_mix"][0] + k0:][:, :4],
                             sems, m.hTh, m.hTl)

        @block.scalar
        def _(act):
            act.wait_ge(eps_set, 2)
            for t in range(3):
                r = ROWS[t]
                act.wait_ge(x_in[t], 16)
                if t:
                    act.wait_ge(ssq_done, t)
                act.activation(junk[:r, :], x[:r, t, :], ACT.Square, accum_out=ssq[:r, t:t + 1]).then_inc(ssq_done, 1)
                act.wait_ge(ssq_done, t + 1)
                act.activation(rms[:r, t:t + 1], ssq[:r, t:t + 1], ACT.Sqrt, bias=m.eps[:r, :], scale=1.0 / D).then_inc(rms_ready, 1)
            split_turned_act(act, jobs, tmp, sems, m.hTh)

        @block.tensor
        def _(pe):
            pe.wait_ge(const_in, 16)
            pe.wait_ge(feat_in, 16 * len(FEAT))
            pe.transpose(tps[:, 0, :NFEAT], frow[:], C("ident")[:NFEAT, :NFEAT]).then_inc(feat_turned, 1)
            for n in range(12):
                t, q = divmod(n, 4)
                r = ROWS[t]
                pe.wait_ge(h_ready, t + 1)
                if n >= 2:
                    pe.wait_ge(stored, n - 1)
                for j in range(4):
                    k = 4 * q + j
                    mm = pe.transpose(tps[:, n % 2 + 1, j * P:j * P + r], h[:r, t, k * P:(k + 1) * P],
                                      C("ident")[:r, :r])
                mm.then_inc(turned, 1)


class Stream:

    def __init__(self, m, name, pairs, width, matrix, xTh, xTl, slots, highs, lows, landed):
        self.pairs, self.width, self.matrix, self.xTh, self.xTl = pairs, width, matrix, xTh, xTl
        self.slots, self.highs, self.lows, self.landed = slots, highs, lows, landed
        self.high, self.low, self.used = m.sem(name + "_w_high"), m.sem(name + "_w_low"), m.sem(name + "_w_used")


def load_piece(sp, matrix, width, slots, landed, chunk, q):
    src = matrix[0, q * 512:(q + 1) * 512, bass.ds(chunk * width, width)]
    sp.dma_start(slots[q][:], src.rearrange("(k p) n -> p k n", p=P)).then_inc(landed[q], 16)


def stream_load(sp, z):
    def load(i, n):
        sp.wait_ge(z.low, i * 8 + (n + 1))
        load_piece(sp, z.matrix, z.width, z.slots, z.landed, 2 * i + (1 + n // 4), n % 4)

    with sp.Fori(0, z.pairs - 1) as i:
        for n in range(8):
            load(i, n)
    for n in range(4):
        load(z.pairs - 1, n)


def stream_pe(pe, z, acc, free_v, free_a):
    with pe.Fori(0, z.pairs) as i:
        for c in range(2):
            pe.wait_ge(free_v, i * 2 + (c + 1))
            pe.wait_ge(free_a, i * 2 + (c + 1))
            for q in range(4):
                pe.wait_ge(z.low, i * 8 + (4 * c + q + 1))
                for kk in range(4):
                    k = 4 * q + kk
                    for t in range(3):
                        x = slice(t * P, t * P + ROWS[t])
                        mm = matmul_split(pe, acc[c][t][:ROWS[t], :z.width], z.xTh(k)[:, x], z.xTl(k)[:, x],
                                          z.highs[q][:, kk, :], z.lows[q][:, kk, :], k == 0, k == KT - 1)
                mm.then_inc(z.used, 1)


def stream_split(eng, z, split, copy_out):
    def chunk(i, c, last=False):
        split(i, 4 * c + 2)
        split(i, 4 * c + 3)
        if not last:
            split(i, 4 * c + 4)
            split(i, 4 * c + 5)
        copy_out(i, c)

    split(0, 0)
    split(0, 1)
    with eng.Fori(0, z.pairs - 1) as i:
        chunk(i, 0)
        chunk(i, 1)
    chunk(z.pairs - 1, 0)
    chunk(z.pairs - 1, 1, last=True)


def stream_act(act, z, copy_out):
    def split(i, n):
        act.wait_ge(z.landed[n % 4], i * 32 + (n // 4 + 1) * 16)
        act.wait_ge(z.used, i * 8 + (n + 1))
        split_high(act.copy, z.highs[n % 4][:], z.slots[n % 4][:]).then_inc(z.high, 1)

    act.sem_inc(z.used, 4)
    stream_split(act, z, split, copy_out)


def stream_dve(dve, z, copy_out):
    def split(i, n):
        dve.wait_ge(z.high, i * 8 + (n + 1))
        split_low(dve, z.lows[n % 4][:], z.slots[n % 4][:], z.highs[n % 4][:]).then_inc(z.low, 1)

    stream_split(dve, z, split, copy_out)


def phase_project(nc, m, io):
    with ExitStack() as ctx:
        acc = [[ctx.enter_context(nc.psum_tensor(f"proj_acc{c}{t}", [P, 512], F32)) for t in range(3)] for c in range(2)]
        highs = [ctx.enter_context(nc.sbuf_tensor(f"w_in_high{q}", [P, 4, PCH], F32)) for q in range(4)]
        lows = [ctx.enter_context(nc.sbuf_tensor(f"w_in_low{q}", [P, 4, PCH], F32)) for q in range(4)]
        free_v, free_a = m.sem("proj_acc_free_v"), m.sem("proj_acc_free_a")
        z = Stream(m, "proj", NPCH // 2, PCH, io["w_in"], lambda k: m.hTh[:, k, :], lambda k: m.hTl[:, k, :], m.wslot, highs, lows, m.w_in_landed)
        block = ctx.enter_context(nc.Block())

        @block.sync
        def _(sp):
            stream_load(sp, z)

        @block.tensor
        def _(pe):
            stream_pe(pe, z, acc, free_v, free_a)

        @block.vector
        def _(dve):
            def copy_out(i, c):
                dve.wait_ge(z.used, i * 8 + (4 * c + 8))
                dve.nop()
                for t in range(2):
                    cp = dve.tensor_copy(m.proj[:, t, bass.ds((2 * i + c) * PCH, PCH)], acc[c][t][:, :PCH])
                cp.then_inc(free_v, 1)

            dve.sem_inc(free_v, 2)
            stream_dve(dve, z, copy_out)

        @block.scalar
        def _(act):
            def copy_out(i, c):
                act.wait_ge(z.used, i * 8 + (4 * c + 8))
                act.nop()
                act.copy(m.proj[:NTS, 2, bass.ds((2 * i + c) * PCH, PCH)], acc[c][2][:NTS, :PCH]).then_inc(free_a, 1)

            act.sem_inc(free_a, 2)
            stream_act(act, z, copy_out)


def load_compress_pages(eng, m, io, b, u, odd):
    for j in range(odd, NPG, 2):
        r = eng.value_load(m.ptab[0:1, bass.ds(b * NPG + j, 1)], min_val=0, max_val=N_PHYS - 1)
        page = io["cache_kv_cmp"][bass.ds(r, 1)].rearrange("n l (p q) h k d -> q p (n l h k) d", q=2)
        for r2 in range(2):
            eng.dma_start(view(m.cmp_pages[u][(j % 2) * 64:(j % 2) * 64 + 64, j // 2, r2 * HD:], (P, 8), (1, HD)),
                          page[r2]).then_inc(m.cmp_pages_in[odd][u], 16)


def compress_first_loads(sp, m, io):
    for kv in range(2):
        for half in range(2):
            sp.dma_start(m.w1[:, kv, :, half * HD:half * HD + HD],
                         dram(io["cmp_w1"], (kv * 2048 + half * 1024) * HD, (HD, P), (P * HD, 8), (1, HD))).then_inc(m.cmp_w_in, 16)
    sp.dma_start(m.w2[:], dram(io["cmp_w2"], 0, (HD, P), (1, HD))).then_inc(m.cmp_w_in, 16)
    for hh in range(2):
        sp.dma_start(m.qkcol[hh * HD:hh * HD + HD, :], dram(io["qk_norm"], 0, (1, HD), (HD, 4))).then_inc(m.cmp_w_in, 16)
    sp.wait_ge(m.p_cmp_out, 32)
    for r2 in range(2):
        sp.dma_start(view(m.cmp_pages[1][:, 0, r2 * HD:], (P, 8), (1, HD)),
                     dram(io["p_kv_cmp"], r2 * 512, (1024, P), (HD, 8), (1, HD))).then_inc(m.p_pages_in, 16)



def phase_heads(nc, m, io):
    NH = NQ + 2 * NKV
    with ExitStack() as ctx:
        sq = ctx.enter_context(nc.sbuf_tensor("head_sq", [P, NH, HD], F32))
        ssq = ctx.enter_context(nc.sbuf_tensor("head_ssq", [P, 3, NH], F32))
        rms = ctx.enter_context(nc.sbuf_tensor("head_rms", [P, 3, NH], F32))
        rstd = ctx.enter_context(nc.sbuf_tensor("head_rstd", [P, 3, NH], F32))
        brow = ctx.enter_context(nc.sbuf_tensor("bias_row", [NQ, LB], F32))
        bps = ctx.enter_context(nc.psum_tensor("bias_ps", [NQ, 1024], F32))
        tab_in, bias_done, brow_ready = m.sem("tab_in"), m.sem("bias_done"), m.sem("brow_ready")
        bias_out, sum_done, rms_done = m.sem("bias_out"), m.sem("head_ssq_done"), m.sem("head_rms_done")
        v_step = m.sem("head_v_step")
        block = ctx.enter_context(nc.Block())
        kv_flat = NKV * 2 * HD

        @block.sync
        def _(sp):
            sp.dma_start(m.tab[:32, :], io["rel_bias"]).then_inc(tab_in, 16)
            for t in range(2):
                sp.dma_start(dram(io["p_kv_cmp"], t * P * kv_flat, (kv_flat, P), (1, kv_flat)),
                             m.proj[:, t, O_KV:O_KV + kv_flat]).then_inc(m.p_cmp_out, 16)
            m.store(sp, dram(io["s_kv_cmp"], 0, (kv_flat, NTS), (1, kv_flat)), m.proj[:NTS, 2, O_KV:O_KV + kv_flat])
            sp.wait_ge(brow_ready, 1)
            sp.dma_start(io["bias_rows"], brow[:]).then_inc(bias_out, 16)
            sp.wait_ge(bias_out, 16)
            sp.dma_start(io["bias_rep"], dram(io["bias_rows"], D0 - 2 * P + 1, (0, P), (LB, NQ), (1, TRI))).then_inc(m.rep_out, 16)
            compress_first_loads(sp, m, io)
            load_compress_pages(sp, m, io, 0, 0, 0)

        @block.gpsimd
        def _(pool):
            load_compress_pages(pool, m, io, 0, 0, 1)

        @block.tensor
        def _(pe):
            pe.wait_ge(tab_in, 16)
            pe.matmul(bps[:, :512], m.tab[:], m.const("bias_onehot")[:, :512], start=True, stop=True)
            pe.matmul(bps[:, 512:LB], m.tab[:], m.const("bias_onehot")[:, 512:], start=True, stop=True).then_inc(bias_done, 1)

        @block.vector
        def _(dve):
            v = Chain(dve, v_step)
            dve.wait_ge(bias_done, 1)
            dve.tensor_copy(brow[:], bps[:, :LB]).then_inc(brow_ready, 1)
            for t in range(3):
                r = ROWS[t]
                q = m.proj[:r, t, O_Q:O_Q + AW]
                k = view(m.proj[:r, t, O_KV + kv_flat:O_KV + kv_flat + 1], (kv_flat, 2), (2 * HD, NKV), (1, HD))
                v.mark(dve.tensor_tensor(view(sq[:r, 0, :], (1, AW)), q, q, ALU.mult))
                v.link(dve.tensor_tensor(view(sq[:r, NQ, :], (NKV * HD, 2), (HD, NKV), (1, HD)), k, k, ALU.mult))
                dve.tensor_reduce(ssq[:r, t, :], sq[:r], AX_X, ALU.add).then_inc(sum_done, 1)
                dve.wait_ge(sum_done, t + 1)
            for t in range(3):
                r = ROWS[t]
                q = view(m.proj[:r, t, O_Q:], (HD, NQ), (1, HD))
                k = view(m.proj[:r, t, O_KV + kv_flat:O_KV + kv_flat + 1], (kv_flat, 2), (2 * HD, NKV), (1, HD))
                dve.wait_ge(rms_done, t + 1)
                v.link(dve.reciprocal(rstd[:r, t, :], rms[:r, t, :]))
                v.mark(dve.tensor_tensor(q, q, view(rstd[:r, t, :], (1, NQ), (0, HD)), ALU.mult))
                v.link(dve.tensor_tensor(k, k, view(rstd[:r, t, NQ:], (NKV, 2), (1, NKV), (0, HD)), ALU.mult))
                gain_k = view(m.qkg[:r, 2, :], (HD, 2), (0, NKV), (1, HD))
                for p in range(2):
                    v.mark(dve.tensor_tensor(view(m.q_pairs[:r, t, p * 512:], (HD, 2), (2 * HD, G), (1, HD)),
                                             view(m.proj[:r, t, O_Q + p * 512:], (G * HD, 2), (HD, G), (1, HD)),
                                             view(m.qkg[:r, 0, :], (0, 2), (0, G), (1, HD)), ALU.mult))
                v.mark(dve.tensor_tensor(view(m.k_pairs[:r, t, :], (KVW, 2), (HD, NKV), (1, HD)), k, gain_k, ALU.mult))
                v.mark(dve.tensor_tensor(k, k, gain_k, ALU.mult))

        @block.scalar
        def _(act):
            for t in range(3):
                r = ROWS[t]
                act.wait_ge(sum_done, t + 1)
                act.activation(rms[:r, t, :], ssq[:r, t, :], ACT.Sqrt, bias=m.eps[:r, :], scale=1.0 / HD).then_inc(rms_done, 1)
            for t in range(3):
                r = ROWS[2 - t]
                g = m.proj[:r, 2 - t, O_GATE:O_GATE + 48]
                act.activation(g, g, ACT.Sigmoid)


class Compression:
    pass


class CompressSems:
    def __init__(self, m, who):
        self.turned, self.stored_v, self.stored_a = m.sem(who + "_turned"), m.sem(who + "_stored_v"), m.sem(who + "_stored_a")
        self.half_blocks, self.half_stored = m.sem(who + "_half_blocks"), m.sem(who + "_half_stored")
        self.pre_gelu, self.gelu = m.sem(who + "_pre_gelu"), m.sem(who + "_gelu")
        self.kv_made, self.kv_stored = m.sem(who + "_kv_made"), m.sem(who + "_kv_stored")


class CompressCounts:

    def __init__(self, b):
        self.turn, self.group, self.two, self.one = b * 16, b * 8, b * 2, b


def compress_pe(pe, m, z, b):
    s = z.s
    n_groups = 8 * z.tiles // 4
    for n in range(n_groups):
        if n >= 4:
            pe.wait_ge((s.stored_v, s.stored_a)[n % 2], b.group + ((n - 4) // 2 + 1))
        for c in range(4):
            hk, j = divmod(4 * n + c, z.tiles)
            kv, h = divmod(hk, NKV)
            pair = z.pages[:, j, (h * 2 + kv) * P:(h * 2 + kv + 1) * P]
            mm = pe.transpose(z.tps[:, n % 4, c * P:(c + 1) * P], pair, m.const("ident"))
        mm.then_inc(s.turned, 1)
        if (n + 1) % (n_groups // 2) == 0:
            kv = (n + 1) // (n_groups // 2) - 1
            pe.wait_ge(s.stored_v, b.group + (n // 2 + 1))
            pe.wait_ge(s.stored_a, b.group + (n + 1) // 2)
            for rp in range(8):
                mov = view(z.xT[:, rp:], (z.tiles * P, NKV), (8, z.hb))
                mm = pe.matmul(view(z.zps[:, kv, :], (z.hb, NKV), (1, z.hb)), m.w1[:, kv, rp, :], mov, start=(rp == 0), stop=(rp == 7))
            mm.then_inc(s.half_blocks, 1)
    n = z.hb - 1
    for kv in range(2):
        pe.wait_ge(s.half_stored, b.two + (kv + 1))
        out = view(z.gps[kv * HD:kv * HD + HD, :], (n, NKV), (1, n))
        for half in range(2):
            mm = pe.matmul(out, m.const("ident")[:, half * HD:half * HD + HD],
                           view(z.zz[:, kv, half:], (z.hb, NKV), (1, n)), start=(half == 0), stop=(half == 1))
    mm.then_inc(s.pre_gelu, 1)
    pe.wait_ge(s.gelu, b.one + 1)
    for h in range(NKV):
        mm = pe.matmul(z.ops[:n, h * HD:(h + 1) * HD], z.gel[HD:, h * n:(h + 1) * n], m.w2[HD:, :],
                       start=True, stop=True)
    for hh in range(2):
        mm = pe.matmul(view(z.zps[hh * HD:hh * HD + HD, 0, :], (n, 2), (1, n)), m.w2[:HD, :],
                       view(z.gel[:HD, hh * n:], (2 * n, 2), (1, n)), start=True, stop=True)
    mm.then_inc(s.kv_made, 1)


def compress_copy(eng, copy, m, z, b, me):
    s = z.s
    n_groups = 8 * z.tiles // 4
    for n in range(me, n_groups, 2):
        eng.wait_ge(s.turned, b.turn + (n + 1))
        o = n % (n_groups // 2) * 512
        copy(z.xT[:, o:o + 512], z.tps[:, n % 4, :]).then_inc((s.stored_v, s.stored_a)[me], 1)


def phase_compress(nc, m, io):
    with ExitStack() as ctx:
        sb = lambda n, sh: ctx.enter_context(nc.sbuf_tensor(n, sh, F32))
        pages, pages_in, pages_in0, w_in = m.cmp_pages, m.cmp_pages_in, m.p_pages_in, m.cmp_w_in
        xT, zz, gel = sb("cmp_xT", [P, 4 * 8 * P]), sb("cmp_half", [P, 2, 512]), sb("cmp_gelu", [P, 512])
        ksq, kinv = sb("cmp_ksq", [P, 512]), sb("cmp_kinv", [P, 512])
        posb = sb("cmp_posb", [P, 1])
        tps = ctx.enter_context(nc.psum_tensor("cmp_tps", [P, 4, 512], F32))
        zps = ctx.enter_context(nc.psum_tensor("cmp_zps", [P, 2, 512], F32))
        gps = ctx.enter_context(nc.psum_tensor("cmp_gps", [P, 512], F32))
        ops = ctx.enter_context(nc.psum_tensor("cmp_ops", [P, 512], F32))
        sems = [CompressSems(m, w) for w in ("pc", "sc")]
        pos_done, pos_ready, kn = m.sem("cmp_pos_done"), m.sem("cmp_pos_ready"), m.sem("kc_step")
        kn_sum, kn_rms, kc_inv = m.sem("kc_sum"), m.sem("kc_rms"), m.sem("kc_inv")
        zp, zs = Compression(), Compression()
        for z, z.s, z.tiles, z.hb in ((zp, sems[0], 1, 16), (zs, sems[1], 8, 128)):
            z.tps, z.zps, z.gps, z.ops, z.zz, z.gel, z.xT = tps, zps, gps, ops, zz, gel, xT
        zero = CompressCounts(0)
        block = ctx.enter_context(nc.Block())

        at = CompressCounts
        @block.sync
        def _(sp):
            sp.wait_ge(sems[0].turned, 2)
            load_compress_pages(sp, m, io, 1, 1, 0)
            with sp.Fori(1, NB // 2) as i:
                for u in range(2):
                    sp.wait_ge(sems[1].turned, i * 32 + (16 * u - 16))
                    load_compress_pages(sp, m, io, 2 * i + u, u, 0)

        @block.gpsimd
        def _(pool):
            pool.wait_ge(sems[0].turned, 2)
            load_compress_pages(pool, m, io, 1, 1, 1)
            with pool.Fori(1, NB // 2) as i:
                for u in range(2):
                    pool.wait_ge(sems[1].turned, i * 32 + (16 * u - 16))
                    load_compress_pages(pool, m, io, 2 * i + u, u, 1)

        @block.tensor
        def _(pe):
            pe.wait_ge(w_in, 16 * 7)
            for kv in range(2):
                for n in range(16):
                    col = FEAT_AT["cmp_pos"][0] + kv * 16 + n
                    mm = pe.matmul(gps[kv * HD:kv * HD + HD, 0:1], m.w1[:, kv, n % 8, (n // 8) * HD:(n // 8) * HD + HD],
                                   m.feat[:, col:col + 1], start=(n == 0), stop=(n == 15))
            mm.then_inc(pos_done, 1)
            pe.wait_ge(pages_in0, 32)
            pe.wait_ge(pos_ready, 1)
            zp.pages = pages[1]
            compress_pe(pe, m, zp, zero)
            pe.wait_ge(sems[0].kv_stored, 2)
            with pe.Fori(0, NB // 2) as i:
                for u in range(2):
                    for odd in range(2):
                        pe.wait_ge(pages_in[odd][u], (i + 1) * (16 * NPG))
                    zs.pages = pages[u]
                    compress_pe(pe, m, zs, at(2 * i + u))
                    pe.wait_ge(sems[1].kv_stored, (2 * i + u) * 2 + 2)
            for c in range(5):
                n = 2 * NC_P if c == 4 else 4 * NC_S
                pe.wait_ge(kn, c + 1)
                if c:
                    pe.wait_ge(kn_rms, c)
                pe.matmul(gps[:, :n], m.const("half_ones"), ksq[:, :n], start=True, stop=True).then_inc(kn_sum, 1)

        @block.vector
        def _(dve):
            dve.wait_ge(pos_done, 1)
            dve.tensor_copy(posb[:], gps[:, 0:1]).then_inc(pos_ready, 1)

            def one(z, b, kdst):
                s, n = z.s, z.hb - 1
                compress_copy(dve, dve.tensor_copy, m, z, b, 0)
                dve.wait_ge(s.half_blocks, b.two + 1)
                dve.tensor_copy(zz[:, 0, :NKV * z.hb], zps[:, 0, :NKV * z.hb]).then_inc(s.half_stored, 1)
                dve.wait_ge(s.half_blocks, b.two + 2)
                dve.wait_ge(s.half_stored, b.two + 1)
                dve.tensor_copy(zz[:, 1, :NKV * z.hb], zps[:, 1, :NKV * z.hb]).then_inc(s.half_stored, 1)
                dve.wait_ge(s.kv_made, b.one + 1)
                dve.nop()
                dve.tensor_copy(kdst, zps[:, 0, :2 * n]).then_inc(s.kv_stored, 1)

            one(zp, zero, m.kc_p[:])
            with dve.Fori(0, NB // 2) as i:
                for u in range(2):
                    one(zs, at(2 * i + u), m.kc_s[:, bass.ds((2 * i + u) * 2 * NC_S, 2 * NC_S)])
            dve.wait_ge(sems[1].kv_stored, 2 * NB)
            gain = m.qkcol[:, 1:2]
            for c in range(5):
                n = 2 * NC_P if c == 4 else 4 * NC_S
                k = m.kc_p[:] if c == 4 else m.kc_s[:, c * n:(c + 1) * n]
                if c:
                    dve.wait_ge(kn_sum, c)
                dve.tensor_tensor(ksq[:, :n], k, k, ALU.mult).then_inc(kn, 1)
                dve.wait_ge(kn_rms, c + 1)
                dve.reciprocal(kinv[:, :n], kinv[:, :n]).then_inc(kc_inv, 1)
                dve.wait_ge(kc_inv, 2 * c + 1)
                dve.scalar_tensor_tensor(out=k, in0=k, scalar=gain, in1=kinv[:, :n], op0=ALU.mult, op1=ALU.mult).then_inc(kc_inv, 1)

        @block.scalar
        def _(act):
            def one(z, b, vdst):
                s, n = z.s, z.hb - 1
                compress_copy(act, act.copy, m, z, b, 1)
                act.wait_ge(s.pre_gelu, b.one + 1)
                act.activation(gel[:, :NKV * n], gps[:, :NKV * n], ACT.Gelu_apprx_tanh, bias=posb[:]).then_inc(s.gelu, 1)
                act.wait_ge(s.kv_made, b.one + 1)
                act.nop()
                act.copy(vdst, ops[:n, :KVW]).then_inc(s.kv_stored, 1)

            act.wait_ge(pos_ready, 1)
            one(zp, zero, m.vc_p[:])
            with act.Fori(0, NB // 2) as i:
                for u in range(2):
                    one(zs, at(2 * i + u), m.vc_s[:, bass.ds((2 * i + u) * KVW, KVW)])
            for c in range(5):
                n = 2 * NC_P if c == 4 else 4 * NC_S
                act.wait_ge(kn_sum, c + 1)
                if c:
                    act.wait_ge(kc_inv, 2 * c)
                act.activation(kinv[:, :n], gps[:, :n], ACT.Sqrt, bias=m.eps[:], scale=1.0 / HD).then_inc(kn_rms, 1)


def phase_turn_heads(nc, m, io):
    with ExitStack() as ctx:
        tps = ctx.enter_context(nc.psum_tensor("turn_tps", [P, 4, 512], F32))
        turned, stored_v, stored_a = m.sem("heads_turned"), m.sem("heads_stored_v"), m.sem("heads_stored_a")
        block = ctx.enter_context(nc.Block())

        @block.tensor
        def _(pe):
            for n in range(9):
                t, q = divmod(n, 3)
                r = ROWS[t]
                if n >= 4:
                    pe.wait_ge((stored_v, stored_a)[n % 2], (n - 4) // 2 + 1)
                for c in range(4):
                    src = m.q_pairs[:r, t, (4 * q + c) * P:][:, :P] if q < 2 else m.k_pairs[:r, t, c * P:(c + 1) * P]
                    mm = pe.transpose(tps[:, n % 4, c * P:c * P + r], src, m.const("ident")[:r, :r])
                mm.then_inc(turned, 1)

        def copy_out(eng, copy, me, sem):
            for n in range(me, 9, 2):
                t, q = divmod(n, 3)
                eng.wait_ge(turned, n + 1)
                copy(m.qkT[:, 4 * q:4 * q + 4, t * P:t * P + ROWS[t]], view(tps[:, n % 4, :], (P, 4), (1, ROWS[t]))).then_inc(sem, 1)

        @block.vector
        def _(dve):
            copy_out(dve, dve.tensor_copy, 0, stored_v)

        @block.scalar
        def _(act):
            copy_out(act, act.copy, 1, stored_a)


def phase_prompt_attention(nc, m, io):
    steps = [(t, h) for t in range(2) for h in range(NKV)]
    kv_flat = NKV * 2 * HD
    with ExitStack() as ctx:
        sb = lambda n, sh: ctx.enter_context(nc.sbuf_tensor(n, sh, F32))
        lg = [sb(f"pa_logits{u}", [P, 2, G, 2 * P]) for u in range(2)]
        lc = [sb(f"pa_logits_cmp{u}", [P, G, 16]) for u in range(2)]
        mx, nmx = sb("pa_max", [P, 12]), [sb(f"pa_neg_max{u}", [P, 12]) for u in range(2)]
        den = [sb(f"pa_den{u}", [P, 12]) for u in range(2)]
        rden, ok, fac = sb("pa_rden", [P, 12]), sb("pa_any_key", [P, 4]), sb("pa_fac", [P, 12])
        pT, pTc = sb("pa_pT", [P, 4, 512]), sb("pa_pTc", [NC_P, 512])
        osw, oc = sb("pa_osw", [P, 2, G * HD]), sb("pa_oc", [P, G * HD])
        S = ctx.enter_context(nc.psum_tensor("pa_S", [P, 4, 512], F32))
        X = ctx.enter_context(nc.psum_tensor("pa_X", [P, 512], F32))
        tps = ctx.enter_context(nc.psum_tensor("pa_tps", [P, 2, 512], F32))
        O = ctx.enter_context(nc.psum_tensor("pa_O", [P, 512], F32))
        bias_tri = sb("pa_bias", [P, NQ, 2 * P])
        near = sb("bias_new_keys", [P, NS])
        qz = sb("pa_q_padded", [P, NQ, 2 * P])
        n_ = lambda n: m.sem("pa_" + n)
        q_zeroed, q_padded = n_("q_zeroed"), n_("q_padded")
        tri_in, bias_in, gate_out, gate_in = n_("tri_in"), n_("bias_in"), n_("gate_out"), n_("gate_in")
        logits, logits_read, neg_max, probs = n_("logits"), n_("logits_read"), n_("neg_max"), n_("probs")
        turned, stored, pv, o_read, v_step = n_("turned"), n_("stored"), n_("pv"), n_("o_read"), n_("v_step")
        block = ctx.enter_context(nc.Block())

        def groups(t):
            return [(0, 0)] + [(br, kt) for br in (1, 2) for kt in range(t + 1)]

        first = [0]
        for t, h in steps:
            first.append(first[-1] + len(groups(t)))

        @block.sync
        def _(sp):
            sp.wait_ge(m.rep_out, 16)
            sp.dma_start(bias_tri[:], dram(io["bias_rep"], P - 1, (NQ * TRI - 1, P), (TRI, NQ), (1, 2 * P))).then_inc(tri_in, 16)
            sp.dma_start(io["gate_rows"], m.proj[:NTS, 2, O_GATE:O_GATE + 48]).then_inc(gate_out, 16)
            for i in range(NS):
                to = slice(i, P, NS)
                sp.dma_start(m.bias_win[to, :], dram(io["bias_rows"], NS - 1 - i, (LB, NQ), (1, WIN))).then_inc(bias_in, 16)
                sp.dma_start(near[to, :], dram(io["bias_rows"], D0 - i, (LB, NQ), (1, NS))).then_inc(bias_in, 16)
                sp.dma_start(m.bias_cmp[to, NC_S - 7:], dram(io["bias_rows"], D0 - 97 - i, (LB, NQ), (16, 7))).then_inc(bias_in, 16)
            sp.wait_ge(gate_out, 16)
            for i in range(NS):
                for br in range(3):
                    sp.dma_start(m.gate_s[i:P:NS, br, :],
                                 dram(io["gate_rows"], i * 48 + br * NQ, (1, NQ), (48 * NS, NB))).then_inc(gate_in, 16)
            for t in range(3):
                r = ROWS[t]
                if t < 2:
                    for out, br in ((io["p_kv_sel"], 1), (io["p_kv_win"], 2)):
                        o = O_KV + br * kv_flat
                        m.store(sp, dram(out, t * P * kv_flat, (kv_flat, P), (1, kv_flat)), m.proj[:, t, o:o + kv_flat])
                else:
                    o = O_KV + kv_flat
                    m.store(sp, dram(io["s_kv_sel"], 0, (kv_flat, NTS), (1, kv_flat)), m.proj[:NTS, 2, o:o + kv_flat])
                    for b in range(NB):
                        m.store(sp, dram(io["s_kv_win"], (b * WIN + WIN - NS) * kv_flat, (kv_flat, NS), (1, kv_flat)),
                                m.proj[b * NS:b * NS + NS, 2, o + kv_flat:o + 2 * kv_flat])
            m.store(sp, dram(io["s_kv_win"], 0, (WIN * kv_flat, NB), (1, (WIN - NS) * kv_flat)),
                    dram(io["cache_kv_win"], NS * kv_flat, (WIN * kv_flat, NB), (1, (WIN - NS) * kv_flat)))
            sp.wait_ge(gate_in, 16 * 3 * NS)


        @block.tensor
        def _(pe):
            def score(i):
                t, h = steps[i]
                p = h // 2
                if i:
                    pe.wait_ge(logits_read, i)
                if i > 1:
                    pe.wait_ge(o_read, i - 1)
                nc_ = NC_P if t else 7
                for g in range(G):
                    q = qz[:, h * G + g, t * P:t * P + P]
                    for br in range(2):
                        pe.matmul(S[:, br * 2 + g // 2, g % 2 * 256:g % 2 * 256 + (t + 1) * P], q,
                                  m.qkT[:, 8 + br * 2 + p, :(t + 1) * P], start=True, stop=True)
                    mm = pe.matmul(X[:, g * 16:g * 16 + nc_], q, m.kc_p[:, p * NC_P:p * NC_P + nc_], start=True, stop=True)
                mm.then_inc(logits, 1)

            pe.wait_ge(q_padded, 1)
            score(0)
            for i, (t, h) in enumerate(steps):
                nc_ = NC_P if t else 7
                if i + 1 < len(steps):
                    score(i + 1)
                pe.wait_ge(probs, i + 1)
                for j, (br, kt) in enumerate(groups(t)):
                    n = first[i] + j
                    if n >= 2:
                        pe.wait_ge(stored, n - 1)
                    for g in range(G):
                        if br:
                            mm = pe.transpose(tps[:, n % 2, g * P:(g + 1) * P], lg[i % 2][:, br - 1, g, kt * P:(kt + 1) * P], m.const("ident"))
                        else:
                            mm = pe.transpose(tps[:nc_, n % 2, g * P:(g + 1) * P], lc[i % 2][:, g, :nc_], m.const("ident"))
                    mm.then_inc(turned, 1)
                pe.wait_ge(stored, first[i + 1])
                if i + 1 < len(steps):
                    pe.wait_ge(logits_read, i + 2)
                if i:
                    pe.wait_ge(o_read, i)
                for g in range(G):
                    pe.matmul(X[:, 256 + g * HD:256 + (g + 1) * HD], pTc[:nc_, g * P:(g + 1) * P],
                              m.vc_p[:nc_, h * HD:(h + 1) * HD], start=True, stop=True)
                    for br in (1, 2):
                        for kt in range(t + 1):
                            v = O_KV + br * kv_flat + h * 2 * HD + HD
                            mm = pe.matmul(O[:, (br - 1) * 256 + g * HD:(br - 1) * 256 + (g + 1) * HD],
                                           pT[:, (br - 1) * 2 + kt, g * P:(g + 1) * P], m.proj[:, kt, v:v + HD],
                                           start=(kt == 0), stop=(kt == t))
                mm.then_inc(pv, 1)

        @block.vector
        def _(dve):
            v = Chain(dve, v_step)
            dve.wait_ge(q_zeroed, 1)
            for hh in range(2):
                rows = slice(hh * HD, hh * HD + HD)
                for p in range(2):
                    c = dve.tensor_copy(qz[rows, (2 * p + hh) * G:(2 * p + hh + 1) * G, :], m.qkT[rows, p * G:(p + 1) * G, :2 * P])
            c.then_inc(q_padded, 1)
            dve.wait_ge(tri_in, 16)

            def logits_and_maxima(i):
                t, h = steps[i]
                nk, nc_ = (t + 1) * P, NC_P if t else 7
                L, Lc = lg[i % 2], lc[i % 2]
                tri = bias_tri[:, h * G, (1 - t) * P:]
                dve.wait_ge(logits, i + 1)
                for br in range(2):
                    v.mark(dve.scalar_tensor_tensor(out=view(L[:, br, 0, :], (2 * P, G), (1, nk)), in0=view(S[:, br * 2, :], (256, G), (1, nk)),
                                                    scalar=SCALE, in1=view(tri, (2 * P, G), (1, nk)), op0=ALU.mult, op1=ALU.add))
                dve.scalar_tensor_tensor(out=Lc[:, :, :nc_], in0=view(X[:], (16, G), (1, nc_)), scalar=SCALE,
                                         in1=view(bias_tri[:, h * G, (1 - t) * P + 31:], (2 * P, G), (16, nc_)),
                                         op0=ALU.mult, op1=ALU.add).then_inc(logits_read, 1)
                v.wait()
                dve.wait_ge(logits_read, i + 1)
                v.mark(dve.tensor_reduce(mx[:, 4:12], view(L[:, 0, 0, :], (2 * P, 2 * G), (1, nk)), AX_X, ALU.max))
                v.link(dve.tensor_reduce(mx[:, 0:4], Lc[:, :, :nc_], AX_X, ALU.max))
                dve.tensor_scalar(nmx[i % 2][:], mx[:], -1.0, None, ALU.mult).then_inc(neg_max, 1)
                dve.wait_ge(neg_max, i + 1)

            logits_and_maxima(0)
            for i, (t, h) in enumerate(steps):
                if i + 1 < len(steps):
                    logits_and_maxima(i + 1)
                v.mark(dve.tensor_scalar(ok[:], nmx[i % 2][:, 0:4], 1e29, None, ALU.is_lt))
                dve.wait_ge(probs, i + 1)
                v.link(dve.reciprocal(rden[:], den[i % 2][:]))
                gates = view(m.proj[:, t, O_GATE + h * G:], (NQ, 3), (1, G))
                v.link(dve.tensor_tensor(view(fac[:], (G, 3), (1, G)), view(rden[:], (G, 3), (1, G)), gates, ALU.mult))
                v.link(dve.tensor_tensor(fac[:, 0:4], fac[:, 0:4], ok[:], ALU.mult))
                dve.wait_ge(pv, i + 1)
                o = m.proj[:, t, O_Q + h * G * HD:O_Q + (h + 1) * G * HD]
                v.mark(dve.tensor_tensor(view(osw[:, 0, :], (HD, 2 * G), (1, HD)), view(O[:], (HD, 2 * G), (1, HD)), view(fac[:, 4:], (1, 2 * G), (0, HD)), ALU.mult))
                v.link(dve.tensor_tensor(view(oc[:], (HD, G), (1, HD)), view(X[:, 256:], (HD, G), (1, HD)), view(fac[:], (1, G), (0, HD)), ALU.mult))
                v.link(dve.tensor_tensor(oc[:], oc[:], osw[:, 0, :], ALU.add))
                dve.tensor_tensor(o, oc[:], osw[:, 1, :], ALU.add).then_inc(o_read, 1)
                dve.wait_ge(o_read, i + 1)
            dve.wait_ge(bias_in, 16 * 3 * NS)
            dve.tensor_copy(m.bias_cmp[:, :NC_S - 7], view(m.bias_win[:, 100:101], (0, NC_S - 7)))
            dve.tensor_tensor(view(m.bias_new[:, 0, :], (NS, NB * NB), (1, NS)), view(m.const("own_seq"), (NS, NB * NB), (1, NS)),
                              view(near[:], (0, NB * NB), (1, NS)), ALU.add)

        @block.gpsimd
        def _(pool):
            pool.memset(qz[:], 0.0).then_inc(q_zeroed, 1)

        @block.scalar
        def _(act):
            def exps(i):
                t, h = steps[i]
                nk, nc_ = (t + 1) * P, NC_P if t else 7
                L, Lc = lg[i % 2], lc[i % 2]
                act.wait_ge(neg_max, i + 1)
                for g in range(G):
                    act.activation(Lc[:, g, :nc_], Lc[:, g, :nc_], ACT.Exp, bias=nmx[i % 2][:, g:g + 1], accum_out=den[i % 2][:, g:g + 1])
                    for br in range(2):
                        c = 4 + br * G + g
                        e = act.activation(L[:, br, g, :nk], L[:, br, g, :nk], ACT.Exp, bias=nmx[i % 2][:, c:c + 1], accum_out=den[i % 2][:, c:c + 1])
                e.then_inc(probs, 1)

            exps(0)
            for i, (t, h) in enumerate(steps):
                nc_ = NC_P if t else 7
                for j, (br, kt) in enumerate(groups(t)):
                    n = first[i] + j
                    act.wait_ge(turned, n + 1)
                    if i:
                        act.wait_ge(pv, i)
                    if br:
                        act.copy(pT[:, (br - 1) * 2 + kt, :], tps[:, n % 2, :]).then_inc(stored, 1)
                    else:
                        act.copy(pTc[:nc_, :], tps[:nc_, n % 2, :]).then_inc(stored, 1)
                if i + 1 < len(steps):
                    exps(i + 1)


SA_NOW = (("w0", "a"), ("w1", "a"))
SA_NEXT = (("wk0", "a"), ("wk1", "a")) + tuple((f"k{n}", "a") for n in range(8))
SA_LAST = (("p0", "v"), ("p1", "a"), ("p2", "v"), ("p3", "a"), ("p4", "v"))
SA_CMP = (("c", "v"),)


class Turned:

    def __init__(self, order, turned0, v0, a0):
        self.at, self.order = {}, order
        self.v0, self.a0 = v0, a0
        done = {"v": v0, "a": a0}
        for i, (name, eng) in enumerate(order):
            done[eng] = done[eng] + 1
            self.at[name] = (i, eng, turned0 + (i + 1), done[eng])

    def bank(self, name):
        return self.at[name][0] % 2

    def turned(self, name):
        return self.at[name][2]

    def wait_stored(self, pe, sems, name):
        i, eng, _, n = self.at[name]
        pe.wait_ge(sems[eng], n)

    def wait_bank(self, pe, sems, name):
        i = self.at[name][0]
        if i >= 2:
            self.wait_stored(pe, sems, self.order[i - 2][0])
        elif self.order is not SA_FIRST:
            pe.wait_ge(sems["v"], self.v0)
            pe.wait_ge(sems["a"], self.a0)


SA_FIRST = tuple((n, "va"[i % 2]) for i, (n, _) in enumerate(SA_NEXT)) + SA_CMP


def sa_first():
    return Turned(SA_FIRST, 0, 0, 0)


def sa_step(b, more):
    order = SA_NOW + (SA_NEXT + SA_LAST + SA_CMP if more else SA_LAST)
    full = SA_NOW + SA_NEXT + SA_LAST + SA_CMP
    n = lambda e, o: sum(x == e for _, x in o)
    return Turned(order, b * len(full) + len(SA_FIRST), b * n("v", full) + n("v", SA_FIRST), b * n("a", full) + n("a", SA_FIRST))


def phase_sample_attention(nc, m, io):
    kv_flat = NKV * 2 * HD
    NK = PAST + NTS
    with ExitStack() as ctx:
        sb = lambda n, sh: ctx.enter_context(nc.sbuf_tensor(n, sh, F32))
        krows, vrows = sb("sel_k_rows", [P, NPG, KVW]), sb("sel_v_rows", [P, NPG, KVW])
        wkrows, wvrows = sb("win_k_rows", [P, 4, KVW]), sb("win_v_rows", [P, 4, KVW])
        kT, wkT = sb("sel_kT", [P, 2, PAST]), sb("win_kT", [P, 2, WIN])
        qb, kcb, gb = sb("q_blocks", [P, 2, 64]), sb("kc_b", [P, 2 * NC_S]), sb("gate_b", [P, 3])
        Ls, Lw, Lc = sb("sel_logits", [P, NK]), sb("win_logits", [P, WIN + NTS]), sb("cmp_logits", [P, NC_S])
        mx, nmx, den, rden, fac = sb("sa_max", [P, 3]), sb("sa_neg_max", [P, 3]), sb("sa_den", [P, 3]), sb("sa_rden", [P, 3]), sb("sa_fac", [P, 3])
        pT, pTw, pTc = sb("sel_pT", [P, (NPG + 1) * P]), sb("win_pT", [P, 5 * P]), sb("cmp_pT", [NC_S, P])
        U, sc, top8 = sb("blk_part", [P, NBLK]), sb("blk_score", [P, NBLK]), sb("blk_top8", [P, 8])
        mask, mb, tail = sb("blk_mask", [P, NBLK]), sb("blk_bias", [P, NBLK]), sb("blk_tail", [P, P])
        osum, oc = sb("sa_out", [P, HD]), sb("sa_cmp_out", [P, HD])
        psm = lambda n, sh: ctx.enter_context(nc.psum_tensor(n, sh, F32))
        tps, S, X, O = psm("sa_tps", [P, 2, 512]), psm("sa_S", [P, 4, 512]), psm("sa_X", [P, 512]), psm("sa_O", [P, 512])
        n_ = lambda n: m.sem("sa_" + n)
        k_in, v_in, wk_in, wv_in = ((n_(x + "_in"), pool_in) for x, pool_in in zip(("sel_k", "sel_v", "win_k", "win_v"), m.pool_in))
        pages_used, wrows_used = n_("pages_used"), n_("wrows_used")
        q_ready, x_ready, turned, stored_v, stored_a = n_("q_ready"), n_("x_ready"), n_("turned"), n_("stored_v"), n_("stored_a")
        win_ready, early_read, neg_c, neg_w, neg_s = n_("win_ready"), n_("early_read"), n_("neg_c"), n_("neg_w"), n_("neg_s")
        exp_c, exp_w, exp_s, pc_ready = n_("exp_c"), n_("exp_w"), n_("exp_s"), n_("pc_ready")
        u_ready, u_stored, score_ready, score_read = n_("u_ready"), n_("u_stored"), n_("score_ready"), n_("score_read")
        oc_ready, oc_read, sel_ready, sel_read, o_ready, o_done, o_out = (n_("oc_ready"), n_("oc_read"), n_("sel_ready"),
                                                                         n_("sel_read"), n_("o_ready"), n_("o_done"), n_("o_out"))
        zeroed, v_step = n_("zeroed"), n_("v_step")
        block = ctx.enter_context(nc.Block())
        stored = {"v": stored_v, "a": stored_a}

        STEP = len(SA_NOW + SA_NEXT + SA_LAST + SA_CMP)
        KEYS_AT = len(SA_NOW + SA_NEXT)

        def load(eng, half, b, kv, wrows, wsem, rows, sem, free=None):
            src = io["cache_kv_win"][bass.ds(b, 1)].rearrange("b l (t p) h k d -> k t p (b l h) d", p=P)[kv]
            if free is not None:
                eng.wait_ge(turned, free - 6)
            for t in range(half, 4, 2):
                eng.dma_start(view(wrows[:, t, :], (HD, NKV), (1, HD)), src[t]).then_inc(wsem[half], 16)
            for j in range(half, NPG, 2):
                if free is not None and j // 2 % 2 == 0 and j > 1:
                    eng.wait_ge(turned, free - 6 + j // 4 * 2)
                r = eng.value_load(m.ptab[0:1, bass.ds(b * NPG + j, 1)], min_val=0, max_val=N_PHYS - 1)
                page = io["cache_kv_sel"][bass.ds(r, 1)].rearrange("n l p h k d -> k p (n l h) d")
                eng.dma_start(view(rows[:, j, :], (HD, NKV), (1, HD)), page[kv]).then_inc(sem[half], 16)

        def load_keys(eng, half, b, free=None):
            load(eng, half, b, 0, wkrows, wk_in, krows, k_in, free)

        def load_values(eng, half, b):
            load(eng, half, b, 1, wvrows, wv_in, vrows, v_in)

        def load_all(eng, half):
            load_keys(eng, half, 0)
            load_values(eng, half, 0)
            load_keys(eng, half, 1, len(SA_NEXT))
            with eng.Fori(1, NB - 1) as b:
                load_keys(eng, half, b + 1, b * STEP + (len(SA_FIRST) - STEP + KEYS_AT))
                eng.wait_ge(pages_used, b)
                load_values(eng, half, b)
            eng.wait_ge(pages_used, NB - 1)
            load_values(eng, half, NB - 1)

        @block.gpsimd
        def _(pool):
            load_all(pool, 1)

        @block.sync
        def _(sp):
            load_all(sp, 0)
            sp.wait_ge(o_out, 16 * NB + 16)
            for b in range(NB):
                sp.dma_start(view(m.proj[b * NS:b * NS + NS, 2, O_Q:], (HD, NQ), (1, HD)),
                             dram(io["o_rows"], b * P * HD, (HD, NS), (NS * HD, NQ), (1, HD))).then_inc(m.o_back, 16)

        @block.tensor
        def _(pe):
            I = m.const("ident")

            def turn(g, name, tiles):
                g.wait_bank(pe, stored, name)
                for c, (src, w) in enumerate(tiles):
                    mm = pe.transpose(tps[:w, g.bank(name), c * P:(c + 1) * P], src, I)
                mm.then_inc(turned, 1)

            def arrived(b, sems, n):
                for sem in sems:
                    pe.wait_ge(sem, b * (16 * n) + 16 * n)

            def turn_keys(b, g):
                arrived(b, wk_in, 2)
                for p in range(2):
                    turn(g, f"wk{p}", [(wkrows[:, t, p * P:(p + 1) * P], P) for t in range(4)])
                arrived(b, k_in, NPG // 2)
                for n in range(8):
                    quad, p = divmod(n, 2)
                    turn(g, f"k{n}", [(krows[:, quad * 4 + t, p * P:(p + 1) * P], P) for t in range(4)])

            def first_logits(b, g):
                pe.wait_ge(q_ready, b + 1)
                for p in range(2):
                    pe.matmul(X[p * 64:p * 64 + 64, 256:256 + NTS], qb[:, p, :], m.qkT[:, 10 + p, 2 * P:], start=True, stop=True)
                for p in range(2):
                    mm = pe.matmul(X[p * 64:p * 64 + 64, :NC_S], qb[:, p, :], kcb[:, p * NC_S:(p + 1) * NC_S], start=True, stop=True)
                mm.then_inc(x_ready, 1)
                g.wait_stored(pe, stored, "wk0")
                g.wait_stored(pe, stored, "wk1")
                for p in range(2):
                    mm = pe.matmul(S[p * 64:p * 64 + 64, 0, :], qb[:, p, :], wkT[:, p, :], start=True, stop=True)
                mm.then_inc(win_ready, 1)

            def compressed(b):
                pe.matmul(X[:, 128:128 + NBLK], pTc[:], m.const("overlap"), start=True, stop=True).then_inc(u_ready, 1)
                pe.wait_ge(early_read, b + 1)
                pe.matmul(S[:, 1, :KVW], pTc[:], m.vc_s[:, bass.ds(b * KVW, KVW)], start=True, stop=True).then_inc(oc_ready, 1)
                pe.wait_ge(u_stored, b + 1)
                pe.matmul(X[:, 192:192 + NBLK], m.const("sum_group"), U[:], start=True, stop=True).then_inc(score_ready, 1)

            def step(b, more, before):
                g = sa_step(b, more)
                before(b)
                for c in (0, 2, 3, 1):
                    if c == 1:
                        pe.wait_ge(oc_read, b + 1)
                    for p in range(2):
                        mm = pe.matmul(S[p * 64:p * 64 + 64, c, :], qb[:, p, :], kT[:, p, c * 512:(c + 1) * 512], start=True, stop=True)
                    mm.then_inc(sel_ready, 1)
                pe.wait_ge(score_read, b + 1)
                for p in range(2):
                    mm = pe.matmul(X[p * 64:p * 64 + 64, 320:320 + NTS], qb[:, p, :], m.qkT[:, 8 + p, 2 * P:], start=True, stop=True)
                mm.then_inc(sel_ready, 1)
                new_v = lambda br: view(m.proj[:NTS, 2, O_KV + br * kv_flat + HD:], (2 * HD, NKV), (1, HD))
                pe.wait_ge(exp_w, b + 1)
                turn(g, "w0", [(Lw[:, t * P:t * P + P], P) for t in range(3)])
                turn(g, "w1", [(Lw[:, 3 * P:4 * P], P), (Lw[:, 4 * P:4 * P + NTS], NTS)])
                arrived(b, wv_in, 2)
                g.wait_stored(pe, stored, "w1")
                pe.wait_ge(o_done, b + 1)
                for t in range(4):
                    pe.matmul(O[:, KVW:], pTw[:, t * P:(t + 1) * P], wvrows[:, t, :], start=(t == 0), stop=False)
                pe.matmul(O[:, KVW:], pTw[:NTS, 4 * P:], new_v(2), start=False, stop=True).then_inc(wrows_used, 1)
                if more:
                    turn_keys(b + 1, g)
                    pe.wait_ge(sel_read, b + 1)
                    first_logits(b + 1, g)
                pe.wait_ge(exp_s, b + 1)
                for n, (lo, hi) in enumerate(((0, 4), (4, 8), (8, 12), (12, 15), (15, 17))):
                    turn(g, f"p{n}", [(Ls[:, t * P:t * P + w], w) for t, w in ((t, P if t < NPG else NTS) for t in range(lo, hi))])
                if more:
                    pe.wait_ge(pc_ready, b + 2)
                    turn(g, "c", [(Lc[:], NC_S)])
                arrived(b, v_in, NPG // 2)
                g.wait_stored(pe, stored, "p4")
                g.wait_stored(pe, stored, "p3")
                for t in range(NPG):
                    mm = pe.matmul(O[:, :KVW], pT[:, t * P:(t + 1) * P], vrows[:, t, :], start=(t == 0), stop=False)
                mm.then_inc(pages_used, 1)
                pe.matmul(O[:, :KVW], pT[:NTS, NPG * P:], new_v(1), start=False, stop=True).then_inc(o_ready, 1)
                if more:
                    g.wait_stored(pe, stored, "c")
                    compressed(b + 1)

            def keys_stored(b):
                g = sa_step(b, True)
                pe.wait_ge(stored_v, g.v0)
                pe.wait_ge(stored_a, g.a0)

            g = sa_first()
            turn_keys(0, g)
            first_logits(0, g)
            pe.wait_ge(pc_ready, 1)
            turn(g, "c", [(Lc[:], NC_S)])
            g.wait_stored(pe, stored, "c")
            compressed(0)
            with pe.Fori(0, NB - 1) as b:
                step(b, True, keys_stored)
            step(NB - 1, False, keys_stored)

        def copy_turned(eng, copy, g, name):
            _, e, n, _ = g.at[name]
            src = tps[:, g.bank(name), :]
            if name == "c":
                pairs = [(pTc[:], src[:NC_S, :P])]
            elif name == "w0":
                pairs = [(pTw[:, :3 * P], src[:, :3 * P])]
            elif name == "w1":
                pairs = [(pTw[:, 3 * P:4 * P], src[:, :P]), (pTw[:NTS, 4 * P:], src[:NTS, P:2 * P])]
            elif name[:2] == "wk":
                pairs = [(wkT[:, int(name[2]), :], src)]
            elif name[0] == "k":
                quad, p = divmod(int(name[1]), 2)
                pairs = [(kT[:, p, quad * 512:(quad + 1) * 512], src)]
            elif name == "p4":
                pairs = [(pT[:, 15 * P:16 * P], src[:, :P]), (pT[:NTS, 16 * P:], src[:NTS, P:2 * P])]
            else:
                lo, w = int(name[1]) * 4, 3 if name == "p3" else 4
                pairs = [(pT[:, lo * P:(lo + w) * P], src[:, :w * P])]
            eng.wait_ge(turned, n)
            for dst, s_ in pairs:
                c = copy(dst, s_)
            c.then_inc(stored[e], 1)

        def copy_mine(eng, copy, g, names, mine):
            for name, e in names:
                if e == mine:
                    copy_turned(eng, copy, g, name)

        @block.vector
        def _(dve):
            def set_q(b):
                for hh in range(2):
                    r0 = hh * HD
                    dve.tensor_copy(view(qb[r0:r0 + HD, 0, hh * 32:], (64, 2), (NS, G), (1, NS)),
                                         view(m.qkT[r0:r0 + HD, 0, bass.ds(b * NS + 2 * P, NS)], (G * T, 2), (T, G), (1, NS)))
                dve.tensor_copy(kcb[:], m.kc_s[:, bass.ds(b * (2 * NC_S), 2 * NC_S)]).then_inc(q_ready, 1)

            def first_softmaxes(b, v):
                dve.wait_ge(x_ready, b + 1)
                v.mark(dve.scalar_tensor_tensor(out=Lc[:], in0=X[:, :NC_S], scalar=SCALE, in1=m.bias_cmp[:], op0=ALU.mult, op1=ALU.add))
                dve.wait_ge(x_ready, b + 1)
                v.link(dve.scalar_tensor_tensor(out=Lw[:, WIN:], in0=X[:, 256:256 + NTS], scalar=SCALE,
                                                in1=m.bias_new[:, bass.ds(b, 1), :].rearrange("p a b -> p (a b)"), op0=ALU.mult, op1=ALU.add))
                v.link(dve.tensor_reduce(mx[:, 0:1], Lc[:], AX_X, ALU.max))
                dve.tensor_scalar(nmx[:, 0:1], mx[:, 0:1], -1.0, None, ALU.mult).then_inc(neg_c, 1)
                dve.wait_ge(win_ready, b + 1)
                dve.scalar_tensor_tensor(out=Lw[:, :WIN], in0=S[:, 0, :], scalar=SCALE, in1=m.bias_win[:], op0=ALU.mult, op1=ALU.add).then_inc(early_read, 1)
                dve.wait_ge(early_read, b + 1)
                v.link(dve.tensor_reduce(mx[:, 1:2], Lw[:], AX_X, ALU.max))
                dve.tensor_scalar(nmx[:, 1:2], mx[:, 1:2], -1.0, None, ALU.mult).then_inc(neg_w, 1)

            def compressed_probs(b, v, g):
                v.mark(dve.tensor_copy(gb[:, 0:1], m.gate_s[:, 0, bass.ds(b, 1)]))
                dve.wait_ge(exp_c, b + 1)
                v.link(dve.reciprocal(rden[:, 0:1], den[:, 0:1]))
                dve.tensor_scalar(Lc[:], Lc[:], rden[:, 0:1], None, ALU.mult).then_inc(pc_ready, 1)
                copy_turned(dve, dve.tensor_copy, g, "c")

            def block_parts(b):
                dve.wait_ge(u_ready, b + 1)
                dve.tensor_copy(U[:], X[:, 128:128 + NBLK]).then_inc(u_stored, 1)

            def compressed_output(b):
                dve.wait_ge(oc_ready, b + 1)
                for h in range(NKV):
                    r = slice(h * 32, h * 32 + 32)
                    cp = dve.tensor_scalar(oc[r, :], S[r, 1, h * HD:(h + 1) * HD], gb[r, 0:1], None, ALU.mult)
                cp.then_inc(oc_read, 1)

            def step(b, more):
                v = Chain(dve, v_step, b * m.SA_V + V0)
                g = sa_step(b, more)
                v.mark(dve.tensor_copy(gb[:, 1:3], view(m.gate_s[:, 1, bass.ds(b, 1)], (NB, 2))))
                dve.wait_ge(exp_w, b + 1)
                v.link(dve.reciprocal(rden[:, 1:2], den[:, 1:2]))
                dve.wait_ge(score_ready, b + 1)
                dve.tensor_tensor(sc[:], X[:, 192:192 + NBLK], m.const("sel_keep"), ALU.mult).then_inc(score_read, 1)
                dve.wait_ge(score_read, b + 1)
                v.link(dve.tensor_tensor(sc[:], sc[:], m.const("sel_force"), ALU.add))
                for _ in range(TOPK // 8):
                    dve.nop(nofuse=True)
                    v.link(dve.max(top8[:], sc[:]))
                    dve.nop(nofuse=True)
                    v.link(dve.match_replace(sc[:], top8[:], sc[:], NEG))
                v.link(dve.tensor_scalar(mask[:], sc[:], NEG / 10, NEG, ALU.is_gt, ALU.mult))
                v.mark(dve.tensor_scalar(mb[:], mask[:], m.bias_win[:, 100:101], None, ALU.add))
                v.link(dve.tensor_tensor(view(tail[:], (SELB, 2), (1, SELB)), view(m.bias_win[:, WIN - P:], (SELB, 2), (1, SELB)),
                                         view(mask[:, NBLK - 3:], (1, 2), (0, SELB)), ALU.add))
                for i, c in enumerate((0, 2, 3, 1)):
                    dve.wait_ge(sel_ready, b * 5 + (i + 1))
                    w = 8 if c < 3 else 6
                    ins = dve.scalar_tensor_tensor(out=view(Ls[:, c * 512:], (SELB, w), (1, SELB)), in0=view(S[:, c, :], (SELB, w), (1, SELB)), scalar=SCALE,
                                                   in1=view(mb[:, c * 8:], (1, w), (0, SELB)), op0=ALU.mult, op1=ALU.add)
                    v.mark(ins)
                v.mark(dve.scalar_tensor_tensor(out=Ls[:, PAST - P:PAST], in0=S[:, 3, 384:], scalar=SCALE, in1=tail[:], op0=ALU.mult, op1=ALU.add))
                dve.wait_ge(sel_ready, b * 5 + 5)
                dve.scalar_tensor_tensor(out=Ls[:, PAST:], in0=X[:, 320:320 + NTS], scalar=SCALE,
                                         in1=m.bias_new[:, bass.ds(b, 1), :].rearrange("p a b -> p (a b)"), op0=ALU.mult, op1=ALU.add).then_inc(sel_read, 1)
                v.wait()
                dve.wait_ge(sel_read, b + 1)
                v.link(dve.tensor_reduce(mx[:, 2:3], Ls[:], AX_X, ALU.max))
                dve.tensor_scalar(nmx[:, 2:3], mx[:, 2:3], -1.0, None, ALU.mult).then_inc(neg_s, 1)
                if more:
                    set_q(b + 1)
                    first_softmaxes(b + 1, v)
                copy_mine(dve, dve.tensor_copy, g, SA_LAST, "v")
                if more:
                    compressed_probs(b + 1, v, g)
                dve.wait_ge(exp_s, b + 1)
                v.link(dve.reciprocal(rden[:, 2:3], den[:, 2:3]))
                v.mark(dve.tensor_tensor(fac[:, 1:2], rden[:, 1:2], gb[:, 2:3], ALU.mult))
                v.link(dve.tensor_tensor(fac[:, 2:3], rden[:, 2:3], gb[:, 1:2], ALU.mult))
                if more:
                    block_parts(b + 1)
                dve.wait_ge(o_ready, b + 1)
                dve.wait_ge(oc_read, b + 1)
                dve.wait_ge(o_out, b * 16 + 16)
                for part, col, before in ((2, 1, oc), (1, 2, osum)):
                    for h in range(NKV):
                        r = slice(h * 32, h * 32 + 32)
                        c0 = (KVW if part == 2 else 0) + h * HD
                        ins = dve.scalar_tensor_tensor(out=osum[r, :], in0=O[r, c0:c0 + HD], scalar=fac[r, col:col + 1], in1=before[r, :], op0=ALU.mult, op1=ALU.add)
                        if part == 1 and h == NKV - 1:
                            ins.then_inc(o_done, 1)
                        else:
                            v.mark(ins)
                    if part == 2:
                        v.wait()
                dve.wait_ge(o_done, b + 2)
                if more:
                    compressed_output(b + 1)
                return v.n

            dve.sem_inc(o_done, 1)
            dve.memset(qb[:], 0.0).then_inc(zeroed, 1)
            dve.wait_ge(zeroed, 1)
            V0 = 6
            v = Chain(dve, v_step)
            set_q(0)
            g = sa_first()
            copy_mine(dve, dve.tensor_copy, g, SA_FIRST[:len(SA_NEXT)], "v")
            first_softmaxes(0, v)
            compressed_probs(0, v, g)
            block_parts(0)
            compressed_output(0)
            assert v.n == V0, v.n
            with dve.Fori(0, NB - 1) as b:
                n = step(b, True)
            assert n == m.SA_V, n
            step(NB - 1, False)

        @block.scalar
        def _(act):
            def first_exps(b):
                act.wait_ge(neg_c, b + 1)
                act.activation(Lc[:], Lc[:], ACT.Exp, bias=nmx[:, 0:1], accum_out=den[:, 0:1]).then_inc(exp_c, 1)
                act.wait_ge(neg_w, b + 1)
                act.activation(Lw[:], Lw[:], ACT.Exp, bias=nmx[:, 1:2], accum_out=den[:, 1:2]).then_inc(exp_w, 1)

            def store_o(b):
                act.wait_ge(o_done, b + 2)
                act.dma_start(io["o_rows"][bass.ds(b, 1)].rearrange("b p d -> p (b d)"), osum[:]).then_inc(o_out, 16)

            def step(b, more):
                g = sa_step(b, more)
                copy_mine(act, act.copy, g, SA_NOW + (SA_NEXT if more else ()), "a")
                act.wait_ge(neg_s, b + 1)
                act.activation(Ls[:], Ls[:], ACT.Exp, bias=nmx[:, 2:3], accum_out=den[:, 2:3]).then_inc(exp_s, 1)
                if more:
                    first_exps(b + 1)
                copy_mine(act, act.copy, g, SA_LAST, "a")
                store_o(b)

            act.sem_inc(o_out, 16)
            copy_mine(act, act.copy, sa_first(), SA_FIRST, "a")
            first_exps(0)
            with act.Fori(0, NB - 1) as b:
                step(b, True)
            step(NB - 1, False)


TWO_PI_HI = 6.28125
TWO_PI_LO = float(2 * np.pi - 6.28125)
ROUND = 12582912.0
SG, SN, SC = 32, 64, 16
ST = SG * SN // P
CH = 16


def late_inputs(nc, m, scope):
    sb = lambda n, sh: scope.enter_context(nc.sbuf_tensor(n, sh, F32))
    m.s5_ldt, m.s5_b, m.s5_c = sb("s5_dt", [P, ST]), sb("s5_b", [P, 2, ST, SC]), sb("s5_c", [P, 2, 4, SN])
    m.s5_h0, m.s5_glu = sb("s5_h0rows", [P, 2, P]), sb("s5_glu_w", [P, 4, 512])
    m.gm_w, m.gm_gain = sb("gm_w", [P, 4, P]), sb("gm_gain", [P, 512])


def load_late_inputs(sp, m, io):
    for par in range(2):
        sp.dma_start(m.s5_ldt[par * SN:(par + 1) * SN, :], dram(io["ssm_log_dt"], par, (0, SN), (2, ST))).then_inc(m.s5_in, 16)
    for ri, src in enumerate((io["ssm_b_re"], io["ssm_b_im"])):
        sp.dma_start(m.s5_b[:, ri], dram(src, 0, (SC, P), (P * SC, ST), (1, SC))).then_inc(m.s5_in, 16)
    for ri, src in enumerate((io["ssm_c_re"], io["ssm_c_im"])):
        sp.dma_start(m.s5_c[:, ri], dram(src, 0, (SN, P), (P * SN, 4), (1, SN))).then_inc(m.s5_in, 16)
    for ri, src in enumerate((io["state_ssm_re"], io["state_ssm_im"])):
        sp.dma_start(m.s5_h0[:, ri, :], dram(src, 0, (P, P), (1, P))).then_inc(m.s5_in, 16)
    sp.dma_start(m.s5_glu[:], dram(io["ssm_glu_w"], 0, (512, P), (P * 512, 4), (1, 512))).then_inc(m.s5_in, 16)
    sp.dma_start(m.gm_w[:], dram(io["gmlp_ws"], 0, (P, P), (P * P, 4), (1, P))).then_inc(m.gm_in, 16)
    sp.dma_start(m.gm_gain[:], dram(io["gmlp_norm"], 0, (0, P), (1, 512))).then_inc(m.gm_in, 16)


def phase_s5(nc, m, io):
    with ExitStack() as ctx:
        sb = lambda n, sh: ctx.enter_context(nc.sbuf_tensor(n, sh, F32))
        ldt, braw, craw, h0r, glu, in_done = m.s5_ldt, m.s5_b, m.s5_c, m.s5_h0, m.s5_glu, m.s5_in
        A = sb("s5_small", [P, 16, ST])
        bb, bx = sb("s5_bb", [P, 3, ST, SC]), sb("s5_bx", [P, 2, ST, 2, SC])
        cx = sb("s5_cx", [P, 2, 4, 2, SN])
        BT, CT = sb("s5_BT", [P, 2, ST, P]), sb("s5_CT", [P, 2, 4, P])
        uT, H = sb("s5_uT", [P, 4, T]), sb("s5_H", [P, 2, ST, T])
        h0 = sb("s5_h0", [P, 2, NB, ST])
        a2, ai2 = sb("s5_a_re", [P, 2, ST]), sb("s5_a_im_signed", [P, 2, ST])
        t1, t2 = sb("s5_t1", [P, 2, ST, CH]), sb("s5_t2", [P, 2, ST, CH])
        q1, q2 = sb("s5_q1", [P, 2, ST, NB]), sb("s5_q2", [P, 2, ST, NB])
        pw, carry = sb("s5_powers", [P, 2, ST, CH]), sb("s5_carry", [P, 2, ST, CH])
        fx = sb("s5_fix", [P, 2, 4, (CH - 1) * CH])
        DVE_TILES, POOL_TILES = (0, 12), (12, 4)
        endp, ends, endrow = sb("s5_end_p", [P, 2, ST]), sb("s5_end_s", [P, 2, NB, ST]), sb("s5_end_rows", [P, 3, P])
        y, yg, sg = sb("s5_y", [P, 4, T]), sb("s5_yg", [P, 4, T]), sb("s5_sig", [P, 4, T])
        tps = ctx.enter_context(nc.psum_tensor("s5_tps", [P, 4, 512], F32))
        yps = ctx.enter_context(nc.psum_tensor("s5_yps", [P, 4, 512], F32))
        n_ = lambda n: m.sem("s5_" + n)
        v_step, a_dt, v_arg, a_sin = n_("v_step"), n_("dt"), n_("arg"), n_("sin")
        bx_ready, turned, stored, x_made, x_stored = n_("bx_ready"), n_("turned"), n_("stored"), n_("x_made"), (n_("x_stored_v"), n_("x_stored_a"))
        init, pool_step, p_done, s_done = n_("sample_ready"), n_("pool_step"), n_("prompt_done"), n_("sample_done")
        y_made, y_ready, gelu, z_made, sig, sq_ready = n_("y_made"), n_("y_ready"), n_("gelu"), n_("z_made"), n_("sig"), n_("sq_ready")
        n_ready, n_high, pool_prompt, carried, zeroed = n_("norm_ready"), n_("norm_high"), n_("pool_prompt"), n_("carried"), n_("zeroed")
        sum_made, rms, ends_ready, ends_turned, ends_stored = n_("sum_made"), n_("rms"), n_("ends_ready"), n_("ends_turned"), n_("ends_stored")
        block = ctx.enter_context(nc.Block())
        AR, AI = m.feat[:, FEAT_AT["ssm_a_re"][0]:][:, :ST], m.feat[:, FEAT_AT["ssm_a_im"][0]:][:, :ST]

        @block.sync
        def _(sp):
            sp.wait_ge(ends_stored, 3)
            m.store(sp, dram(io["s_ssm_re"], 0, (P, P), (1, P)), endrow[:, 0, :])
            m.store(sp, dram(io["s_ssm_im"], 0, (P, P), (1, P)), endrow[:, 1, :])
            m.store(sp, dram(io["p_ssm_re"], 0, (P, ST), (1, P)), endrow[:ST, 2, :])
            m.store(sp, dram(io["p_ssm_im"], 0, (P, ST), (1, P)), endrow[ST:2 * ST, 2, :])

        N_IN = 16 * 9
        @block.tensor
        def _(pe):
            pe.wait_ge(in_done, N_IN)
            I = m.const("ident")
            n = 0
            for t in range(3):
                if n >= 4:
                    pe.wait_ge(stored, n - 3)
                for k in range(4):
                    mm = pe.transpose(tps[:, n % 4, k * P:k * P + ROWS[t]], m.proj[:ROWS[t], t, O_U + k * P:O_U + (k + 1) * P], I[:ROWS[t], :ROWS[t]])
                mm.then_inc(turned, 1)
                n += 1
            for ri in range(2):
                mm = pe.transpose(tps[:, 3, ri * P:(ri + 1) * P], h0r[:, ri, :], I)
            mm.then_inc(turned, 1)
            pe.wait_ge(bx_ready, 2)
            for n, (src, ri) in enumerate(((bx, 0), (bx, 1), (cx, 0), (cx, 1)), 4):
                pe.wait_ge(stored, n - 3)
                for k in range(4):
                    w = view(src[:, ri, 4 * k, 0, :] if src is bx else src[:, ri, k, 0, :], (1, P))
                    mm = pe.transpose(tps[:, n % 4, k * P:(k + 1) * P], w, I)
                mm.then_inc(turned, 1)
            pe.wait_ge(stored, 8)
            for j in range(2 * ST):
                ri, i = divmod(j, ST)
                if j >= 4:
                    pe.wait_ge(x_stored[j % 2], j // 2 - 1)
                pe.matmul(tps[:, j % 4, :T], BT[:, ri, i, :], uT[:, i // 4, :], start=True, stop=True).then_inc(x_made, 1)
            pe.wait_ge(p_done, 2)
            pe.wait_ge(s_done, 1)
            for i in range(ST):
                r0 = i % 4 * 32
                for ri in range(2):
                    mm = pe.matmul(yps[r0:r0 + 32, i // 4, :T], CT[:, ri, i // 4, r0:r0 + 32], H[:, ri, i, :], start=(ri == 0), stop=(ri == 1))
                if i % 4 == 3:
                    mm.then_inc(y_made, 1)
            pe.wait_ge(ends_ready, 1)
            for sem in x_stored:
                pe.wait_ge(sem, ST)
            for ri in range(2):
                pe.transpose(tps[:, ri, :P], view(ends[:, ri, 0, :], (1, P)), I).then_inc(ends_turned, 1)
            pe.transpose(tps[:2 * ST, 2, :P], view(endp[:, 0, :], (1, 2 * ST)), I).then_inc(ends_turned, 1)
            pe.wait_ge(y_ready, 4)
            pe.wait_ge(gelu, 4)
            for mo in range(4):
                for k in range(4):
                    mm = pe.matmul(yps[:, mo, :T], glu[:, k, mo * P:(mo + 1) * P], yg[:, k, :], start=(k == 0), stop=(k == 3))
                mm.then_inc(z_made, 1)
            pe.wait_ge(ends_stored, 3)
            pe.wait_ge(sq_ready, 4)
            for mo in range(4):
                mm = pe.matmul(tps[:, 3, :T], m.const("ones"), y[:, mo, :], start=(mo == 0), stop=(mo == 3))
            mm.then_inc(sum_made, 1)

        @block.scalar
        def _(act):
            act.wait_ge(in_done, N_IN)
            act.activation(ldt[:], ldt[:], ACT.Exp).then_inc(a_dt, 1)
            act.wait_ge(v_arg, 1)
            act.activation(A[:, 0, :], A[:, 0, :], ACT.Exp).then_inc(a_dt, 1)
            act.wait_ge(v_arg, 2)
            act.activation(view(A[:, 3, :], (1, 2 * ST)), view(A[:, 1, :], (1, 2 * ST)), ACT.Sin).then_inc(a_sin, 1)
            for j in range(1, 2 * ST, 2):
                ri, i = divmod(j, ST)
                act.wait_ge(x_made, j + 1)
                act.copy(H[:, ri, i, :], tps[:, j % 4, :T]).then_inc(x_stored[1], 1)
            for k in range(4):
                act.wait_ge(y_ready, k + 1)
                act.activation(yg[:, k, :], y[:, k, :], ACT.Gelu_apprx_tanh).then_inc(gelu, 1)
            gb = FEAT_AT["ssm_glu_b"][0]
            for mo in range(4):
                act.wait_ge(z_made, mo + 1)
                act.activation(sg[:, mo, :], yps[:, mo, :T], ACT.Sigmoid, bias=m.feat[:, gb + mo:gb + mo + 1]).then_inc(sig, 1)
            act.wait_ge(sum_made, 1)
            act.activation(sg[:, 0, :], tps[:, 3, :T], ACT.Sqrt, bias=m.eps[:], scale=1.0 / 512).then_inc(rms, 1)
            for mo in range(4):
                act.wait_ge(n_ready, mo + 1)
                split_high(act.copy, m.ssmTh[:, mo, :], y[:, mo, :]).then_inc(n_high, 1)

        def recur(eng, ch, cur, prev, w, sa, sb_, tiles):
            i0, n = tiles
            ar = view(a2[:, 0, i0:], (ST, 2), (1, n), (0, w))
            ai = view(ai2[:, 0, i0:], (ST, 2), (1, n), (0, w))
            sa, sb_ = sa[:, :, i0:i0 + n, :], sb_[:, :, i0:i0 + n, :]
            ch.mark(eng.tensor_tensor(sa, prev, ar, ALU.mult))
            ch.mark(eng.tensor_tensor(sb_, prev, ai, ALU.mult))
            ch.wait()
            ch.link(eng.tensor_tensor(cur, cur, sa, ALU.add))
            for ri in range(2):
                c = view(cur[:, ri], *cur.ap[2:])
                ch.mark(eng.tensor_tensor(c, c, sb_[:, 1 - ri], ALU.add))
            ch.wait()

        def at_p(j, tiles):
            return view(H[:, 0, tiles[0], j:], (ST * T, 2), (T, tiles[1]), (CH, CH))

        def at_s(j):
            return view(H[:, 0, 0, 2 * P + j:], (ST * T, 2), (T, ST), (NS, NB))

        def fix(eng, ch, f, qi):
            N, i0 = CH - 1, qi * 4
            pv_ = [view(pw[:, ri, i0, :], (CH, 4), (0, N), (1, CH)) for ri in range(2)]
            cv = [view(carry[:, ri, i0, :], (CH, 4), (1, N), (0, CH)) for ri in range(2)]
            hv = [view(H[:, ri, i0, CH:], (T, 4), (CH, N), (1, CH)) for ri in range(2)]
            f = [view(f[:, ri, 0, :], (N * CH, 4), (CH, N), (1, CH)) for ri in range(2)]
            for ri in range(2):
                ch.mark(eng.tensor_tensor(f[0], pv_[0], cv[ri], ALU.mult))
                ch.link(eng.tensor_tensor(f[1], pv_[1], cv[1 - ri], ALU.mult))
                ch.link(eng.tensor_tensor(hv[ri], hv[ri], f[0], ALU.add))
                ch.link(eng.tensor_tensor(hv[ri], hv[ri], f[1], (ALU.subtract, ALU.add)[ri]))

        @block.gpsimd
        def _(pool):
            c = Chain(pool, pool_step)
            pool.memset(BT[:], 0.0).then_inc(zeroed, 1)
            pool.wait_ge(init, 1)
            for j in range(1, CH):
                recur(pool, c, at_p(j, POOL_TILES), at_p(j - 1, POOL_TILES), CH, t1, t2, POOL_TILES)
            pool.sem_inc(pool_prompt, 1)
            for j in range(1, NS):
                recur(pool, c, at_s(j), at_s(j - 1), NB, q1, q2, (0, ST))
            c.link(pool.tensor_copy(ends[:], view(H[:, 0, 0, 2 * P + NS - 1:], (ST * T, 2), (NS, NB), (T, ST))))
            pool.wait_ge(carried, 1)
            fix(pool, c, BT, 3)
            pool.sem_inc(s_done, 1)

        @block.vector
        def _(dve):
            v = Chain(dve, v_step)
            tt, ts = dve.tensor_tensor, dve.tensor_scalar
            dve.wait_ge(a_dt, 1)
            v.mark(tt(A[:, 6, :], ldt[:], AI, ALU.mult))
            tt(A[:, 0, :], ldt[:], AR, ALU.mult).then_inc(v_arg, 1)
            v.wait()
            v.link(ts(A[:, 7, :], A[:, 6, :], 1.0 / (2 * np.pi), None, ALU.mult))
            v.link(ts(A[:, 7, :], A[:, 7, :], ROUND, None, ALU.add))
            v.link(ts(A[:, 7, :], A[:, 7, :], ROUND, None, ALU.subtract))
            v.link(dve.scalar_tensor_tensor(out=A[:, 6, :], in0=A[:, 7, :], scalar=-TWO_PI_HI, in1=A[:, 6, :], op0=ALU.mult, op1=ALU.add))
            v.link(dve.scalar_tensor_tensor(out=A[:, 6, :], in0=A[:, 7, :], scalar=-TWO_PI_LO, in1=A[:, 6, :], op0=ALU.mult, op1=ALU.add))
            v.link(ts(A[:, 2, :], A[:, 6, :], 3.1415925, -3.1415925, ALU.min, ALU.max))
            v.link(dve.scalar_tensor_tensor(out=A[:, 7, :], in0=A[:, 2, :], scalar=-1.0, in1=A[:, 2, :], op0=ALU.mult, op1=ALU.min))
            ts(A[:, 1, :], A[:, 7, :], float(np.pi / 2), None, ALU.add).then_inc(v_arg, 1)
            v.mark(tt(A[:, 8, :], AR, AR, ALU.mult))
            v.link(tt(A[:, 9, :], AI, AI, ALU.mult))
            v.link(tt(A[:, 8, :], A[:, 8, :], A[:, 9, :], ALU.add))
            v.link(dve.reciprocal(A[:, 9, :], A[:, 8, :]))
            dve.wait_ge(a_dt, 2)
            dve.wait_ge(a_sin, 1)
            v.mark(tt(a2[:, 0, :], A[:, 0, :], A[:, 3, :], ALU.mult))
            v.mark(tt(a2[:, 1, :], A[:, 0, :], A[:, 3, :], ALU.mult))
            v.link(tt(ai2[:, 0, :], A[:, 0, :], A[:, 4, :], ALU.mult))
            v.mark(ts(ai2[:, 1, :], ai2[:, 0, :], -1.0, None, ALU.mult))
            v.link(ts(A[:, 5, :], a2[:, 0, :], -1.0, None, ALU.add))
            v.mark(tt(A[:, 10, :], A[:, 5, :], AR, ALU.mult))
            v.mark(tt(A[:, 11, :], ai2[:, 0, :], AI, ALU.mult))
            v.mark(tt(A[:, 12, :], ai2[:, 0, :], AR, ALU.mult))
            v.link(tt(A[:, 13, :], A[:, 5, :], AI, ALU.mult))
            v.mark(tt(A[:, 10, :], A[:, 10, :], A[:, 11, :], ALU.add))
            v.link(tt(A[:, 12, :], A[:, 12, :], A[:, 13, :], ALU.subtract))
            v.mark(tt(A[:, 10, :], A[:, 10, :], A[:, 9, :], ALU.mult))
            v.link(tt(A[:, 12, :], A[:, 12, :], A[:, 9, :], ALU.mult))
            fr, fi = (view(A[:, x, :], (1, ST), (0, SC)) for x in (10, 12))
            v.mark(tt(bb[:, 0], braw[:, 0], fr, ALU.mult))
            v.mark(tt(bb[:, 1], braw[:, 1], fr, ALU.mult))
            v.link(tt(bb[:, 2], braw[:, 1], fi, ALU.mult))
            v.link(tt(bb[:, 0], bb[:, 0], bb[:, 2], ALU.subtract))
            v.link(tt(bb[:, 2], braw[:, 0], fi, ALU.mult))
            v.link(tt(bb[:, 1], bb[:, 1], bb[:, 2], ALU.add))
            for ri in range(2):
                for par in range(2):
                    last = ts(bx[:, ri, :, par, :], bb[:, ri], m.const("low_half")[:, par:par + 1], None, ALU.mult)
            last.then_inc(bx_ready, 1)
            for ri in range(2):
                for par in range(2):
                    last = ts(cx[:, ri, :, par, :], craw[:, ri], m.const("even_group")[:, par:par + 1], (1.0, -1.0)[ri], ALU.mult, ALU.mult)
            last.then_inc(bx_ready, 1)
            for n in range(8):
                dve.wait_ge(turned, n + 1)
                if n < 3:
                    c = dve.tensor_copy(uT[:, :, n * P:n * P + ROWS[n]], view(tps[:, n, :], (P, 4), (1, ROWS[n])))
                elif n == 3:
                    c = dve.tensor_copy(view(h0[:, 0, 0, :], (1, 2 * P)), tps[:, 3, :2 * P])
                elif n < 6:
                    if n == 4:
                        dve.wait_ge(zeroed, 1)
                    for r in range(4):
                        rows = slice(r * 32, r * 32 + 32)
                        c = dve.tensor_copy(view(BT[rows, n % 2, r, :], (4 * P, 4), (1, P)), view(tps[rows, n % 4, :], (P, 4), (1, P)))
                else:
                    c = dve.tensor_copy(view(CT[:, n % 2, 0, :], (1, 512)), tps[:, n % 4, :])
                c.then_inc(stored, 1)
            v.mark(dve.tensor_copy(pw[:, 0, :, 0], a2[:, 0, :]))
            v.link(dve.tensor_copy(pw[:, 1, :, 0], ai2[:, 0, :]))
            w = 1
            while w < CH:
                lo = [pw[:, ri, :, :w] for ri in range(2)]
                top = [view(pw[:, ri, 0, w - 1:w], (CH, ST), (0, w)) for ri in range(2)]
                tmp = [t1[:, ri, :, :w] for ri in range(2)]
                new = [pw[:, ri, :, w:2 * w] for ri in range(2)]
                v.mark(tt(new[0], lo[0], top[0], ALU.mult))
                v.mark(tt(tmp[0], lo[1], top[1], ALU.mult))
                v.mark(tt(new[1], lo[0], top[1], ALU.mult))
                v.link(tt(tmp[1], lo[1], top[0], ALU.mult))
                v.mark(tt(new[0], new[0], tmp[0], ALU.subtract))
                v.link(tt(new[1], new[1], tmp[1], ALU.add))
                w *= 2
            for j in range(0, 2 * ST, 2):
                ri, i = divmod(j, ST)
                dve.wait_ge(x_made, j + 1)
                dve.tensor_copy(H[:, ri, i, :], tps[:, j % 4, :T]).then_inc(x_stored[0], 1)
            for sem in x_stored:
                dve.wait_ge(sem, ST)
            h0v = view(h0[:, 0, 0, :], (P, 2), (1, ST), (ST, NB))
            v.mark(tt(q1[:], h0v, view(a2[:, 0, :], (ST, 2), (1, ST), (0, NB)), ALU.mult))
            v.link(tt(q2[:], h0v, view(ai2[:, 0, :], (ST, 2), (1, ST), (0, NB)), ALU.mult))
            v.link(tt(at_s(0), at_s(0), q1[:], ALU.add))
            for ri in range(2):
                c = view(H[:, ri, 0, 2 * P:], (T, ST), (NS, NB))
                v.mark(tt(c, c, q2[:, 1 - ri], ALU.add))
            v.wait()
            dve.sem_inc(init, 1)
            for j in range(1, CH):
                recur(dve, v, at_p(j, DVE_TILES), at_p(j - 1, DVE_TILES), CH, t1, t2, DVE_TILES)
            dve.wait_ge(pool_prompt, 1)
            v.link(dve.tensor_copy(carry[:], at_p(CH - 1, (0, ST))))
            p16 = [view(pw[:, ri, 0, CH - 1:], (CH, ST)) for ri in range(2)]
            for c in range(1, CH - 1):
                pr, cr = [carry[:, ri, :, c - 1] for ri in range(2)], [carry[:, ri, :, c] for ri in range(2)]
                x = [t1[:, 0, 0, :], t1[:, 0, 1, :], t1[:, 0, 2, :], t1[:, 0, 3, :]]
                v.mark(tt(x[0], p16[0], pr[0], ALU.mult))
                v.mark(tt(x[1], p16[1], pr[1], ALU.mult))
                v.mark(tt(x[2], p16[0], pr[1], ALU.mult))
                v.link(tt(x[3], p16[1], pr[0], ALU.mult))
                v.mark(tt(cr[0], cr[0], x[0], ALU.add))
                v.mark(tt(cr[1], cr[1], x[2], ALU.add))
                v.wait()
                v.mark(tt(cr[0], cr[0], x[1], ALU.subtract))
                v.link(tt(cr[1], cr[1], x[3], ALU.add))
            dve.sem_inc(carried, 1)
            for qi in range(3):
                fix(dve, v, fx, qi)
            dve.sem_inc(p_done, 2)
            dve.wait_ge(s_done, 1)
            dve.tensor_copy(endp[:], view(H[:, 0, 0, SEQ - 1:], (ST * T, 2), (T, ST))).then_inc(ends_ready, 1)
            dcol = FEAT_AT["ssm_d"][0]
            for k in range(4):
                dve.wait_ge(y_made, k + 1)
                dve.scalar_tensor_tensor(out=y[:, k, :], in0=uT[:, k, :], scalar=m.feat[:, dcol + k:dcol + k + 1], in1=yps[:, k, :T],
                                         op0=ALU.mult, op1=ALU.add).then_inc(y_ready, 1)
            for n in range(3):
                dve.wait_ge(ends_turned, n + 1)
                r = 2 * ST if n == 2 else P
                dve.tensor_copy(endrow[:r, n, :], tps[:r, n, :P]).then_inc(ends_stored, 1)
            dve.wait_ge(gelu, 4)
            for mo in range(4):
                if mo == 0:
                    dve.wait_ge(sig, 4)
                v.link(tt(yg[:, mo, :], yg[:, mo, :], sg[:, mo, :], ALU.mult))
                tt(y[:, mo, :], yg[:, mo, :], yg[:, mo, :], ALU.mult).then_inc(sq_ready, 1)
            dve.wait_ge(rms, 1)
            v.link(dve.reciprocal(sg[:, 1, :], sg[:, 0, :]))
            oc = FEAT_AT["out_norm"][0] + 8
            for mo in range(4):
                dve.scalar_tensor_tensor(out=y[:, mo, :], in0=yg[:, mo, :], scalar=m.feat[:, oc + mo:oc + mo + 1], in1=sg[:, 1, :],
                                         op0=ALU.mult, op1=ALU.mult).then_inc(n_ready, 1)
            for mo in range(4):
                dve.wait_ge(n_high, mo + 1)
                split_low(dve, m.ssmTl[:, mo, :], y[:, mo, :], m.ssmTh[:, mo, :])


def phase_gmlp(nc, m, io):
    with ExitStack() as ctx:
        sb = lambda n, sh: ctx.enter_context(nc.sbuf_tensor(n, sh, F32))
        ws, gain, in_done = m.gm_w, m.gm_gain, m.gm_in
        wT, wS = sb("gm_wT", [P, 4, P]), sb("gm_wS", [NTS, 4, NTS])
        sq, bsS = sb("gm_sq", [P, 512]), sb("gm_bsS", [NTS, 4])
        ssq, rms, rstd = sb("gm_ssq", [P, 3, 4]), sb("gm_rms", [P, 3, 4]), sb("gm_rstd", [P, 3, 4])
        tps = ctx.enter_context(nc.psum_tensor("gm_tps", [P, 512], F32))
        sps = ctx.enter_context(nc.psum_tensor("gm_sps", [NTS, 64], F32))
        mps = ctx.enter_context(nc.psum_tensor("gm_mix", [P, 3, 512], F32))
        n_ = lambda n: m.sem("gm_" + n)
        gelu, summed, rooted, vn, v_step = n_("gelu"), n_("summed"), n_("rooted"), n_("vn"), n_("v_step")
        turned, wT_ready, spread, wS_ready, mixed = n_("turned"), n_("wT_ready"), n_("spread"), n_("wS_ready"), n_("mixed")
        block = ctx.enter_context(nc.Block())
        bs = FEAT_AT["gmlp_bs"][0]

        @block.sync
        def _(sp):
            sp.wait_ge(vn, 3)
            m.store(sp, dram(io["p_gmlp_v"], 0, (512, P), (1, 512)), m.proj[:, 1, O_VG:O_VG + 512])
            m.store(sp, dram(io["s_gmlp_v"], 0, (512, NTS), (1, 512)), m.proj[:NTS, 2, O_VG:O_VG + 512])

        @block.scalar
        def _(act):
            for t in range(3):
                g = m.proj[:ROWS[t], t, O_UG:O_UG + 1024]
                act.activation(g, g, ACT.Gelu_apprx_tanh).then_inc(gelu, 1)
            for t in range(3):
                r = ROWS[t]
                act.wait_ge(summed, t + 1)
                act.activation(rms[:r, t, :], ssq[:r, t, :], ACT.Sqrt, bias=m.eps[:r, :], scale=1.0 / P).then_inc(rooted, 1)

        @block.tensor
        def _(pe):
            pe.wait_ge(in_done, 32)
            for g in range(4):
                mm = pe.transpose(tps[:, g * P:(g + 1) * P], ws[:, g, :], m.const("ident"))
            mm.then_inc(turned, 1)
            pe.wait_ge(wT_ready, 1)
            pe.matmul(sps[:, :32], m.const("spread8"), view(wT[:NS, 0, :], (P, 4), (1, NS)), start=True, stop=True)
            pe.matmul(sps[:, 32:36], m.const("spread8"), m.feat[:NS, bs:bs + 4], start=True, stop=True).then_inc(spread, 1)
            pe.wait_ge(wS_ready, 1)
            for t in range(3):
                pe.wait_ge(vn, t + 1)
                for g in range(4):
                    v = m.proj[:ROWS[t], t, O_VG + g * P:O_VG + (g + 1) * P]
                    mm = pe.matmul(mps[:ROWS[t], t, g * P:(g + 1) * P], wT[:, g, :] if t < 2 else wS[:, g, :], v, start=True, stop=True)
                mm.then_inc(mixed, 1)

        @block.vector
        def _(dve):
            v = Chain(dve, v_step)
            dve.wait_ge(turned, 1)
            dve.tensor_tensor(wT[:], view(tps[:], (P, 4), (1, P)), view(m.const("causal_T"), (0, 4), (1, P)), ALU.mult).then_inc(wT_ready, 1)
            dve.wait_ge(spread, 1)
            v.link(dve.tensor_copy(bsS[:], sps[:, 32:36]))
            dve.tensor_tensor(view(wS[:, 0, :], (NTS, 4), (NS, NB), (1, NS)), view(sps[:], (NS, 4), (0, NB), (1, NS)),
                              view(m.const("causal_seq_T"), (0, 4), (NS, NB), (1, NS)), ALU.mult).then_inc(wS_ready, 1)
            for t in range(3):
                r = ROWS[t]
                x = m.proj[:r, t, O_VG:O_VG + 512]
                dve.wait_ge(gelu, t + 1)
                v.link(dve.tensor_tensor(sq[:r], x, x, ALU.mult))
                dve.tensor_reduce(ssq[:r, t, :], view(sq[:r], (P, 4), (1, P)), AX_X, ALU.add).then_inc(summed, 1)
                dve.wait_ge(summed, t + 1)
            for t in range(3):
                r = ROWS[t]
                x = view(m.proj[:r, t, O_VG:], (P, 4), (1, P))
                dve.wait_ge(rooted, t + 1)
                v.link(dve.reciprocal(rstd[:r, t, :], rms[:r, t, :]))
                v.link(dve.tensor_tensor(x, x, view(rstd[:r, t, :], (1, 4), (0, P)), ALU.mult))
                dve.tensor_tensor(x, x, view(gain[:r], (P, 4), (1, P)), ALU.mult).then_inc(vn, 1)
            for t in range(3):
                r = ROWS[t]
                dve.wait_ge(mixed, t + 1)
                for g in range(4):
                    u = m.proj[:r, t, O_UG + g * P:O_UG + (g + 1) * P]
                    b_ = m.feat[:, bs + g:bs + g + 1] if t < 2 else bsS[:, g:g + 1]
                    v.mark(dve.scalar_tensor_tensor(out=u, in0=mps[:r, t, g * P:(g + 1) * P], scalar=b_, in1=u, op0=ALU.add, op1=ALU.mult))


def turn_with_gain_pe(pe, m, src, tps, jobs, ready, turned, stored):
    for n, (t, k0) in enumerate(jobs):
        r = ROWS[t]
        ready(pe, n)
        if n >= 2:
            pe.wait_ge(stored, n - 1)
        for j in range(4):
            mm = pe.transpose(tps[:, n % 2, j * P:j * P + r], src(t, k0 + j), m.const("ident")[:r, :r])
        mm.then_inc(turned, 1)


def phase_merge(nc, m, io):
    with ExitStack() as ctx:
        sb = lambda n, sh: ctx.enter_context(nc.sbuf_tensor(n, sh, F32))
        junk, ssq, rms, rstd = sb("mg_junk", [P, 1024]), sb("mg_ssq", [P, 6]), sb("mg_rms", [P, 6]), sb("mg_rstd", [P, 6])
        tps = ctx.enter_context(nc.psum_tensor("mg_tps", [P, 2, 512], F32))
        n_ = lambda n: m.sem("mg_" + n)
        summed, rooted, normed, turned, stored, v_step = n_("summed"), n_("rooted"), n_("normed"), n_("turned"), n_("stored"), n_("v_step")
        sems = (turned, stored, n_("high"), n_("low"))
        tmp = [sb(f"mg_tmp{u}", [P, 4, P]) for u in range(2)]
        jobs = [(t, k0) for t in range(3) for k0 in (0, 4, 8)]
        block = ctx.enter_context(nc.Block())

        def part(t, c):
            r = ROWS[t]
            return m.proj[:r, t, O_Q:O_Q + AW] if c == 0 else m.proj[:r, t, O_UG:O_UG + 512]

        @block.sync
        def _(sp):
            for q in range(4):
                load_piece(sp, io["w_out"], 512, m.oslot, m.w_out_landed, 0, q)

        @block.scalar
        def _(act):
            for t in range(3):
                r = ROWS[t]
                if t == 2:
                    act.wait_ge(m.o_back, 16 * NB)
                for c in range(2):
                    i = 2 * t + c
                    if i:
                        act.wait_ge(summed, i)
                    act.activation(junk[:r, :(AW, 512)[c]], part(t, c), ACT.Square, accum_out=ssq[:r, i:i + 1]).then_inc(summed, 1)
                    act.wait_ge(summed, i + 1)
                    act.activation(rms[:r, i:i + 1], ssq[:r, i:i + 1], ACT.Sqrt, bias=m.eps[:r, :], scale=1.0 / (AW, 512)[c]).then_inc(rooted, 1)
            split_turned_act(act, jobs, tmp, sems, m.agTh)

        @block.tensor
        def _(pe):
            src = lambda t, k: m.proj[:ROWS[t], t, O_Q + k * P:O_Q + (k + 1) * P] if k < 8 else \
                m.proj[:ROWS[t], t, O_UG + (k - 8) * P:O_UG + (k - 7) * P]
            turn_with_gain_pe(pe, m, src, tps, jobs, lambda e, n: e.wait_ge(normed, 2 * (n // 3) + n % 3 // 2 + 1), turned, stored)

        @block.vector
        def _(dve):
            v = Chain(dve, v_step)
            for i in range(6):
                t, c = divmod(i, 2)
                r = ROWS[t]
                dve.wait_ge(rooted, i + 1)
                v.link(dve.reciprocal(rstd[:r, i:i + 1], rms[:r, i:i + 1]))
                dve.tensor_scalar(part(t, c), part(t, c), rstd[:r, i:i + 1], None, ALU.mult).then_inc(normed, 1)
            split_turned_dve(dve, jobs, lambda n: tps[:, n % 2, :], tmp,
                             lambda k0: m.feat[:, FEAT_AT["out_norm"][0] + (k0 if k0 < 8 else 12):][:, :4],
                             sems, m.agTh, m.agTl)


def cat(ag, ssm, k):
    return ssm[:, k - 8, :] if 8 <= k < 12 else ag[:, k if k < 8 else k - 4, :]


def phase_out(nc, m, io):
    NCH = D // 512
    with ExitStack() as ctx:
        sb = lambda n, sh: ctx.enter_context(nc.sbuf_tensor(n, sh, F32))
        ssq, rms, rstd = sb("ffn_ssq", [P, 3]), sb("ffn_rms", [P, 3]), sb("ffn_rstd", [P, 3])
        gain = view(m.oslot[0][:], (1, D))
        acc = [[ctx.enter_context(nc.psum_tensor(f"out_acc{c}{t}", [P, 512], F32)) for t in range(3)] for c in range(2)]
        n_ = lambda n: m.sem("out_" + n)
        free_v, free_a, x_in, step = n_("acc_free_v"), n_("acc_free_a"), n_("x_in"), n_("v_step")
        summed, rooted = n_("summed"), n_("rooted")
        highs = [sb(f"w_out_high{q}", [P, 4, 512]) for q in range(4)]
        lows = [sb(f"w_out_low{q}", [P, 4, 512]) for q in range(4)]
        z = Stream(m, "out", NCH // 2, 512, io["w_out"], lambda k: cat(m.agTh, m.ssmTh, k), lambda k: cat(m.agTl, m.ssmTl, k), m.oslot, highs, lows, m.w_out_landed)
        gain_in = n_("gain_in")
        block = ctx.enter_context(nc.Block())

        @block.sync
        def _(sp):
            for t in range(3):
                src = dram(io["x_prompt"], t * P * D, (D, P), (1, D)) if t < 2 else dram(io["x_sample"], 0, (D, NTS), (1, D))
                sp.dma_start(m.x1[:ROWS[t], t, :], src).then_inc(x_in, 16)
            stream_load(sp, z)
            sp.wait_ge(z.low, 4 * NCH - 3)
            sp.dma_start(gain, dram(io["norm_ffn"], 0, (0, P), (1, D))).then_inc(gain_in, 16)

        @block.tensor
        def _(pe):
            stream_pe(pe, z, acc, free_v, free_a)

        @block.vector
        def _(dve):
            v = Chain(dve, step)

            def copy_out(i, c):
                dve.wait_ge(z.used, i * 8 + (4 * c + 8))
                for t in range(3):
                    r = ROWS[t]
                    x = m.x1[:r, t, bass.ds((2 * i + c) * 512, 512)]
                    ad = dve.tensor_tensor(x, acc[c][t][:r, :], x, ALU.add)
                ad.then_inc(free_v, 1)

            dve.sem_inc(free_v, 2)
            dve.wait_ge(x_in, 48)
            stream_dve(dve, z, copy_out)
            dve.wait_ge(gain_in, 16)
            for t in range(3):
                r = ROWS[t]
                dve.wait_ge(rooted, t + 1)
                v.link(dve.reciprocal(rstd[:r, t:t + 1], rms[:r, t:t + 1]))
                v.link(dve.tensor_scalar(m.h2[:r, t, :], m.x1[:r, t, :], rstd[:r, t:t + 1], None, ALU.mult))
                v.mark(dve.tensor_tensor(m.h2[:r, t, :], m.h2[:r, t, :], gain[:r, :], ALU.mult))

        @block.scalar
        def _(act):
            act.sem_inc(free_a, 2 + NCH)
            stream_act(act, z, lambda i, c: None)
            act.wait_ge(free_v, 2 + NCH)
            for t in range(3):
                r = ROWS[t]
                act.activation(m.h2[:r, t, :], m.x1[:r, t, :], ACT.Square, accum_out=ssq[:r, t:t + 1]).then_inc(summed, 1)
                act.wait_ge(summed, t + 1)
                act.activation(rms[:r, t:t + 1], ssq[:r, t:t + 1], ACT.Sqrt, bias=m.eps[:r, :], scale=1.0 / D).then_inc(rooted, 1)


NE, NG4 = 4, 4
SLOTS = 8
ITEMS = 6


def phase_route(nc, m, io):
    with ExitStack() as ctx:
        sb = lambda n, sh: ctx.enter_context(nc.sbuf_tensor(n, sh, F32))
        h2T, rw, rb = sb("rt_h2T", [P, KT, T]), sb("rt_w", [P, KT, 20]), sb("rt_b", [P, 20])
        lg, le = sb("rt_lg", [P, 3, 4]), sb("rt_le", [P, 12, 4])
        c1, c2 = sb("rt_c1", [P, 12, 4, 4]), sb("rt_c2", [P, 12, 4, 4])
        rk, oh, sel = sb("rt_rank", [P, 12, 4]), sb("rt_onehot", [P, 3, 4]), sb("rt_sel", [P, 12, 4])
        mg, eg, gs, gp = sb("rt_mg", [P, 3]), sb("rt_eg", [P, 3, 4]), sb("rt_gs", [P, 3]), sb("rt_gp", [P, 3])
        me, ex, es, gt = sb("rt_me", [P, 12]), sb("rt_ex", [P, 12, 4]), sb("rt_es", [P, 12]), sb("rt_gate", [P, 12, 4])
        pos, cnt, nt, start, nx = sb("rt_pos", [P, 3, 4]), sb("rt_cnt", [P, 4]), sb("rt_nt", [P, 4]), sb("rt_start", [P, 4]), sb("rt_nx", [P, 4])
        actv, wst, w_t, w_g = sb("rt_active", [P, ITEMS, 4]), sb("rt_wst", [P, ITEMS, 4]), sb("rt_wtile", [P, ITEMS]), sb("rt_wgroup", [P, ITEMS])
        big = sb("rt_big", [P, 3, ITEMS, 4])
        has, plan = sb("rt_has", [P, 3, ITEMS]), sb("rt_plan", [1, 8])
        tps = ctx.enter_context(nc.psum_tensor("rt_tps", [P, 2, 512], F32))
        lps = ctx.enter_context(nc.psum_tensor("rt_lps", [P, 3, 512], F32))
        pps = ctx.enter_context(nc.psum_tensor("rt_pps", [P, 64], F32))
        n_ = lambda n: m.sem("rt_" + n)
        in_done, turned, stored, logits, oh_ready, counted = n_("in"), n_("turned"), n_("stored"), n_("logits"), n_("oh_ready"), n_("counted")
        sub_done, exps, v_step = n_("sub_done"), n_("exps"), n_("v_step")
        jobs = [(t, k0) for t in range(3) for k0 in (0, 4, 8, 12)]
        block = ctx.enter_context(nc.Block())

        @block.sync
        def _(sp):
            sp.dma_start(rw[:, :, :4], dram(io["router_group_w"], 0, (4, P), (P * 4, KT), (1, 4))).then_inc(in_done, 16)
            for g in range(4):
                sp.dma_start(rw[:, :, 4 + 4 * g:8 + 4 * g], dram(io["router_expert_w"], g * D * 4, (4, P), (P * 4, KT), (1, 4))).then_inc(in_done, 16)
            sp.dma_start(rb[:, :4], dram(io["router_group_b"], 0, (0, P), (1, 4))).then_inc(in_done, 16)
            sp.dma_start(rb[:, 4:], dram(io["router_expert_b"], 0, (0, P), (1, 16))).then_inc(in_done, 16)

        @block.tensor
        def _(pe):
            turn_with_gain_pe(pe, m, lambda t, k: m.h2[:ROWS[t], t, k * P:(k + 1) * P], tps, jobs, lambda e, n: None, turned, stored)
            pe.wait_ge(in_done, 16 * 7)
            for t in range(3):
                r = ROWS[t]
                pe.wait_ge(stored, 4 * t + 4)
                for k in range(KT):
                    mm = pe.matmul(lps[:r, t, :20], h2T[:, k, t * P:t * P + r], rw[:, k, :], start=(k == 0), stop=(k == KT - 1))
                mm.then_inc(logits, 1)
            pe.wait_ge(oh_ready, 1)
            for t in range(3):
                for t2 in range(t + 1):
                    pe.matmul(pps[:, 4 * t:4 * t + 4], m.const("before" if t2 == t else "ones"), oh[:, t2, :], start=(t2 == 0), stop=(t2 == t))
            for t in range(3):
                mm = pe.matmul(pps[:, 12:16], m.const("ones"), oh[:, t, :], start=(t == 0), stop=(t == 2))
            mm.then_inc(counted, 1)

        @block.scalar
        def _(act):
            act.wait_ge(sub_done, 1)
            act.activation(eg[:], eg[:], ACT.Exp)
            act.activation(ex[:], ex[:], ACT.Exp).then_inc(exps, 1)

        @block.vector
        def _(dve):
            v = Chain(dve, v_step)
            tt, ts, red = dve.tensor_tensor, dve.tensor_scalar, dve.tensor_reduce
            v.mark(dve.memset(lg[:], 0.0))
            v.link(dve.memset(le[:], 0.0))
            for n, (t, k0) in enumerate(jobs):
                dve.wait_ge(turned, n + 1)
                dve.tensor_copy(h2T[:, k0:k0 + 4, t * P:t * P + ROWS[t]], view(tps[:, n % 2, :], (P, 4), (1, ROWS[t]))).then_inc(stored, 1)
            for t in range(3):
                r = ROWS[t]
                dve.wait_ge(logits, t + 1)
                v.mark(tt(lg[:r, t, :], lps[:r, t, :4], rb[:r, :4], ALU.add))
                v.mark(tt(view(le[:r, 4 * t, :], (1, 16)), lps[:r, t, 4:20], rb[:r, 4:], ALU.add))
            v.wait()

            def rank(x, n, out):
                vj = view(x, (4, n), (0, 4), (1, 4))
                vi = view(x, (4, n), (1, 4), (0, 4))
                a_, b_ = (view(c[:, 0, 0, :], (16, n), (4, 4), (1, 4)) for c in (c1, c2))
                v.mark(tt(a_, vj, vi, ALU.is_gt))
                v.link(tt(b_, vj, vi, ALU.is_equal))
                v.link(tt(b_, b_, view(m.const("earlier4"), (0, n), (4, 4), (1, 4)), ALU.mult))
                v.link(tt(a_, a_, b_, ALU.add))
                v.link(red(out, a_, AX_X, ALU.add))

            rank(lg[:], 3, rk[:, :3, :])
            v.link(ts(oh[:], rk[:, :3, :], 0.5, None, ALU.is_lt))
            ts(oh[:, 2, :], oh[:, 2, :], m.const("low_half")[:, 0:1], None, ALU.mult).then_inc(oh_ready, 1)
            dve.wait_ge(oh_ready, 1)
            rank(le[:], 12, rk[:])
            v.mark(ts(sel[:], rk[:], 1.5, None, ALU.is_lt))
            v.mark(red(mg[:], lg[:], AX_X, ALU.max))
            v.link(red(me[:], le[:], AX_X, ALU.max))
            v.mark(tt(eg[:], lg[:], view(mg[:], (1, 3), (0, 4)), ALU.subtract))
            tt(ex[:], le[:], view(me[:], (1, 12), (0, 4)), ALU.subtract).then_inc(sub_done, 1)
            v.wait()
            dve.wait_ge(exps, 1)
            v.mark(red(gs[:], eg[:], AX_X, ALU.add))
            v.link(tt(ex[:], ex[:], sel[:], ALU.mult))
            v.mark(dve.reciprocal(gp[:], gs[:]))
            v.link(red(es[:], ex[:], AX_X, ALU.add))
            v.link(dve.reciprocal(es[:], es[:]))
            v.link(tt(ex[:], ex[:], view(es[:], (1, 12), (0, 4)), ALU.mult))
            v.link(tt(gt[:], ex[:], view(oh[:, 0, :], (1, 12), (0, 4)), ALU.mult))
            v.link(red(m.gate4[:], view(gt[:, 0, :], (16, 3), (1, 4), (4, 4)), AX_X, ALU.add))
            v.mark(tt(m.gate4[:], m.gate4[:], view(gp[:], (1, 3), (0, 4)), ALU.mult))
            dve.wait_ge(counted, 1)
            v.mark(dve.tensor_copy(pos[:], view(pps[:], (4, 3), (1, 4))))
            v.link(dve.tensor_copy(cnt[:], pps[:, 12:16]))
            v.mark(ts(nt[:], cnt[:], 0.5, None, ALU.is_gt))
            v.link(ts(nx[:], cnt[:], 128.5, None, ALU.is_gt))
            v.link(tt(nt[:], nt[:], nx[:], ALU.add))
            v.link(ts(nx[:], cnt[:], 256.5, None, ALU.is_gt))
            v.link(tt(nt[:], nt[:], nx[:], ALU.add))
            v.link(dve.memset(start[:, 0:1], 0.0))
            for g in range(1, 4):
                v.link(tt(start[:, g:g + 1], start[:, g - 1:g], nt[:, g - 1:g], ALU.add))
            v.link(tt(wst[:], view(m.const("iota"), (1, ITEMS), (0, 4)), view(start[:], (0, ITEMS), (1, 4)), ALU.subtract))
            v.mark(ts(actv[:], wst[:], -0.5, None, ALU.is_gt))
            v.link(tt(view(big[:, 0, 0, :], (4, ITEMS), (1, 4)), wst[:], view(nt[:], (0, ITEMS), (1, 4)), ALU.is_lt))
            v.link(tt(actv[:], actv[:], view(big[:, 0, 0, :], (4, ITEMS), (1, 4)), ALU.mult))
            v.link(tt(wst[:], wst[:], actv[:], ALU.mult))
            v.link(red(w_t[:], wst[:], AX_X, ALU.add))
            v.link(tt(wst[:], actv[:], view(m.const("group4"), (0, ITEMS), (1, 4)), ALU.mult))
            v.link(red(w_g[:], wst[:], AX_X, ALU.add))
            v.mark(ts(plan[:, :ITEMS], w_g[0:1, :], 4.0, None, ALU.mult))
            v.mark(red(plan[:, 6:7], nt[0:1, :], AX_X, ALU.add))
            v.link(dve.memset(plan[:, 7:8], 0.0))
            v.link(dve.tensor_copy(m.plan[:], plan[:]))
            v.link(tt(pos[:], pos[:], oh[:], ALU.mult))
            slot = view(m.slot[:], (SLOTS, 3), (1, ITEMS))
            for t in range(3):
                v.mark(tt(big[:, t], view(actv[:, 0, :], (4, ITEMS), (1, 4)), view(pos[:, t, :], (0, ITEMS), (1, 4)), ALU.mult))
            v.wait()
            v.mark(dve.memset(m.slot[:], -1.0))
            v.wait()
            v.link(red(slot, big[:], AX_X, ALU.add))
            for t in range(3):
                v.mark(tt(big[:, t], view(actv[:, 0, :], (4, ITEMS), (1, 4)), view(oh[:, t, :], (0, ITEMS), (1, 4)), ALU.mult))
            v.wait()
            v.link(red(has[:], big[:], AX_X, ALU.add))
            v.link(ts(w_t[:], w_t[:], float(P), None, ALU.mult))
            v.link(tt(slot, slot, view(w_t[:], (0, 3), (1, ITEMS)), ALU.subtract))
            v.link(ts(slot, slot, 1.0, None, ALU.add))
            v.link(tt(slot, slot, has[:], ALU.mult))
            v.link(ts(slot, slot, -1.0, None, ALU.add))


RING = 4
AHEAD = 3
CHUNKS = 48


def weight_order():
    order = [("w1", 0)]
    for e in range(NE - 1):
        order += [("w3", e), ("w1", e + 1)]
        if e < NE - 2:
            order.append(("w2", e))
    order += [("w3", NE - 1), ("w2", NE - 2), ("w2", NE - 1)]
    return order


def phase_moe(nc, m, io):
    with ExitStack() as ctx:
        sb = lambda n, sh: ctx.enter_context(nc.sbuf_tensor(n, sh, F32))
        ring = [sb(f"ex_w{s}", [P, 4, 512]) for s in range(RING)]
        high = [sb(f"ex_w_high{s}", [P, 4, 512]) for s in range(RING)]
        low = [sb(f"ex_w_low{s}", [P, 4, 512]) for s in range(RING)]
        Dm, DT, XT, XTh = sb("ex_D", [P, 3, P]), sb("ex_DT", [P, 3, P]), sb("ex_XT", [P, KT, P]), sb("ex_XT_high", [P, KT, P])
        sl, gsl = sb("ex_slot", [P, 3]), sb("ex_gate", [P, NE])
        s1, hid, hT, hTh = sb("ex_silu", [P, 512]), sb("ex_hid", [P, 512]), sb("ex_hT", [P, 2, 4, P]), sb("ex_hT_high", [P, 2, 4, P])
        ysb, yh = sb("ex_y", [P, 4, 512]), sb("ex_y_high", [P, 4, 512])
        Y = ctx.enter_context(nc.psum_tensor("ex_Y", [P, 4, 512], F32))
        A = ctx.enter_context(nc.psum_tensor("ex_A", [P, 2, 512], F32))
        B = ctx.enter_context(nc.psum_tensor("ex_B", [P, 2, 512], F32))
        n_ = lambda n: m.sem("ex_" + n)
        landed = [n_(f"landed{s}") for s in range(RING)]
        free, D_ready, D_turned, DT_ready, g_made, g_ready = n_("slot_free"), n_("D_ready"), n_("D_turned"), n_("DT_ready"), n_("g_made"), n_("g_ready")
        x_made, x_high, x_low, silu, gated = n_("x_made"), n_("x_high"), n_("x_low"), n_("silu"), n_("gated")
        w_high, w_low = n_("w_high"), n_("w_low")
        h_turned, h_high, h_low, y_high, y_low = n_("h_turned"), n_("h_high"), n_("h_low"), n_("y_high"), n_("y_low")
        back, added, slot_ready = n_("back"), n_("added"), n_("slot_ready")
        order = weight_order()

        turn_at = [4 * order.index(("w1", e + 1)) + 2 for e in range(NE - 1)] + [4 * order.index(("w2", NE - 2)) + 2]
        gather_at = [4 * order.index(("w2", NE - 2)) + 1 + 2 * q for q in range(4)]

        def used(mat, e, w):
            return w * CHUNKS + (RING + 4 * (order.index((mat, e)) + 1))

        block = ctx.enter_context(nc.Block())

        def count(eng):
            return eng.value_load(m.plan[0:1, 6:7], min_val=1, max_val=ITEMS)

        @block.sync
        def _(sp):
            sp.sem_inc(w_low, RING)

            def load(w, item, chunks):
                e0 = sp.value_load(m.plan[0:1, bass.ds(item, 1)], min_val=0, max_val=12)
                for n in chunks:
                    mat, e = order[n % CHUNKS // 4]
                    c = n % 4
                    src = {"w1": io["expert_w1"], "w3": io["expert_w3"], "w2": io["expert_w2"]}[mat][0, bass.ds(e0 + e, 1)]
                    sp.wait_ge(w_low, w * CHUNKS + (n + 1))
                    if mat == "w2":
                        part, dst = src[:, c * P:(c + 1) * P, :].rearrange("e p n -> p (e n)"), view(ring[n % RING][:], (1, D))
                    else:
                        part, dst = src[:, c * 512:(c + 1) * 512, :].rearrange("e (k p) n -> p (e k) n", p=P), ring[n % RING][:]
                    sp.dma_start(dst, part).then_inc(landed[n % RING], 16)

            load(0, 0, range(RING))
            with sp.Fori(0, count(sp)) as w:
                load(w, w, range(RING, CHUNKS))
                load(w, w + 1, range(CHUNKS, CHUNKS + RING))
        @block.tensor
        def _(pe):
            I = m.const("ident")

            def gather(q):
                bank = A[:, q, :] if q < 2 else B[:, q - 2, :]
                for j in range(4):
                    k = 4 * q + j
                    for t in range(3):
                        mm = pe.matmul(bank[:, j * P:(j + 1) * P], m.h2[:ROWS[t], t, k * P:(k + 1) * P], Dm[:ROWS[t], t, :],
                                       start=(t == 0), stop=(t == 2))
                mm.then_inc(x_made, 1)

            pe.wait_ge(D_ready, 1)
            for q in range(4):
                gather(q)
            pe.wait_ge(x_low, 4)
            with pe.Fori(0, count(pe)) as w:
                for t in range(3):
                    mm = pe.transpose(B[:, 0, t * P:t * P + ROWS[t]], Dm[:ROWS[t], t, :], I[:ROWS[t], :ROWS[t]])
                mm.then_inc(D_turned, 1)
                for t in range(3):
                    mm = pe.matmul(B[:, 1, :NE], Dm[:ROWS[t], t, :], m.gate4[:ROWS[t], t, :], start=(t == 0), stop=(t == 2))
                mm.then_inc(g_made, 1)
                pe.wait_ge(DT_ready, w + 1)
                pe.wait_ge(g_ready, w + 1)
                for q, (mat, e) in enumerate(order):
                    if mat == "w2":
                        pe.wait_ge(h_low, w * NE + (e + 1))
                    elif mat != "w2" and e > 0:
                        pe.wait_ge(silu if mat == "w1" else gated, w * NE + e)
                    for c in range(4):
                        n = 4 * q + c
                        if n in turn_at:
                            f_ = turn_at.index(n)
                            pe.wait_ge(gated, w * NE + (f_ + 1))
                            for f in range(4):
                                mm = pe.transpose(B[:, f_ % 2, f * P:(f + 1) * P], hid[:, f * P:(f + 1) * P], I)
                            mm.then_inc(h_turned, 1)
                        if n in gather_at:
                            if n == gather_at[0]:
                                pe.wait_ge(D_ready, w + 2)
                                pe.wait_ge(silu, w * NE + NE)
                            if n == gather_at[1]:
                                pe.wait_ge(gated, w * NE + NE)
                            gather(gather_at.index(n))
                        pe.wait_ge(w_low, w * CHUNKS + (RING + n + 1))
                        for j in range(4):
                            if mat == "w2":
                                mm = matmul_split(pe, Y[:, j, :], hTh[:, e % 2, c, :], hT[:, e % 2, c, :], high[n % RING][:, j, :], low[n % RING][:, j, :],
                                                  e == 0 and c == 0, e == NE - 1 and c == 3)
                            else:
                                k = 4 * c + j
                                mm = matmul_split(pe, A[:, 0 if mat == "w1" else 1, :], XTh[:, k, :], XT[:, k, :],
                                                  high[n % RING][:, j, :], low[n % RING][:, j, :], k == 0, k == KT - 1)
                        mm.then_inc(free, 1)
                pe.wait_ge(x_low, w * 4 + 8)
                for n in range(12):
                    t, c = divmod(n, 4)
                    if t == 0:
                        pe.wait_ge(y_low, w * 4 + (c + 1))
                    if n >= 4:
                        pe.wait_ge(added, w * 12 + (n - 3))
                    bank = A[:, n % 4, :] if n % 4 < 2 else B[:, n % 4 - 2, :]
                    sel = DT[:, t, :ROWS[t]].bitcast(F32R)
                    pe.matmul(bank[:ROWS[t], :], sel, yh[:, c, :].bitcast(F32R), start=True, stop=False)
                    pe.matmul(bank[:ROWS[t], :], sel, ysb[:, c, :].bitcast(F32R), start=False, stop=True).then_inc(back, 1)
                pe.wait_ge(added, w * 12 + 12)

        @block.scalar
        def _(act):
            act.sem_inc(free, RING)
            def split(w, n):
                act.wait_ge(free, w * CHUNKS + (n + 1))
                act.wait_ge(landed[n % RING], w * (CHUNKS // RING * 16) + (n // RING + 1) * 16)
                split_high(act.copy, high[n % RING][:], ring[n % RING][:]).then_inc(w_high, 1)

            for n in range(RING):
                split(0, n)

            def split_x(w, q):
                act.wait_ge(x_made, w * 4 + (q + 1))
                split_high(act.copy, view(XTh[:, 4 * q, :], (1, 512)), (A if q < 2 else B)[:, q % 2, :]).then_inc(x_high, 1)

            for q in range(4):
                split_x(0, q)
            with act.Fori(0, count(act)) as w:
                for n in range(CHUNKS):
                    if n + AHEAD >= RING:
                        split(w, n + AHEAD)
                    mat, e = order[n // 4]
                    if mat == "w1" and n % 4 == 3:
                        act.wait_ge(free, used("w1", e, w))
                        if e:
                            act.wait_ge(gated, w * NE + e)
                        act.activation(s1[:], A[:, 0, :], ACT.Silu).then_inc(silu, 1)
                    if n in turn_at:
                        f_ = turn_at.index(n)
                        act.wait_ge(h_turned, w * NE + (f_ + 1))
                        split_high(act.copy, view(hTh[:, f_ % 2, 0, :], (1, 512)), B[:, f_ % 2, :]).then_inc(h_high, 1)
                    if n in gather_at:
                        split_x(w + 1, gather_at.index(n))
                act.wait_ge(free, used("w2", NE - 1, w))
                for c in range(4):
                    split_high(act.copy, yh[:, c, :], Y[:, c, :]).then_inc(y_high, 1)
                split(w, CHUNKS + AHEAD)

        @block.vector
        def _(dve):
            def split(w, n):
                dve.wait_ge(w_high, w * CHUNKS + (n + 1))
                split_low(dve, low[n % RING][:], ring[n % RING][:], high[n % RING][:]).then_inc(w_low, 1)

            def places(w):
                dve.tensor_copy(sl[:], view(m.slot[:, 0, bass.ds(w, 1)], (SLOTS, 3))).then_inc(slot_ready, 1)
                dve.wait_ge(slot_ready, w + 1)
                for t in range(3):
                    d = dve.tensor_scalar(Dm[:, t, :], m.const("iota"), sl[:, t:t + 1], None, ALU.is_equal)
                d.then_inc(D_ready, 1)

            def split_x(w, q):
                dve.wait_ge(x_high, w * 4 + (q + 1))
                split_low(dve, view(XT[:, 4 * q, :], (1, 512)), (A if q < 2 else B)[:, q % 2, :], view(XTh[:, 4 * q, :], (1, 512))).then_inc(x_low, 1)

            places(0)
            for n in range(RING):
                split(0, n)
            for q in range(4):
                split_x(0, q)
            with dve.Fori(0, count(dve)) as w:
                dve.wait_ge(D_turned, w + 1)
                dve.tensor_copy(view(DT[:, 0, :], (1, T)).bitcast(F32R), B[:, 0, :T]).then_inc(DT_ready, 1)
                dve.wait_ge(g_made, w + 1)
                dve.tensor_copy(gsl[:], B[:, 1, :NE]).then_inc(g_ready, 1)
                places(w + 1)
                for n in range(CHUNKS):
                    if n + AHEAD >= RING:
                        split(w, n + AHEAD)
                    mat, e = order[n // 4]
                    if mat == "w3" and n % 4 == 3:
                        dve.wait_ge(silu, w * NE + (e + 1))
                        dve.wait_ge(free, used("w3", e, w))
                        dve.scalar_tensor_tensor(out=hid[:], in0=A[:, 1, :], scalar=gsl[:, e:e + 1], in1=s1[:], op0=ALU.mult, op1=ALU.mult).then_inc(gated, 1)
                    if n in turn_at:
                        f_ = turn_at.index(n)
                        dve.wait_ge(h_high, w * NE + (f_ + 1))
                        split_low(dve, view(hT[:, f_ % 2, 0, :], (1, 512)), B[:, f_ % 2, :], view(hTh[:, f_ % 2, 0, :], (1, 512))).then_inc(h_low, 1)
                    if n in gather_at:
                        split_x(w + 1, gather_at.index(n))
                for c in range(4):
                    dve.wait_ge(y_high, w * 4 + (c + 1))
                    split_low(dve, ysb[:, c, :], Y[:, c, :], yh[:, c, :]).then_inc(y_low, 1)
                split(w, CHUNKS + AHEAD)
                for n in range(12):
                    t, c = divmod(n, 4)
                    bank = A[:, n % 4, :] if n % 4 < 2 else B[:, n % 4 - 2, :]
                    dve.wait_ge(back, w * 12 + (n + 1))
                    x = m.x1[:ROWS[t], t, c * 512:(c + 1) * 512]
                    dve.tensor_tensor(x, bank[:ROWS[t], :], x, ALU.add).then_inc(added, 1)


def phase_store_y(nc, m, io):
    with ExitStack() as ctx:
        block = ctx.enter_context(nc.Block())

        @block.sync
        def _(sp):
            for t in range(3):
                dst = dram(io["y_prompt"], t * P * D, (D, P), (1, D)) if t < 2 else dram(io["y_sample"], 0, (D, NTS), (1, D))
                m.store(sp, dst, m.x1[:ROWS[t], t, :])
            sp.wait_ge(m.out_done, m.n_out)
            sp.wait_ge(m.p_cmp_out, 32)


class Memory:
    pass


def memory(nc, ctx):
    m = Memory()
    m.pack, at = constants()
    m.sem = nc.alloc_semaphore
    sb = lambda name, shape: ctx.enter_context(nc.sbuf_tensor(name, shape, F32))
    m.cpack = sb("cpack", list(m.pack.shape))

    def const(name):
        off, rows, cols = at[name]
        return m.cpack[:rows, off:off + cols]

    m.const = const
    m.feat = sb("feat", [P, NFEAT])
    m.eps = sb("eps", [P, 1])
    m.tab = sb("rel_table", [33, NQ])
    m.qkg = sb("qk_gain", [P, 4, HD])
    m.qkcol = sb("qk_gain_col", [P, 4])
    m.ptab = ctx.enter_context(nc.sbuf_tensor("page_ids", [1, NB * NPG], I32))
    m.plan = ctx.enter_context(nc.sbuf_tensor("work_plan", [1, 8], I32))
    m.slot, m.gate4 = sb("token_slots", [P, 3, SLOTS]), sb("token_gates", [P, 3, NE])
    m.out_done, m.p_cmp_out, m.rep_out = m.sem("out_done"), m.sem("p_cmp_out"), m.sem("bias_rep_out")
    m.n_out = 0

    def store(eng, dst, src, then=None):
        m.n_out += 16
        eng.dma_start(dst, src).then_inc(m.out_done, 16)

    m.SA_V = 32
    m.store = store
    m.w_in_landed = [m.sem(f"w_in_landed{s}") for s in range(4)]
    m.w_out_landed = [m.sem(f"w_out_landed{s}") for s in range(4)]
    m.pool_in = [m.sem(f"pool_{x}_in") for x in ("sel_k", "sel_v", "win_k", "win_v")]
    m.pool_pages_in = [m.sem(f"pool_cmp_pages_in{u}") for u in range(2)]
    m.o_back, m.s5_in, m.gm_in = m.sem("o_back"), m.sem("s5_in"), m.sem("gm_in")
    m.phase_sems = []

    def phase_sem(name):
        m.phase_sems.append(nc.alloc_semaphore(name))
        return m.phase_sems[-1]

    m.sem = phase_sem
    return m


def recycle_semaphores(nc, m, io):
    nums = [s.num for s in m.phase_sems]
    with nc.Block() as block:

        @block.sync
        def _(sp):
            load_late_inputs(sp, m, io)

        @block.gpsimd
        def _(pool):
            pool.sem_clear(range(min(nums), max(nums) + 1))

    for s in m.phase_sems:
        nc.release_semaphore(s)
    m.phase_sems.clear()


def decoder_step(nc, io):
    with ExitStack() as ctx:
        ctx.enter_context(nc.allow_non_contiguous_dma(reason="small tables, and diagonals of the bias row"))
        m = memory(nc, ctx)

        def sb(scope, name, shape):
            return scope.enter_context(nc.sbuf_tensor(name, shape, F32))

        m.proj = sb(ctx, "proj", [P, 3, IN_W])
        with ExitStack() as s:
            m.hTh, m.hTl = sb(s, "hT_high", [P, KT, T]), sb(s, "hT_low", [P, KT, T])
            m.wslot = [sb(s, f"w_in_slot{i}", [P, 4, PCH]) for i in range(4)]
            phase_norm_in(nc, m, io)
            phase_project(nc, m, io)
        with ExitStack() as s:
            m.bias_win, m.bias_cmp = sb(s, "bias_win", [P, WIN]), sb(s, "bias_cmp", [P, NC_S])
            m.bias_new, m.gate_s = sb(s, "bias_new", [P, NB, NTS]), sb(s, "gate_s", [P, 3, NB])
            m.kc_s, m.vc_s = sb(s, "kc_s", [P, NB * 2 * NC_S]), sb(s, "vc_s", [NC_S, NB * KVW])
            m.qkT = sb(s, "qkT", [P, 12, T])
            with ExitStack() as s2:
                m.kc_p, m.vc_p = sb(s2, "kc_p", [P, 2 * NC_P]), sb(s2, "vc_p", [NC_P, KVW])
                with ExitStack() as s3:
                    m.cmp_pages = [sb(s3, f"cmp_pages{u}", [P, 8, 2 * NKV * 2 * HD]) for u in range(2)]
                    m.w1, m.w2 = sb(s3, "cmp_w1s", [P, 2, 8, P]), sb(s3, "cmp_w2s", [P, HD])
                    m.cmp_w_in, m.p_pages_in = m.sem("cmp_w_in"), m.sem("p_pages_in")
                    m.cmp_pages_in = [[m.sem(f"cmp_pages_in{u}") for u in range(2)], m.pool_pages_in]
                    with ExitStack() as s4:
                        m.q_pairs, m.k_pairs = sb(s4, "q_pairs", [P, 3, AW]), sb(s4, "k_pairs", [P, 3, 2 * KVW])
                        phase_heads(nc, m, io)
                        phase_turn_heads(nc, m, io)
                    phase_compress(nc, m, io)
                phase_prompt_attention(nc, m, io)
            phase_sample_attention(nc, m, io)
        with ExitStack() as s:
            m.ssmTh, m.ssmTl = sb(s, "ssmT_high", [P, 4, T]), sb(s, "ssmT_low", [P, 4, T])
            with ExitStack() as s2:
                late_inputs(nc, m, s2)
                recycle_semaphores(nc, m, io)
                phase_s5(nc, m, io)
                phase_gmlp(nc, m, io)
            m.agTh, m.agTl = sb(s, "agT_high", [P, 12, T]), sb(s, "agT_low", [P, 12, T])
            m.oslot = [sb(s, f"w_out_slot{i}", [P, 4, 512]) for i in range(4)]
            phase_merge(nc, m, io)
            m.x1, m.h2 = m.proj[:, :, 0:D], m.proj[:, :, D:2 * D]
            phase_out(nc, m, io)
        phase_route(nc, m, io)
        phase_moe(nc, m, io)
        phase_store_y(nc, m, io)


KV_TAIL = (NKV, 2, HD)
OUTS = (("y_prompt", (1, SEQ, D)), ("y_sample", (NB, NS, D)),
        ("p_kv_cmp", (1, 1, SEQ) + KV_TAIL), ("p_kv_sel", (1, 1, SEQ) + KV_TAIL), ("p_kv_win", (1, 1, SEQ) + KV_TAIL),
        ("p_ssm_re", (1, 1, SG, SN)), ("p_ssm_im", (1, 1, SG, SN)), ("p_gmlp_v", (1, 1, P, 512)),
        ("s_kv_cmp", (NB, 1, NS) + KV_TAIL), ("s_kv_sel", (NB, 1, NS) + KV_TAIL), ("s_kv_win", (NB, 1, WIN) + KV_TAIL),
        ("s_ssm_re", (NB, 1, SG, SN)), ("s_ssm_im", (NB, 1, SG, SN)), ("s_gmlp_v", (NB, 1, NS, 512)))


def kernel(**inputs):
    import concourse.bacc as bacc
    from concourse.bass_utils import run_bass_kernel_spmd

    nc = bacc.Bacc("TRN2", target_bir_lowering=False, num_devices=1)
    arrays = {f"in_{name}": np.ascontiguousarray(a) for name, a in inputs.items()}
    arrays["in_cpack"] = constants()[0]
    io = {}
    for name, a in arrays.items():
        io[name[3:]] = nc.dram_tensor(name, a.shape, mybir.dt.from_np(a.dtype), kind="ExternalInput").ap()
    for name, shape in OUTS:
        io[name] = nc.dram_tensor(name, shape, F32, kind="ExternalOutput").ap()
    io["bias_rows"] = nc.dram_tensor("bias_rows", (NQ, LB), F32).ap()
    io["bias_rep"] = nc.dram_tensor("bias_rep", (P, NQ, TRI), F32).ap()
    io["gate_rows"] = nc.dram_tensor("gate_rows", (NTS, 3 * NQ), F32).ap()
    io["o_rows"] = nc.dram_tensor("o_rows", (NB, P, HD), F32).ap()
    decoder_step(nc, io)
    got = run_bass_kernel_spmd(nc, [arrays], core_ids=[0]).results[0]
    return tuple(got[name] for name, _ in OUTS)
```
